# Optimizing a Trainium2 kernel written in Bass

```python
import math
import jax, jax.numpy as jnp
from jax import lax
import numpy as np

D_MODEL = 1024
BATCH = 1
SEQ = 256
DEPTH = 1

FOX_HEADS = 8
FOX_HEAD_DIM = 128
FOX_WIDTH = FOX_HEADS * FOX_HEAD_DIM
FOX_BLOCK = 128
GDN_HEADS = 8
GDN_HEAD_K = 128
GDN_HEAD_V = 128
GDN_K_WIDTH = GDN_HEADS * GDN_HEAD_K
GDN_V_WIDTH = GDN_HEADS * GDN_HEAD_V
GDN_CONV = 4
GDN_CONV_CH = 2 * GDN_K_WIDTH + GDN_V_WIDTH
GDN_CHUNK = 64
D_FF = 2816
FFN_CONV = 3
EPS = 1e-6

IN_SIZES = (FOX_WIDTH, FOX_WIDTH, FOX_WIDTH, FOX_HEADS,
            GDN_K_WIDTH, GDN_K_WIDTH, GDN_V_WIDTH, GDN_HEADS, GDN_HEADS, GDN_V_WIDTH,
            D_MODEL, D_MODEL)
D_IN = sum(IN_SIZES)


def rmsnorm(x, g):
    xf = x.astype(jnp.float32)
    xf = xf * lax.rsqrt(jnp.mean(xf * xf, axis=-1, keepdims=True) + EPS)
    return (xf * g.astype(jnp.float32)).astype(x.dtype)

def l2norm(x):
    xf = x.astype(jnp.float32)
    return xf * lax.rsqrt(jnp.sum(xf * xf, axis=-1, keepdims=True) + EPS)

def causal_dwconv(x, w):
    K = w.shape[0]
    S = x.shape[1]
    xp = jnp.pad(x, ((0, 0), (K - 1, 0), (0, 0)))
    return sum(xp[:, i:i + S, :] * w[i] for i in range(K))

def split_in(h):
    idx = np.cumsum(np.array(IN_SIZES))[:-1].tolist()
    return jnp.split(h, idx, axis=-1)

def fox_attention(q, k, v, log_f):
    B, S, H, Dh = q.shape
    nb = S // FOX_BLOCK
    scale = Dh ** -0.5
    c = jnp.cumsum(log_f.astype(jnp.float32), axis=1).transpose(0, 2, 1)
    kh = k.transpose(0, 2, 1, 3)
    vh = v.transpose(0, 2, 1, 3)
    qb = q.reshape(B, nb, FOX_BLOCK, H, Dh).transpose(1, 0, 3, 2, 4)
    cb = c.reshape(B, H, nb, FOX_BLOCK).transpose(2, 0, 1, 3)
    key_pos = jnp.arange(S)

    def block(args):
        qi, ci, i = args
        s = jnp.einsum('bhqd,bhkd->bhqk', qi, kh).astype(jnp.float32) * scale
        s = s + (ci[..., :, None] - c[..., None, :])
        q_pos = i * FOX_BLOCK + jnp.arange(FOX_BLOCK)
        causal = key_pos[None, :] <= q_pos[:, None]
        p = jax.nn.softmax(jnp.where(causal, s, -jnp.inf), axis=-1)
        return jnp.einsum('bhqk,bhkd->bhqd', p.astype(vh.dtype), vh)

    o = lax.map(block, (qb, cb, jnp.arange(nb)))
    return o.transpose(1, 0, 3, 2, 4).reshape(B, S, H * Dh)

def gated_delta_rule(q, k, v, g, beta):
    B, S, H, dk = q.shape
    dv = v.shape[-1]
    C = GDN_CHUNK
    N = S // C
    f32 = jnp.float32

    def chunk4(t):
        return t.astype(f32).reshape(B, N, C, H, t.shape[-1]).transpose(0, 3, 1, 2, 4)

    def chunk3(t):
        return t.astype(f32).reshape(B, N, C, H).transpose(0, 3, 1, 2)

    qc = chunk4(q) * (dk ** -0.5)
    kc = chunk4(k)
    vc = chunk4(v)
    bc = chunk3(beta)
    gc = jnp.cumsum(chunk3(g), axis=-1)

    tri_incl = jnp.tril(jnp.ones((C, C), dtype=bool))
    tri_strict = jnp.tril(jnp.ones((C, C), dtype=bool), k=-1)
    diff = gc[..., :, None] - gc[..., None, :]
    decay = jnp.exp(jnp.where(tri_incl, diff, -jnp.inf))

    kb = kc * bc[..., None]
    A = jnp.where(tri_strict, jnp.einsum('bhncd,bhnmd->bhncm', kb, kc) * decay, 0.0)
    lhs = A + jnp.eye(C, dtype=f32)
    rhs = jnp.concatenate([vc * bc[..., None], kb * jnp.exp(gc)[..., None]], axis=-1)
    sol = lax.linalg.triangular_solve(lhs, rhs, left_side=True, lower=True, unit_diagonal=True)
    u_hat, w = sol[..., :dv], sol[..., dv:]

    attn = jnp.einsum('bhncd,bhnmd->bhncm', qc, kc) * decay
    q_dec = qc * jnp.exp(gc)[..., None]
    k_dec = kc * jnp.exp(gc[..., -1:] - gc)[..., None]
    g_last = jnp.exp(gc[..., -1])

    xs = tuple(jnp.moveaxis(t, 2, 0) for t in (u_hat, w, attn, q_dec, k_dec, g_last))

    def step(state, inp):
        u_hat_i, w_i, attn_i, q_dec_i, k_dec_i, gl_i = inp
        u = u_hat_i - jnp.einsum('bhcd,bhdv->bhcv', w_i, state)
        o = jnp.einsum('bhcd,bhdv->bhcv', q_dec_i, state) + jnp.einsum('bhcm,bhmv->bhcv', attn_i, u)
        state = state * gl_i[..., None, None] + jnp.einsum('bhcd,bhcv->bhdv', k_dec_i, u)
        return state, o

    s0 = jnp.zeros((B, H, dk, dv), f32)
    _, o = lax.scan(step, s0, xs)
    return o.transpose(1, 0, 3, 2, 4).reshape(B, S, H, dv).astype(v.dtype)

def first_inputs(seed: int = 0) -> dict:
    key = jax.random.key(seed)
    ks = jax.random.split(key, 20)
    L, D = DEPTH, D_MODEL
    nrm = jax.random.normal
    x = nrm(ks[0], (BATCH, SEQ, D), jnp.float32)
    norm_mix = 1.0 + 0.05 * nrm(ks[1], (L, D), jnp.float32)
    w_in = nrm(ks[2], (L, D, D_IN), jnp.float32) * D ** -0.5
    fox_f_bias = 3.0 + 0.5 * nrm(ks[3], (L, FOX_HEADS), jnp.float32)
    gdn_conv_w = nrm(ks[4], (L, GDN_CONV, GDN_CONV_CH), jnp.float32) * GDN_CONV ** -0.5
    gdn_a_log = jnp.log(jax.random.uniform(ks[5], (L, GDN_HEADS), jnp.float32, 1.0, 16.0))
    dt = jnp.exp(jax.random.uniform(ks[6], (L, GDN_HEADS), jnp.float32, math.log(1e-3), math.log(1e-1)))
    gdn_dt_bias = dt + jnp.log(-jnp.expm1(-dt))
    gdn_norm = 1.0 + 0.05 * nrm(ks[7], (L, GDN_HEAD_V), jnp.float32)
    w_branch_fox = nrm(ks[8], (L, FOX_WIDTH, D), jnp.float32) * FOX_WIDTH ** -0.5
    w_branch_gdn = nrm(ks[9], (L, GDN_V_WIDTH, D), jnp.float32) * GDN_V_WIDTH ** -0.5
    w_out = nrm(ks[10], (L, D, D), jnp.float32) * D ** -0.5
    norm_ffn = 1.0 + 0.05 * nrm(ks[11], (L, D), jnp.float32)
    w_up = nrm(ks[12], (L, D, 2 * D_FF), jnp.float32) * D ** -0.5
    ffn_conv_w = nrm(ks[13], (L, FFN_CONV, 2 * D_FF), jnp.float32) * FFN_CONV ** -0.5
    w_down = nrm(ks[14], (L, D_FF, D), jnp.float32) * D_FF ** -0.5
    norm_final = 1.0 + 0.05 * nrm(ks[15], (D,), jnp.float32)
    return {"x": x, "norm_mix": norm_mix, "w_in": w_in, "fox_f_bias": fox_f_bias,
            "gdn_conv_w": gdn_conv_w, "gdn_a_log": gdn_a_log, "gdn_dt_bias": gdn_dt_bias,
            "gdn_norm": gdn_norm, "w_branch_fox": w_branch_fox, "w_branch_gdn": w_branch_gdn,
            "w_out": w_out, "norm_ffn": norm_ffn, "w_up": w_up, "ffn_conv_w": ffn_conv_w,
            "w_down": w_down, "norm_final": norm_final}

def first_block(x, norm_mix, w_in, fox_f_bias, gdn_conv_w, gdn_a_log, gdn_dt_bias, gdn_norm,
              w_branch_fox, w_branch_gdn, w_out, norm_ffn, w_up, ffn_conv_w, w_down, norm_final):
    B, S, D = x.shape
    h = x
    for l in range(DEPTH):
        hn = rmsnorm(h, norm_mix[l])
        proj = jnp.einsum('bsd,de->bse', hn, w_in[l])
        (fq, fk, fv, ff, gq, gk, gv, ga, gb, gz, gate_fox, gate_gdn) = split_in(proj)

        log_f = jax.nn.log_sigmoid(ff.astype(jnp.float32) + fox_f_bias[l].astype(jnp.float32))
        y_fox = fox_attention(fq.reshape(B, S, FOX_HEADS, FOX_HEAD_DIM),
                              fk.reshape(B, S, FOX_HEADS, FOX_HEAD_DIM),
                              fv.reshape(B, S, FOX_HEADS, FOX_HEAD_DIM), log_f)

        qkv = jax.nn.silu(causal_dwconv(jnp.concatenate([gq, gk, gv], axis=-1), gdn_conv_w[l]))
        cq, ck, cv = jnp.split(qkv, [GDN_K_WIDTH, 2 * GDN_K_WIDTH], axis=-1)
        q = l2norm(cq.reshape(B, S, GDN_HEADS, GDN_HEAD_K))
        k = l2norm(ck.reshape(B, S, GDN_HEADS, GDN_HEAD_K))
        v = cv.reshape(B, S, GDN_HEADS, GDN_HEAD_V)
        g = -jnp.exp(gdn_a_log[l].astype(jnp.float32)) * jax.nn.softplus(
            ga.astype(jnp.float32) + gdn_dt_bias[l].astype(jnp.float32))
        beta = jax.nn.sigmoid(gb.astype(jnp.float32))
        o = gated_delta_rule(q, k, v, g, beta)
        o = rmsnorm(o, gdn_norm[l]) * jax.nn.silu(gz.reshape(B, S, GDN_HEADS, GDN_HEAD_V))
        y_gdn = o.reshape(B, S, GDN_V_WIDTH)

        y = (jax.nn.sigmoid(gate_fox) * jnp.einsum('bse,ed->bsd', y_fox, w_branch_fox[l])
             + jax.nn.sigmoid(gate_gdn) * jnp.einsum('bse,ed->bsd', y_gdn, w_branch_gdn[l]))
        h = h + jnp.einsum('bsd,de->bse', y, w_out[l])

        hn = rmsnorm(h, norm_ffn[l])
        up = causal_dwconv(jnp.einsum('bsd,df->bsf', hn, w_up[l]), ffn_conv_w[l])
        u_gate, u_val = jnp.split(up, 2, axis=-1)
        h = h + jnp.einsum('bsf,fd->bsd', jax.nn.silu(u_gate) * u_val, w_down[l])
    return rmsnorm(h, norm_final)


GRID_W = 64
NA_WIDTH = D_MODEL // 2
NA_HEADS = 8
NA_HEAD_DIM = NA_WIDTH // NA_HEADS
WIN_ROWS_MAX = 8
WIN_COLS = 16
POOL_WIDTH = D_MODEL - NA_WIDTH
POOL_WINDOWS = (2, 4, 8, 16)
POOL_GROUPS = len(POOL_WINDOWS)
POOL_GROUP_DIM = POOL_WIDTH // POOL_GROUPS
MIX_WIDTH = NA_WIDTH + POOL_WIDTH
IN_WIDTH = 3 * NA_WIDTH + POOL_WIDTH
D_FF_2 = -(-8 * D_MODEL // (3 * 256)) * 256


def rms_norm(x, g):
    xf = x.astype(jnp.float32)
    y = xf * lax.rsqrt(jnp.mean(xf * xf, axis=-1, keepdims=True) + EPS)
    return (y * g.astype(jnp.float32)).astype(x.dtype)

def neighbourhood_attention(q, k, v, rpb):
    B, T, H, Dh = q.shape
    rows = T // GRID_W
    wr = min(WIN_ROWS_MAX, rows)
    q = q.reshape(B, rows, GRID_W, H, Dh)
    k = k.reshape(B, rows, GRID_W, H, Dh)
    v = v.reshape(B, rows, GRID_W, H, Dh)
    row_start = jnp.clip(jnp.arange(rows) - wr // 2, 0, rows - wr)
    cols = jnp.arange(GRID_W)
    col_idx = jnp.clip(cols - WIN_COLS // 2, 0, GRID_W - WIN_COLS)[:, None] + jnp.arange(WIN_COLS)
    col_rel = col_idx - cols[:, None] + (WIN_COLS - 1)
    rpb_cols = rpb.astype(jnp.float32)[:, :, col_rel]
    scale = Dh ** -0.5

    def one_row(r):
        rs = row_start[r]
        kb = lax.dynamic_slice_in_dim(k, rs, wr, axis=1)
        vb = lax.dynamic_slice_in_dim(v, rs, wr, axis=1)
        kg = kb[:, :, col_idx]
        vg = vb[:, :, col_idx]
        qr = lax.dynamic_index_in_dim(q, r, axis=1, keepdims=False)
        row_rel = rs + jnp.arange(wr) - r + (WIN_ROWS_MAX - 1)
        bias = jnp.transpose(rpb_cols[:, row_rel], (0, 2, 1, 3))
        s = jnp.einsum('bqhd,bwqkhd->bhqwk', qr, kg,
                       preferred_element_type=jnp.float32) * scale + bias[None]
        p = jax.nn.softmax(s.reshape(B, H, GRID_W, wr * WIN_COLS), axis=-1)
        p = p.reshape(B, H, GRID_W, wr, WIN_COLS).astype(v.dtype)
        return jnp.einsum('bhqwk,bwqkhd->bqhd', p, vg)

    out = lax.map(one_row, jnp.arange(rows))
    return jnp.moveaxis(out, 0, 1).reshape(B, T, H * Dh)

def multiscale_pool(u, w_pool, pool_scale):
    B, T, C = u.shape
    uf = u.astype(jnp.float32)
    csum = jnp.concatenate([jnp.zeros((B, 1, C), jnp.float32), jnp.cumsum(uf, axis=1)], axis=1)
    t = jnp.arange(T)
    outs = []
    for g, w in enumerate(POOL_WINDOWS):
        sl = slice(g * POOL_GROUP_DIM, (g + 1) * POOL_GROUP_DIM)
        lo = jnp.clip(t - w // 2, 0, T)
        hi = jnp.clip(t + w // 2, 0, T)
        cg = csum[:, :, sl]
        mean = (cg[:, hi] - cg[:, lo]) / (hi - lo).astype(jnp.float32)[:, None]
        outs.append(mean - uf[:, :, sl])
    d = jnp.stack(outs, axis=2).astype(u.dtype)
    y = jnp.einsum('btgc,gcd->btgd', d, w_pool).reshape(B, T, C)
    return y * pool_scale

def second_inputs(seed: int = 0) -> dict:
    key = jax.random.key(seed)
    ks = jax.random.split(key, 14)
    f32 = jnp.float32
    nrm = lambda k, shape, fan_in: jax.random.normal(k, shape, f32) * fan_in ** -0.5
    gain = lambda k, shape: 1.0 + 0.02 * jax.random.normal(k, shape, f32)
    return {
        "x": jax.random.normal(ks[0], (BATCH, SEQ, D_MODEL), f32),
        "norm1_g": gain(ks[1], (DEPTH, D_MODEL)),
        "w_in": nrm(ks[2], (DEPTH, D_MODEL, IN_WIDTH), D_MODEL),
        "q_norm_g": gain(ks[3], (DEPTH, NA_HEAD_DIM)),
        "k_norm_g": gain(ks[4], (DEPTH, NA_HEAD_DIM)),
        "rpb": 0.1 * jax.random.normal(ks[5], (DEPTH, NA_HEADS, 2 * WIN_ROWS_MAX - 1, 2 * WIN_COLS - 1), f32),
        "w_pool": nrm(ks[6], (DEPTH, POOL_GROUPS, POOL_GROUP_DIM, POOL_GROUP_DIM), POOL_GROUP_DIM),
        "pool_scale": gain(ks[7], (DEPTH, POOL_WIDTH)),
        "w_out": nrm(ks[8], (DEPTH, MIX_WIDTH, D_MODEL), MIX_WIDTH),
        "norm2_g": gain(ks[9], (DEPTH, D_MODEL)),
        "w_gate": nrm(ks[10], (DEPTH, D_MODEL, D_FF_2), D_MODEL),
        "w_up": nrm(ks[11], (DEPTH, D_MODEL, D_FF_2), D_MODEL),
        "w_down": nrm(ks[12], (DEPTH, D_FF_2, D_MODEL), D_FF_2),
    }

def second_block(x, norm1_g, w_in, q_norm_g, k_norm_g, rpb, w_pool, pool_scale, w_out,
              norm2_g, w_gate, w_up, w_down):
    B, T, _ = x.shape
    for l in range(DEPTH):
        h = rms_norm(x, norm1_g[l])
        proj = h @ w_in[l]
        q = proj[..., :NA_WIDTH].reshape(B, T, NA_HEADS, NA_HEAD_DIM)
        k = proj[..., NA_WIDTH:2 * NA_WIDTH].reshape(B, T, NA_HEADS, NA_HEAD_DIM)
        v = proj[..., 2 * NA_WIDTH:3 * NA_WIDTH].reshape(B, T, NA_HEADS, NA_HEAD_DIM)
        u = proj[..., 3 * NA_WIDTH:]
        q = rms_norm(q, q_norm_g[l])
        k = rms_norm(k, k_norm_g[l])
        a = neighbourhood_attention(q, k, v, rpb[l])
        p = multiscale_pool(u, w_pool[l], pool_scale[l])
        x = x + jnp.concatenate([a, p], axis=-1) @ w_out[l]
        h2 = rms_norm(x, norm2_g[l])
        x = x + (jax.nn.silu(h2 @ w_gate[l]) * (h2 @ w_up[l])) @ w_down[l]
    return x


def setup_inputs(seed=0):
    out = dict(first_inputs(seed))
    for name, value in second_inputs(seed + 1).items():
        if name != "x":
            out[name + "_2"] = value
    return out


def reference(
    x, norm_mix, w_in, fox_f_bias, gdn_conv_w, gdn_a_log, gdn_dt_bias, gdn_norm, w_branch_fox,
    w_branch_gdn, w_out, norm_ffn, w_up, ffn_conv_w, w_down, norm_final, norm1_g_2, w_in_2,
    q_norm_g_2, k_norm_g_2, rpb_2, w_pool_2, pool_scale_2, w_out_2, norm2_g_2, w_gate_2, w_up_2,
    w_down_2,
):
    x = first_block(
        x, norm_mix, w_in, fox_f_bias, gdn_conv_w, gdn_a_log, gdn_dt_bias, gdn_norm,
        w_branch_fox, w_branch_gdn, w_out, norm_ffn, w_up, ffn_conv_w, w_down, norm_final,
    )
    return second_block(
        x, norm1_g_2, w_in_2, q_norm_g_2, k_norm_g_2, rpb_2, w_pool_2, pool_scale_2, w_out_2,
        norm2_g_2, w_gate_2, w_up_2, w_down_2,
    )


_drawn_inputs = setup_inputs


def setup_inputs(seed=0):
    import zlib

    import numpy as np

    out = dict(_drawn_inputs(seed))
    spreads = {}
    factors = {'gdn_norm': 2.929,
     'norm1_g_2': 4.546,
     'q_norm_g_2': 8.0,
     'k_norm_g_2': 8.0,
     'rpb_2': 19.992,
     'pool_scale_2': 5.232,
     'norm2_g_2': 12.524}
    for name, (base, spread) in spreads.items():
        noise = np.random.default_rng([zlib.crc32(name.encode()), seed]).standard_normal(out[name].shape)
        drawn = base * np.exp(spread * noise) if base else spread * noise
        out[name] = __import__('jax').numpy.asarray(drawn.astype(out[name].dtype))
    for name, factor in factors.items():
        out[name] = (out[name] * factor).astype(out[name].dtype)
    return out
```

```python
from contextlib import ExitStack

import numpy as np

import concourse.bass as bass
from concourse import mybir

F32 = mybir.dt.float32
F32R = mybir.dt.float32r
ALU = mybir.AluOpType
ACT = mybir.ActivationFunctionType
AX = mybir.AxisListType

P = 128
T = 256
TT = T // P
D = 1024
KD = D // P
HEADS = 8
DH = 128
UNITS = HEADS * TT
FF = 2816
KF = FF // P
PW = 256
EPS = 1e-6
NEG = -1e30
GRID = 64
GRID_ROWS = T // GRID
WIN_COLS = 16
RPB_ROWS, RPB_COLS = 15, 31
NA_DIM = 64
NA_W = HEADS * NA_DIM
POOL_WINDOWS = (2, 4, 8, 16)
BLOCK = 16
NBLK = P // BLOCK

SIZES = (D, D, D, HEADS, D, D, D, HEADS, HEADS, D, D, D)
C_FQ, C_FK, C_FV, C_FF, C_GQ, C_GK, C_GV, C_GA, C_GB, C_GZ, C_GF, C_GG = (sum(SIZES[:i]) for i in range(12))
SMALL = 3 * HEADS

PARAMS = {}
_at = 0
for _name, _n in (("norm_mix", KD), ("norm_ffn", KD), ("norm1", KD), ("norm2", KD), ("gconv", 24 * 4),
                  ("fconv", 2 * KF * 3), ("gdn_norm", 1), ("pool_scale", 4), ("qg", 1), ("kg", 1),
                  ("gate_bias", 2 * HEADS), ("a_log", HEADS)):
    PARAMS[_name] = (_at, _at + _n)
    _at += _n
N_PARAMS = _at

CONSTS = {}
_at = 0
for _name, _n in (("ident", P), ("upper", P), ("ones", P), ("causal", 3 * P), ("decay_mask", P),
                  ("level", 3 * P)):
    CONSTS[_name] = (_at, _at + _n)
    _at += _n
N_CONSTS = _at


class Queue:

    def __init__(self, engine, sem):
        self.engine, self.sem, self.count, self.seen = engine, sem, 0, {}

    def wait(self, *tokens):
        for token in tokens:
            if token is None:
                continue
            sem, value = token
            if self.seen.get(id(sem), 0) < value:
                self.seen[id(sem)] = value
                self.engine.wait_ge(sem, value)

    def run(self, make, *after, signal=True):
        self.wait(*after)
        if not signal:
            make(self.engine)
            return None
        self.count += 1
        make(self.engine).then_inc(self.sem, 1)
        return (self.sem, self.count)

    def dma(self, sem_box, out, in_, *after):
        self.wait(*after)
        sem_box[1] += 16
        self.engine.dma_start(out, in_).then_inc(sem_box[0], 16)
        return (sem_box[0], sem_box[1])


class Slots:

    def __init__(self, buffers):
        self.buffers, self.readers, self.at = buffers, [[] for _ in buffers], 0

    def take(self):
        n = self.at % len(self.buffers)
        self.at += 1
        return n, self.buffers[n], list(self.readers[n])

    def free(self, n, *tokens):
        self.readers[n] = list(tokens)


def build(nc, a, out, scratch_a, scratch_x):
    ctx = ExitStack()
    with ctx:
        def sem(name):
            return ctx.enter_context(nc.semaphore(name))

        PE, DVE, SC, PL, SP = (Queue(e, sem(f"done_{n}")) for n, e in (
            ("pe", nc.tensor), ("dve", nc.vector), ("act", nc.scalar), ("pool", nc.gpsimd), ("sp", nc.sync)))

        BASE, UNIT = 16512, 8192

        def at(name, shape, unit, dt=F32, skip=0):
            return nc.alloc_sbuf_tensor_at(name, shape, dt, offset=BASE + int(unit * UNIT) + skip)[:]

        h_first = at("h_first", [P, TT, D], 0)
        xhi = at("xhi", [P, KD, T], 1, F32R)
        xlo = at("xlo", [P, KD, T], 2, F32R)
        raw = Slots([at(f"panel_raw{i}", [P, KD, PW], 3 + i) for i in range(3)])
        split = Slots([(at(f"panel_hi{i}", [P, KD, PW], 6 + i, F32R), at(f"panel_lo{i}", [P, KD, PW], 8 + i, F32R))
                       for i in range(2)])
        normed = at("normed", [P, TT, D], 10)
        acc_t = Slots([at(f"conv_acc{i}", [P, 2, T], 10, skip=2048 * i) for i in range(2)])
        tmp_t = Slots([at(f"conv_tmp{i}", [P, 2, T], 10, skip=4096 + 2048 * i) for i in range(2)])
        fox_p = Slots([at(f"fox_p{i}", [P, 3 * P], 10, skip=2048 * i) for i in range(2)])
        fox_pT = Slots([at(f"fox_pT{i}", [P, 3 * P], 10, skip=4096 + 2048 * i) for i in range(2)])
        tok_k = at("tok_k", [P, UNITS, DH], 11)
        tok_q = at("tok_q", [P, UNITS, DH], 12)
        tok_v = at("tok_v", [P, UNITS, DH], 13)
        tok_kb = at("tok_kb", [P, UNITS, DH], 14)
        tok_kbe = at("tok_kbe", [P, HEADS, DH], 15)
        tok_kdec = at("tok_kdec", [P, HEADS, DH], 15.5)
        tok_qdec = at("tok_qdec", [P, HEADS, DH], 16)
        qdecT = at("qdecT", [P, HEADS, P], 16.5)
        kT = at("kT", [P, UNITS, P], 17)
        qT = at("qT", [P, UNITS, P], 18)
        kbT = at("kbT", [P, UNITS, P], 19)
        decayT = at("decayT", [P, UNITS, P], 20)
        AT = at("AT", [P, UNITS, P], 11)
        attnT = at("attnT", [P, UNITS, P], 12)
        X = at("X", [P, UNITS, P], 17)
        XT = at("XT", [P, UNITS, P], 18)
        PX = at("PX", [P, UNITS, P], 19)
        BT = at("BT", [P, UNITS, P], 14)
        U0 = at("U0", [P, HEADS, DH], 20)
        U1 = at("U1", [P, HEADS, DH], 20.5)
        nwT = at("nwT", [P, HEADS, P], 11)
        S1 = at("S1", [P, HEADS, DH], 11.5)
        o_tok = at("o_tok", [P, UNITS, DH], 14)
        qfT = at("qfT", [P, HEADS, T], 21)
        kfT = at("kfT", [P, HEADS, T], 22)
        yfh = at("yf_hi", [P, HEADS, T], 21, F32R)
        yfl = at("yf_lo", [P, HEADS, T], 22, F32R)
        vf = at("vf", [P, TT, D], 23)
        gz = at("gz", [P, TT, D], 24)
        gate_f = at("gate_f", [P, KD, T], 0)
        gate_g = at("gate_g", [P, KD, T], 18)
        ygh = at("yg_hi", [P, HEADS, T], 17, F32R)
        ygl = at("yg_lo", [P, HEADS, T], 19, F32R)
        h = at("h", [P, TT, D], 24)
        acth = at("act_hi", [P, KF, T], 11, F32R)
        actl = at("act_lo", [P, KF, T], 13.75, F32R)
        q2 = at("q2", [P, TT, NA_W], 17)
        k2 = at("k2", [P, TT, NA_W], 17.5)
        v2 = at("v2", [P, TT, NA_W], 18)
        u2 = at("u2", [P, TT, NA_W], 18.5)
        q2T = at("q2T", [P, 4, T], 19)
        k2T = at("k2T", [P, 4, T], 19.5)
        bias2 = at("bias2", [P, HEADS, TT, T], 20)
        band = at("band", [P, 4, TT, T], 22)
        wpool = at("wpool", [P, 4, P], 23)
        poolT = at("poolT", [P, 4, T], 23.25)
        gain_final = at("gain_final", [P, D], 16.5)
        small_at = [BASE + 25 * UNIT]

        def small(name, shape, dt=F32, bytes_=4):
            n = bytes_
            for s in shape[1:]:
                n *= s
            t = nc.alloc_sbuf_tensor_at(name, shape, dt, offset=small_at[0])[:]
            small_at[0] += -(-n // 32) * 32
            return t

        cst = small("constants", [P, N_CONSTS])
        prm = small("params", [P, N_PARAMS])
        st = small("stats", [P, 160])
        blkA = at("blocks_A", [P, BLOCK, BLOCK], 16)
        blkX = at("blocks_X", [P, BLOCK, BLOCK], 16, skip=1024)
        blkT = at("blocks_T", [P, BLOCK * BLOCK], 16, skip=2048)
        wsm = at("small_raw", [P, KD, SMALL], 15)
        wsmh = at("small_hi", [P, KD, SMALL], 15, F32R, skip=1024)
        wsml = at("small_lo", [P, KD, SMALL], 15, F32R, skip=2048)
        row_nc = small("minus_c_rows", [HEADS, T])
        row_gc = at("gc_rows", [HEADS, T], 23)
        gts = at("gates", [P, 512], 23, skip=2048)

        def C(name):
            lo, hi = CONSTS[name]
            return cst[:, lo:hi]

        def PR(name):
            lo, hi = PARAMS[name]
            return prm[:, lo:hi]

        ident, upper, ones = C("ident"), C("upper"), C("ones")
        banks = [ctx.enter_context(nc.psum_tensor(f"bank{i}", [P, 512], F32)) for i in range(8)]
        gemm_banks = Slots([b[:, :] for b in banks[:4]])
        side_banks = Slots([b[:, :] for b in banks[4:]])

        raw_sem = [[sem(f"panel_landed{i}"), 0] for i in range(3)]

        def load(name, out_, in_, *after, q=SP):
            return q.dma([sem(f"landed_{name}"), 0], out_, in_, *after)

        x_in = load("x", h_first, a["x"][0].rearrange("(t p) d -> p t d", p=P))
        c_in = load("constants", cst, a["constants"])
        p_in = load("params", prm, a["params"])
        w_in = a["w_in"][0]

        def w_rows(w, k0, kt, c0, n):
            return w[k0 * P:(k0 + kt) * P, c0:c0 + n].rearrange("(k p) c -> p k c", p=P)

        sm_in = [load("small_f", wsm[:, :, 0:HEADS], w_rows(w_in, 0, KD, C_FF, HEADS)),
                 load("small_ab", wsm[:, :, HEADS:SMALL], w_rows(w_in, 0, KD, C_GA, 2 * HEADS))]

        plan = []
        for c in [C_GK, C_GQ, C_GV, C_GZ, C_FQ, C_FK, C_FV, C_GF, C_GG]:
            plan += [(w_in, 0, KD, c + j * PW) for j in range(4)]
        for j in range(4):
            plan += [(a["w_branch_fox"][0], 0, KD, j * PW), (a["w_branch_gdn"][0], 0, KD, j * PW)]
        plan += [(a["w_out"][0], 0, KD, j * PW) for j in range(4)]
        for j in range(KF // 2):
            plan += [(a["w_up"][0], 0, KD, j * PW), (a["w_up"][0], 0, KD, FF + j * PW)]
        plan += [(a["w_down"][0], k, min(8, KF - k), j * PW) for k in range(0, KF, 8) for j in range(4)]
        plan += [(a["w_in_2"][0], 0, KD, j * PW) for j in range(8)]
        plan += [(a["w_out_2"][0], 0, KD, j * PW) for j in range(4)]
        for j in range(KF // 2):
            plan += [(a["w_gate_2"][0], 0, KD, j * PW), (a["w_up_2"][0], 0, KD, j * PW)]
        plan += [(a["w_down_2"][0], k, min(8, KF - k), j * PW) for k in range(0, KF, 8) for j in range(4)]
        landed, ready = {}, {}

        def fetch(i):
            if i >= len(plan):
                return
            w, k0, kt, c0 = plan[i]
            n, buf, readers = raw.take()
            landed[i] = (n, buf, kt, SP.dma(raw_sem[n], buf[:, 0:kt, :], w_rows(w, k0, kt, c0, PW), *readers))

        def split_panel(i):
            if i >= len(plan):
                return
            n_raw, buf, kt, tok = landed.pop(i)
            n, (hi, lo), readers = split.take()
            t_hi = SC.run(lambda e: e.activation(hi[:, 0:kt, :], buf[:, 0:kt, :], ACT.Copy), tok, *readers)
            t_lo = DVE.run(lambda e: e.tensor_tensor(lo[:, 0:kt, :], buf[:, 0:kt, :], hi[:, 0:kt, :].bitcast(F32),
                                                     ALU.subtract), tok, t_hi, *readers)
            raw.free(n_raw, t_hi, t_lo)
            ready[i] = (n, hi, lo, kt, t_hi, t_lo)
            fetch(i + 3)

        step_no = [0]

        def gemm(bank, bank_free, xh, xl, x_ready, feature_major):
            i = step_no[0]
            step_no[0] += 1
            n, hi, lo, kt, t_hi, t_lo = ready.pop(i)
            split_panel(i + 1)
            PE.wait(*bank_free, *x_ready, t_hi, t_lo)
            last = None
            for j in range(2):
                js = slice(j * P, (j + 1) * P)
                o = bank[:, j * 256:(j + 1) * 256]
                seq = [(xx, ww, k) for k in range(kt) for xx, ww in ((xh, hi), (xl, hi), (xh, lo))]
                for m, (xx, ww, k) in enumerate(seq):
                    st_, sp_ = m == 0, m == len(seq) - 1
                    if feature_major:
                        l, r = ww[:, k, js], xx[:, k, :]
                    else:
                        l, r = xx[:, k, js], ww[:, k, :]
                    last = PE.run(lambda e, o=o, l=l, r=r, a_=st_, b_=sp_: e.matmul(
                        o, l, r, start=a_, stop=b_, skip_group_check=True),
                        signal=(j == 1 and m == len(seq) - 1))
            split.free(n, last)
            return last

        def mm(o, l, r, start=True, stop=True, *after, signal=True):
            return PE.run(lambda e: e.matmul(o, l, r, start=start, stop=stop, skip_group_check=True),
                          *after, signal=signal)

        def tr(o, i_, *after, signal=True):
            return PE.run(lambda e: e.transpose(o, i_, ident), *after, signal=signal)

        def vec(fn, *after):
            return DVE.run(fn, *after)

        def pool(fn, *after):
            return PL.run(fn, (PL.sem, PL.count) if PL.count else None, *after)

        def act(fn, *after):
            return SC.run(fn, *after)

        half_exp = st[:, 127:128]
        t_half = pool(lambda e: e.memset(st[:, 120:128], -0.5))

        def rsqrt(cols, n, *after, scale=1.0):
            t = vec(lambda e: e.tensor_scalar(cols, cols, scale, EPS, ALU.mult, ALU.add), *after)
            return pool(lambda e: e.tensor_tensor(cols, cols, half_exp.broadcast_to([P, n]), ALU.pow), t, t_half)

        def rms(src, out_, *after, out_free=()):
            ss = st[:, 0:2]
            t0 = act(lambda e: e.activation(out_[:, 0, :], src[:, 0, :], ACT.Square, accum_out=st[:, 0:1]),
                     *after, *out_free)
            t1 = vec(lambda e: e.tensor_tensor_reduce(out_[:, 1, :], src[:, 1, :], src[:, 1, :], 1.0, 0.0,
                                                      ALU.mult, ALU.add, st[:, 1:2]), *after, *out_free)
            tr_ = rsqrt(ss, 2, t0, t1, scale=1.0 / D)
            s0 = act(lambda e: e.activation(out_[:, 0, :], src[:, 0, :], ACT.Copy, scale=st[:, 0:1]), tr_)
            s1 = vec(lambda e: e.tensor_scalar(out_[:, 1, :], src[:, 1, :], st[:, 1:2], None, ALU.mult), tr_)
            return [s0, s1]

        def split_from(src, hi, lo, *after):
            t = act(lambda e: e.activation(hi, src, ACT.Copy), *after)
            return vec(lambda e: e.tensor_tensor(lo, src, hi.bitcast(F32), ALU.subtract), t, *after)

        def to_features(gain, src_ready, x_free):
            done = []
            for g in range(4):
                n, bank, free = side_banks.take()
                b3 = bank.rearrange("p (k t) -> p k t", k=2)
                for k in range(2):
                    for t in range(TT):
                        f = 2 * g + k
                        last = tr(b3[:, k, t * P:(t + 1) * P], normed[:, t, f * P:(f + 1) * P],
                                  *free, src_ready[t], signal=(k == 1 and t == 1))
                nt, tmp, tfree = norm_t.take()
                gb = gain[:, 2 * g:2 * g + 2].unsqueeze(2).broadcast_to([P, 2, T])
                t1 = vec(lambda e, b3=b3, gb=gb, tmp=tmp: e.tensor_tensor(tmp, b3, gb, ALU.mult), last, p_in, *tfree)
                side_banks.free(n, t1)
                t2 = split_from(tmp, xhi[:, 2 * g:2 * g + 2, :], xlo[:, 2 * g:2 * g + 2, :], t1, *x_free)
                norm_t.free(nt, t2)
                done.append(t2)
            return done

        norm_t = Slots([at(f"norm_tmp{i}", [P, 2, T], 16.5, skip=2048 * i) for i in range(2)])

        for i in range(3):
            fetch(i)

        PE.wait(c_in)
        r0 = rms(h_first, normed, x_in)
        x_ready = to_features(PR("norm_mix"), r0, ())
        split_panel(0)

        t_prm = [vec(lambda e: e.tensor_scalar(PR("gconv"), PR("gconv"), 0.5, None, ALU.mult), p_in),
                 vec(lambda e: e.tensor_scalar(PR("fconv")[:, 0:KF * 3], PR("fconv")[:, 0:KF * 3], 0.5, None,
                                               ALU.mult)),
                 vec(lambda e: e.tensor_scalar(PR("gdn_norm"), PR("gdn_norm"), 0.5, None, ALU.mult))][-1]

        t_sm = split_from(wsm, wsmh, wsml, *sm_in)
        n, bank, free = side_banks.take()
        PE.wait(*free, *x_ready, t_sm)
        for j in range(TT):
            seq = [(xx, ww, k) for k in range(KD) for xx, ww in ((xhi, wsmh), (xlo, wsmh), (xhi, wsml))]
            for m, (xx, ww, k) in enumerate(seq):
                t_g = mm(bank[:, j * SMALL:(j + 1) * SMALL], xx[:, k, j * P:(j + 1) * P], ww[:, k, :],
                         m == 0, m == len(seq) - 1, signal=(j == 1 and m == len(seq) - 1))
        gsm = gts[:, 0:48].rearrange("p (t c) -> p t c", t=2)
        z = gts[:, 48:80].rearrange("p (t c) -> p t c", t=2)
        em = gts[:, 80:112].rearrange("p (t c) -> p t c", t=2)
        zz = gts[:, 112:144].rearrange("p (t c) -> p t c", t=2)
        z2 = gts[:, 144:176].rearrange("p (t c) -> p t c", t=2)
        lg = gts[:, 176:208].rearrange("p (t c) -> p t c", t=2)
        cum = gts[:, 208:248]
        coef = gts[:, 248:264]
        beta_u = st[:, 16:32]
        gc_u = st[:, 32:48]
        egc_u = st[:, 48:64]
        kdec_s = st[:, 64:72]
        c_u = st[:, 72:88]
        bu = beta_u.rearrange("p (h t) -> p h t", t=2)
        t = vec(lambda e: e.tensor_copy(gsm, bank[:, 0:48].rearrange("p (t c) -> p t c", t=2)), t_g)
        side_banks.free(n, t)
        gb_ = PR("gate_bias").unsqueeze(1).broadcast_to([P, 2, 16])
        t = vec(lambda e: e.tensor_tensor(z, gsm[:, :, 0:16], gb_, ALU.add), t)
        t = vec(lambda e: e.tensor_scalar(z[:, :, 0:8], z[:, :, 0:8], -1.0, None, ALU.mult), t)
        t_abs = vec(lambda e: e.scalar_tensor_tensor(em, z, -1.0, z, ALU.mult, ALU.min), t)
        t_e = act(lambda e: e.activation(em, em, ACT.Exp), t_abs)
        t_tb = act(lambda e: e.activation(bu, gsm[:, :, 16:24].rearrange("p t c -> p c t"), ACT.Tanh, scale=0.5))
        t_beta = vec(lambda e: e.tensor_scalar(beta_u, beta_u, 0.5, 0.5, ALU.mult, ALU.add), t_tb)
        t_al = act(lambda e: e.activation(coef[:, 8:16], PR("a_log"), ACT.Exp), p_in)
        t = vec(lambda e: e.tensor_scalar(coef[:, 8:16], coef[:, 8:16], -1.0, None, ALU.mult), t_al)
        t_coef = vec(lambda e: e.memset(coef[:, 0:8], -1.0))
        t = vec(lambda e: e.tensor_scalar(zz, em, 2.0, None, ALU.add), t_e)
        t = vec(lambda e: e.reciprocal(zz, zz), t)
        t = vec(lambda e: e.tensor_tensor(zz, zz, em, ALU.mult), t)
        t = vec(lambda e: e.tensor_tensor(z2, zz, zz, ALU.mult), t)
        t = vec(lambda e: e.tensor_scalar(lg, z2, 1.0 / 19, None, ALU.mult), t)
        for k in range(8, 0, -1):
            t = vec(lambda e, k=k: e.scalar_tensor_tensor(lg, lg, 1.0 / (2 * k + 1), z2, ALU.add, ALU.mult), t)
        t = vec(lambda e: e.scalar_tensor_tensor(lg, lg, 1.0, zz, ALU.add, ALU.mult), t)
        t = vec(lambda e: e.tensor_scalar(z, z, 0.0, None, ALU.max), t)
        t = vec(lambda e: e.scalar_tensor_tensor(lg, lg, 2.0, z, ALU.mult, ALU.add), t)
        t_lg = vec(lambda e: e.tensor_tensor(lg, lg, coef.unsqueeze(1).broadcast_to([P, 2, 16]), ALU.mult),
                   t, t_coef)
        n, bank, free = side_banks.take()
        PE.wait(t_lg, c_in, *free)
        lg0, lg1 = lg[:, 0, :], lg[:, 1, :]
        mm(bank[:, 0:16], upper, lg0, signal=False)
        mm(bank[:, 16:24], ones, lg0[:, 0:8], True, False, signal=False)
        mm(bank[:, 16:24], upper, lg1[:, 0:8], False, True, signal=False)
        mm(bank[:, 24:32], upper, lg1[:, 8:16], signal=False)
        t_c = mm(bank[:, 32:40], ones, lg0[:, 8:16])
        t = vec(lambda e: e.tensor_copy(cum, bank[:, 0:40]), t_c)
        side_banks.free(n, t)
        n, bank, free = side_banks.take()
        PE.wait(*free)
        for b0, c0 in ((0, 0), (256, 8)):
            mm(bank[0:8, b0:b0 + 128], lg0[:, c0:c0 + 8], upper, signal=False)
            if c0 == 0:
                mm(bank[0:8, b0 + 128:b0 + 256], lg0[:, 0:8], ones, True, False, signal=False)
            t_r = mm(bank[0:8, b0 + 128:b0 + 256], lg1[:, c0:c0 + 8], upper, c0 != 0, True)
        t_nc = vec(lambda e: e.tensor_scalar(row_nc, bank[0:8, 0:256], -1.0, None, ALU.mult), t_r)
        t_rows = vec(lambda e: e.tensor_copy(row_gc, bank[0:8, 256:512]))
        side_banks.free(n, t_rows)
        cu, gu = c_u.rearrange("p (h t) -> p t h", t=2), gc_u.rearrange("p (h t) -> p t h", t=2)
        t = vec(lambda e: e.tensor_copy(cu[:, 0, :], cum[:, 0:8]), t)
        t = vec(lambda e: e.tensor_copy(cu[:, 1, :], cum[:, 16:24]))
        t = vec(lambda e: e.tensor_copy(gu[:, 0, :], cum[:, 8:16]))
        t_gc = vec(lambda e: e.tensor_copy(gu[:, 1, :], cum[:, 24:32]))
        t = vec(lambda e: e.tensor_tensor(kdec_s, cum[:, 32:40], cum[:, 8:16], ALU.subtract))
        t_kdec_s = act(lambda e: e.activation(kdec_s, kdec_s, ACT.Exp), t)
        t_egc = act(lambda e: e.activation(egc_u, gc_u, ACT.Exp), t_gc)

        side = []

        def step_side():
            for g in list(side):
                try:
                    next(g)
                except StopIteration:
                    side.remove(g)

        def projected(feature_major):
            n, bank, free = gemm_banks.take()
            t = gemm(bank, free, xhi, xlo, x_ready, feature_major)
            return n, bank, t

        tok_ready = {}

        def conv_silu(kind, j, dst, after_dst):
            n, bank, t = projected(True)
            b3 = bank.rearrange("p (c t) -> p c t", c=2)
            na, acc, afree = acc_t.take()
            nt, tmp, tfree = tmp_t.take()
            base = PARAMS["gconv"][0]
            first = 8 * kind + 2 * j
            for c in range(2):
                w = base + (first + c) * 4
                t2 = act(lambda e, c=c, w=w: e.activation(acc[:, c, :], b3[:, c, :], ACT.Copy,
                                                          scale=prm[:, w + 3:w + 4]), t, t_prm, *afree)
            prev = [None, None]
            for back in (1, 2, 3):
                for c in range(2):
                    w = base + (first + c) * 4 + 3 - back
                    t3 = prev[c] = vec(lambda e, c=c, w=w, back=back: e.scalar_tensor_tensor(
                        acc[:, c, back:], b3[:, c, 0:T - back], prm[:, w:w + 1], acc[:, c, back:],
                        ALU.mult, ALU.add), t2, prev[c])
            gemm_banks.free(n, t3)
            t4 = act(lambda e: e.activation(tmp, acc, ACT.Tanh), t3, *tfree)
            t5 = vec(lambda e: e.scalar_tensor_tensor(tmp, tmp, 1.0, acc, ALU.add, ALU.mult), t4)
            acc_t.free(na, t5)
            yield
            m, bank2, free = side_banks.take()
            PE.wait(*free, t5)
            b4 = bank2.rearrange("p (u d) -> p u d", u=4)
            for c in range(2):
                for tt in range(TT):
                    t6 = tr(b4[:, 2 * c + tt, :], tmp[:, c, tt * P:(tt + 1) * P], signal=(c == 1 and tt == 1))
            tmp_t.free(nt, t6)
            t7 = act(lambda e: e.activation(dst[:, 4 * j:4 * j + 4, :], b4, ACT.Copy), t6, *after_dst)
            side_banks.free(m, t7)
            tok_ready[kind, j] = t7
            yield

        ss_at = {1: st[:, 88:104], 0: st[:, 104:120]}
        sq = at("squares", [P, 4, DH], 14)
        rn_done = {}

        def inv_norms(kind, src):
            tm = None
            for j in range(4):
                tm = pool(lambda e, j=j: e.tensor_tensor(sq, src[:, 4 * j:4 * j + 4, :], src[:, 4 * j:4 * j + 4, :],
                                                         ALU.mult), tok_ready[kind, j], tm)
                tm = vec(lambda e, j=j: e.tensor_reduce(ss_at[kind][:, 4 * j:4 * j + 4], sq, AX.X, ALU.add), tm)
            rn_done[kind] = rsqrt(ss_at[kind], 16, tm)
            rn_done["sq"] = tm

        def run_all(gens):
            for g in gens:
                next(g)
                step_side()
                side.append(g)

        def per_unit(col, n=UNITS):
            return col.unsqueeze(2).broadcast_to([P, n, DH])

        GK, GQ, GV = 1, 0, 2
        run_all([conv_silu(GK, j, tok_k, ()) for j in range(4)])
        run_all([conv_silu(GQ, j, tok_q, ()) for j in range(4)])
        run_all([conv_silu(GV, j, tok_v, ()) for j in range(4)])

        gdn_out = {}

        def gdn():
            inv_norms(GK, tok_k)
            inv_norms(GQ, tok_q)
            yield
            halves = [slice(0, 8), slice(8, 16)]
            kdone = []
            for s in halves:
                t = vec(lambda e, s=s: e.tensor_tensor(tok_k[:, s, :], tok_k[:, s, :],
                                                       per_unit(ss_at[GK][:, s], 8), ALU.mult), rn_done[GK])
                kdone.append(t)
            t_kb = [pool(lambda e, s=s: e.tensor_tensor(tok_kb[:, s, :], tok_k[:, s, :], per_unit(beta_u[:, s], 8),
                                                        ALU.mult), t, t_beta, rn_done["sq"])
                    for s, t in zip(halves, kdone)]
            tq = vec(lambda e: e.tensor_scalar(ss_at[GQ], ss_at[GQ], float(DH) ** -0.5, None, ALU.mult), rn_done[GQ])
            t_q = [vec(lambda e, s=s: e.tensor_tensor(tok_q[:, s, :], tok_q[:, s, :], per_unit(ss_at[GQ][:, s], 8),
                                                      ALU.mult), tq) for s in halves]
            yield

            def tile(t_, n_):
                return t_.rearrange("p (h t) d -> p h t d", t=2)[:, :, n_, :]

            def tcol(c_, n_):
                return c_.rearrange("p (h t) -> p h t", t=2)[:, :, n_]
            t_qdec = pool(lambda e: e.tensor_tensor(tok_qdec, tile(tok_q, 1), per_unit(tcol(egc_u, 1), 8), ALU.mult),
                          *t_q, t_egc)
            t_v = vec(lambda e: e.tensor_tensor(tok_v, tok_v, per_unit(beta_u), ALU.mult),
                      *[tok_ready[GV, j] for j in range(4)], t_beta)
            kT_r = turn(tok_k, kT, [kdone[0], kdone[1]])
            yield
            t_kbe = pool(lambda e: e.tensor_tensor(tok_kbe, tile(tok_kb, 1), per_unit(tcol(egc_u, 1), 8), ALU.mult),
                         *t_kb, t_egc)
            t_kdec = pool(lambda e: e.tensor_tensor(tok_kdec, tile(tok_k, 0), per_unit(kdec_s, 8), ALU.mult),
                          *kdone, t_kdec_s)
            qT_r = turn(tok_q, qT, t_q)
            yield
            kbT_r = turn(tok_kb, kbT, t_kb)
            dec = []
            for b in range(4):
                n, bank, free = side_banks.take()
                b4 = bank.rearrange("p (u t) -> p u t", u=4)
                for c in range(2):
                    hh = 2 * b + c
                    t = mm(bank[:, c * T:(c + 1) * T], ident[0:8, hh:hh + 1].broadcast_to([8, P]), row_gc,
                           True, True, *free, t_rows, signal=(c == 1))
                us = slice(4 * b, 4 * b + 4)
                t = vec(lambda e, us=us, b4=b4: e.tensor_tensor(decayT[:, us, :], b4, per_unit(gc_u[:, us], 4),
                                                               ALU.subtract), t, t_gc)
                side_banks.free(n, t)
                dec.append(t)
            yield
            t_dec = []
            for b in range(4):
                us = slice(4 * b, 4 * b + 4)
                t = pool(lambda e, us=us: e.tensor_tensor(
                    decayT[:, us, :], decayT[:, us, :],
                    C("decay_mask").unsqueeze(1).broadcast_to([P, 4, P]), ALU.add), dec[b])
                t_dec.append(act(lambda e, us=us: e.activation(decayT[:, us, :], decayT[:, us, :], ACT.Exp), t))
            qd_r = []
            for b in range(2):
                n, bank, free = side_banks.take()
                b4 = bank.rearrange("p (u t) -> p u t", u=4)
                for u in range(4):
                    t = tr(b4[:, u, :], tok_qdec[:, 4 * b + u, :], *free, t_qdec, signal=(u == 3))
                t = act(lambda e, b=b, b4=b4: e.activation(qdecT[:, 4 * b:4 * b + 4, :], b4, ACT.Copy), t)
                side_banks.free(n, t)
                qd_r.append(t)
            yield
            at_r, an_r = [], []
            for dst, lhs_r, rhs, rr, res, wfree in (
                    (AT, kT_r, kbT, kbT_r, at_r, [t_kbe, t_kdec, t_qdec] + kT_r),
                    (attnT, kT_r, qT, qT_r, an_r, qT_r)):
                for b in range(4):
                    n, bank, free = side_banks.take()
                    b4 = bank.rearrange("p (u t) -> p u t", u=4)
                    PE.wait(*free, *lhs_r, *rr)
                    for u in range(4):
                        uu = 4 * b + u
                        t = mm(b4[:, u, :], kT[:, uu, :], rhs[:, uu, :], signal=(u == 3))
                    us = slice(4 * b, 4 * b + 4)
                    t = vec(lambda e, dst=dst, us=us, b4=b4: e.tensor_tensor(dst[:, us, :], b4, decayT[:, us, :],
                                                                             ALU.mult), t, t_dec[b], *wfree)
                    side_banks.free(n, t)
                    res.append(t)
                    kk_last = t
                if dst is AT:
                    yield
            yield
            outs = []
            box = [sem("blocks_out"), 0]
            for b in range(NBLK):
                src = AT[b * BLOCK:(b + 1) * BLOCK, :, b * BLOCK:(b + 1) * BLOCK]
                dst = scratch_a[b].rearrange("u s t -> s u t")
                outs.append(SP.dma(box, dst, src, *at_r))
            t_in = load("blocks_A", blkA, scratch_a.rearrange("b u s t -> (b u) s t"), outs[-1], *qd_r)
            x0 = pool(lambda e: e.memset(X, 0.0), kk_last, an_r[-1], *at_r)
            yield
            yield
            t0 = vec(lambda e: e.tensor_scalar(blkA, blkA, -1.0, None, ALU.mult), t_in)
            t = vec(lambda e: e.memset(blkX, 0.0), *qd_r)
            t = vec(lambda e: e.memset(blkX.rearrange("p a b -> p (a b)")[:, ::BLOCK + 1], 1.0), t)
            for i in range(1, BLOCK):
                t = vec(lambda e, i=i: e.tensor_tensor(
                    blkT[:, 0:i * i].rearrange("p (k j) -> p k j", j=i),
                    blkX[:, 0:i, 0:i].rearrange("p j k -> p k j"),
                    blkA[:, 0:i, i].unsqueeze(1).broadcast_to([P, i, i]), ALU.mult), t, t0)
                t = vec(lambda e, i=i: e.tensor_reduce(
                    blkX[:, i, 0:i], blkT[:, 0:i * i].rearrange("p (k j) -> p k j", j=i), AX.X, ALU.add), t)
            yield
            t = SP.dma([sem("blocks_back"), 0], scratch_x.rearrange("b u s t -> (b u) s t"), blkX, t)
            box = [sem("blocks_in"), 0]
            for b in range(NBLK):
                t_x = SP.dma(box, X[b * BLOCK:(b + 1) * BLOCK, :, b * BLOCK:(b + 1) * BLOCK],
                             scratch_x[b].rearrange("u s t -> s u t"), t, x0)
            yield
            yield
            xT_r = turn(X, XT, [t_x], [kk_last, an_r[-1]])
            x_r = [t_x] * 4
            bt_free = kbT_r + t_kb + [t_kbe]
            yield
            for lv in range(3):
                last_level = lv == 2
                mask = C("level")[:, lv * P:(lv + 1) * P]
                bts = [pool(lambda e, b=b: e.tensor_tensor(
                    BT[:, 4 * b:4 * b + 4, :], AT[:, 4 * b:4 * b + 4, :],
                    mask.unsqueeze(1).broadcast_to([P, 4, P]), ALU.mult), at_r[b], *bt_free) for b in range(4)]
                if lv == 0:
                    yield
                px = []
                for b in range(4):
                    n, bank, free = side_banks.take()
                    b4 = bank.rearrange("p (u t) -> p u t", u=4)
                    PE.wait(*free, bts[b], x_r[b])
                    for u in range(4):
                        t = mm(b4[:, u, :], BT[:, 4 * b + u, :], X[:, 4 * b + u, :], signal=(u == 3))
                    if b % 2:
                        t = act(lambda e, b=b, b4=b4: e.activation(PX[:, 4 * b:4 * b + 4, :], b4, ACT.Copy), t,
                                *bt_free, kk_last)
                    else:
                        t = vec(lambda e, b=b, b4=b4: e.tensor_copy(PX[:, 4 * b:4 * b + 4, :], b4), t,
                                *bt_free, kk_last)
                    side_banks.free(n, t)
                    px.append(t)
                yield
                new_x, new_xt = [], []
                tpes = []
                for b in range(4):
                    us = slice(4 * b, 4 * b + 4)
                    if not last_level:
                        n, bank, free = side_banks.take()
                        b4 = bank.rearrange("p (u t) -> p u t", u=4)
                        PE.wait(*free, px[b], xT_r[b])
                        for u in range(4):
                            t1 = mm(b4[:, u, :], XT[:, 4 * b + u, :], PX[:, 4 * b + u, :], signal=(u == 3))
                    n2, bank2, free2 = side_banks.take()
                    c4 = bank2.rearrange("p (u t) -> p u t", u=4)
                    PE.wait(*free2, px[b], xT_r[b])
                    for u in range(4):
                        t2 = mm(c4[:, u, :], PX[:, 4 * b + u, :], XT[:, 4 * b + u, :], signal=(u == 3))
                    if not last_level:
                        t = vec(lambda e, us=us, b4=b4: e.tensor_tensor(X[:, us, :], X[:, us, :], b4, ALU.subtract),
                                t1)
                        side_banks.free(n, t)
                        new_x.append(t)
                    t = vec(lambda e, us=us, c4=c4: e.tensor_tensor(XT[:, us, :], XT[:, us, :], c4, ALU.subtract), t2)
                    side_banks.free(n2, t)
                    new_xt.append(t)
                    tpes.append(t2)
                x_r, xT_r = new_x, new_xt
                bt_free = [tpes[-1]]
                yield
            u0_r, nw_r, s1_r, u1_r, o_r = [], [], [], [], []

            def four(b, dst, pairs, res, *after, neg=False, dfree=()):
                n, bank, free = side_banks.take()
                b4 = bank.rearrange("p (u t) -> p u t", u=4)
                PE.wait(*free, *after)
                for u in range(4):
                    ps = pairs(4 * b + u)
                    for m, (l, r) in enumerate(ps):
                        t = mm(b4[:, u, :], l, r, m == 0, m == len(ps) - 1,
                               signal=(u == 3 and m == len(ps) - 1))
                if neg or b % 2:
                    t = act(lambda e: e.activation(dst, b4, ACT.Copy, scale=-1.0 if neg else 1.0), t, *dfree)
                else:
                    t = vec(lambda e: e.tensor_copy(dst, b4), t, *dfree)
                side_banks.free(n, t)
                res.append(t)
            hs = [slice(0, 4), slice(4, 8)]
            for b in range(2):
                four(b, U0[:, hs[b], :], lambda q_: [(XT[:, 2 * q_, :], tok_v[:, 2 * q_, :])], u0_r, *xT_r, t_v,
                     dfree=[kk_last, an_r[-1]])
                four(b, nwT[:, hs[b], :], lambda q_: [(tok_kbe[:, q_, :], XT[:, 2 * q_ + 1, :])], nw_r, t_kbe,
                     neg=True, dfree=bts)
            yield
            for b in range(2):
                four(b, S1[:, hs[b], :], lambda q_: [(tok_kdec[:, q_, :], U0[:, q_, :])], s1_r, *u0_r, dfree=bts)
            yield
            for b in range(2):
                four(b, U1[:, hs[b], :], lambda q_: [(XT[:, 2 * q_ + 1, :], tok_v[:, 2 * q_ + 1, :]),
                                                     (nwT[:, q_, :], S1[:, q_, :])], u1_r, *s1_r, *nw_r)
            o4 = o_tok.rearrange("p (h t) d -> p h t d", t=2)
            for b in range(2):
                four(b, o4[:, hs[b], 0, :], lambda q_: [(attnT[:, 2 * q_, :], U0[:, q_, :])], o_r, *u0_r,
                     dfree=bt_free)
            yield
            for b in range(2):
                four(b, o4[:, hs[b], 1, :], lambda q_: [(qdecT[:, q_, :], S1[:, q_, :]),
                                                        (attnT[:, 2 * q_ + 1, :], U1[:, q_, :])], o_r, *u1_r)
            gdn_out["solve_done"] = o_r[-1]
            yield
            t = pool(lambda e: e.tensor_tensor(X, o_tok, o_tok, ALU.mult), *o_r, *u0_r)
            t = vec(lambda e: e.tensor_reduce(st[:, 0:16], X, AX.X, ALU.add), t)
            t_ro = rsqrt(st[:, 0:16], 16, t, scale=1.0 / DH)
            t = vec(lambda e: e.tensor_tensor(o_tok, o_tok, per_unit(st[:, 0:16]), ALU.mult), t_ro)
            t = pool(lambda e: e.tensor_tensor(
                o_tok.rearrange("p (h t) d -> p t h d", t=2), o_tok.rearrange("p (h t) d -> p t h d", t=2),
                gz.rearrange("p t (h d) -> p t h d", h=HEADS), ALU.mult), t, *gz_r)
            gdn_out["gz_done"] = t
            yield
            yg = []
            for b in range(4):
                n, bank, free = side_banks.take()
                b4 = bank.rearrange("p (u t) -> p u t", u=4)
                for u in range(4):
                    tt_ = tr(b4[:, u, :], o_tok[:, 4 * b + u, :], *free, t, signal=(u == 3))
                hi = ygh[:, 2 * b:2 * b + 2, :].rearrange("p h (t q) -> p (h t) q", t=2)
                lo = ygl[:, 2 * b:2 * b + 2, :].rearrange("p h (t q) -> p (h t) q", t=2)
                t1 = act(lambda e, hi=hi, b4=b4: e.activation(hi, b4, ACT.Copy, scale=PR("gdn_norm")), tt_, t_prm,
                         t_ro)
                t2 = vec(lambda e, hi=hi, lo=lo, b4=b4: e.scalar_tensor_tensor(
                    lo, b4, PR("gdn_norm"), hi.bitcast(F32), ALU.mult, ALU.subtract), t1)
                side_banks.free(n, t2)
                yg.append(t2)
            gdn_out["y"] = yg
            yield

        def turn(src, dst, ready_, dfree=()):
            res = []
            for b in range(4):
                n, bank, free = side_banks.take()
                b4 = bank.rearrange("p (u t) -> p u t", u=4)
                PE.wait(*free, *ready_)
                for u in range(4):
                    t = tr(b4[:, u, :], src[:, 4 * b + u, :], signal=(u == 3))
                if b % 2:
                    t = act(lambda e, b=b, b4=b4: e.activation(dst[:, 4 * b:4 * b + 4, :], b4, ACT.Copy), t, *dfree)
                else:
                    t = vec(lambda e, b=b, b4=b4: e.tensor_copy(dst[:, 4 * b:4 * b + 4, :], b4), t, *dfree)
                side_banks.free(n, t)
                res.append(t)
            return res

        side.append(gdn())

        gz_r = []
        for j in range(4):
            n, bank, t = projected(False)
            b3 = bank.rearrange("p (t c) -> p t c", t=2)
            dst = gz[:, :, j * PW:(j + 1) * PW]
            t = act(lambda e, dst=dst, b3=b3: e.activation(dst, b3, ACT.Tanh, scale=0.5), t)
            t = vec(lambda e, dst=dst, b3=b3: e.scalar_tensor_tensor(dst, dst, 1.0, b3, ALU.add, ALU.mult), t)
            gemm_banks.free(n, t)
            gz_r.append(t)
            step_side()
        fox_r = {}
        for name, dst, scale in (("q", qfT, float(DH) ** -0.5), ("k", kfT, 1.0)):
            for j in range(4):
                n, bank, t = projected(True)
                b3 = bank.rearrange("p (c t) -> p c t", c=2)
                t = act(lambda e, dst=dst, b3=b3, j=j, s_=scale: e.activation(dst[:, 2 * j:2 * j + 2, :], b3, ACT.Copy,
                                                                            scale=s_), t)
                gemm_banks.free(n, t)
                fox_r[name, j] = t
                step_side()
        for j in range(4):
            n, bank, t = projected(False)
            b3 = bank.rearrange("p (t c) -> p t c", t=2)
            t = act(lambda e, b3=b3, j=j: e.activation(vf[:, :, j * PW:(j + 1) * PW], b3, ACT.Copy), t)
            gemm_banks.free(n, t)
            fox_r["v", j] = t
            step_side()

        yf = []

        def fox():
            stage = {}
            fst = st[:, 128:128 + 4 * HEADS]
            for i in range(HEADS + 2):
                if i < HEADS:
                    hh = i
                    n, bank, free = side_banks.take()
                    PE.wait(*free, fox_r["q", hh // 2], fox_r["k", hh // 2], t_nc)
                    e_h = ident[0:8, hh:hh + 1].broadcast_to([8, P])
                    mm(bank[:, 0:P], qfT[:, hh, 0:P], kfT[:, hh, 0:P], True, False, signal=False)
                    mm(bank[:, 0:P], e_h, row_nc[:, 0:P], False, True, signal=False)
                    mm(bank[:, P:3 * P], qfT[:, hh, P:T], kfT[:, hh, :], True, False, signal=False)
                    t_s = mm(bank[:, P:3 * P], e_h, row_nc, False, True)
                    npb, pb, pfree = fox_p.take()
                    nm, sm_ = fst[:, 4 * hh:4 * hh + 2], fst[:, 4 * hh + 2:4 * hh + 4]
                    parts = [slice(0, P), slice(P, 3 * P)]
                    tt_ = []
                    for m, s in enumerate(parts):
                        tt_.append(vec(lambda e, s=s, m=m: e.scalar_tensor_tensor(
                            pb[:, s], bank[:, s], c_u[:, 2 * hh + m:2 * hh + m + 1], C("causal")[:, s],
                            ALU.add, ALU.add), t_s, *pfree))
                    side_banks.free(n, tt_[1])
                    tx = []
                    for m, s in enumerate(parts):
                        t = vec(lambda e, s=s, m=m: e.tensor_reduce(nm[:, m:m + 1], pb[:, s], AX.X, ALU.max,
                                                                    negate=True), tt_[m])
                        tx.append(act(lambda e, s=s, m=m: e.activation(pb[:, s], pb[:, s], ACT.Exp,
                                                                      bias=nm[:, m:m + 1],
                                                                      accum_out=sm_[:, m:m + 1]), t))
                    t = vec(lambda e: e.reciprocal(sm_, sm_), *tx)
                    for m, s in enumerate(parts):
                        t_p = vec(lambda e, s=s, m=m: e.tensor_scalar(pb[:, s], pb[:, s], sm_[:, m:m + 1], None,
                                                                      ALU.mult), t)
                    stage[hh] = (npb, pb, t_p, t_s)
                if 1 <= i <= HEADS:
                    hh = i - 1
                    npb, pb, t_p, t_s = stage[hh]
                    n, bank, free = side_banks.take()
                    for u in range(3):
                        t = tr(bank[:, u * P:(u + 1) * P], pb[:, u * P:(u + 1) * P], *free, t_p, signal=(u == 2))
                    fox_p.free(npb, t)
                    nT, pT, tfree = fox_pT.take()
                    t = act(lambda e, bank=bank, pT=pT: e.activation(pT, bank[:, 0:3 * P], ACT.Copy), t, *tfree)
                    side_banks.free(n, t)
                    stage[hh] = (nT, pT, t, t_s)
                if i >= 2:
                    hh = i - 2
                    nT, pT, t, t_s = stage[hh]
                    n, bank, free = side_banks.take()
                    PE.wait(*free, t, *[fox_r["v", j] for j in range(4)])
                    vs = slice(hh * DH, (hh + 1) * DH)
                    mm(bank[:, 0:P], vf[:, 0, vs], pT[:, 0:P], True, True, signal=False)
                    mm(bank[:, P:T], vf[:, 0, vs], pT[:, P:2 * P], True, False, signal=False)
                    t = mm(bank[:, P:T], vf[:, 1, vs], pT[:, 2 * P:3 * P], False, True)
                    fox_pT.free(nT, t)
                    t = split_from(bank[:, 0:T], yfh[:, hh, :], yfl[:, hh, :], t, t_s)
                    side_banks.free(n, t)
                    yf.append(t)
                yield

        side.append(fox())
        gate_r = {}
        for name, dst, dfree in (("f", gate_f, r0), ("g", gate_g, None)):
            for j in range(4):
                if name == "g" and dfree is None:
                    while "solve_done" not in gdn_out:
                        step_side()
                    dfree = [gdn_out["solve_done"]]
                n, bank, t = projected(True)
                b3 = bank.rearrange("p (c t) -> p c t", c=2)
                d = dst[:, 2 * j:2 * j + 2, :]
                t = act(lambda e, d=d, b3=b3: e.activation(d, b3, ACT.Tanh, scale=0.5), t, *dfree)
                gemm_banks.free(n, t)
                gate_r[name, j] = pool(lambda e, d=d: e.tensor_scalar(d, d, 0.5, 0.5, ALU.mult, ALU.add), t)
                x_done = t
                step_side()
        while side:
            step_side()

        yt_tmp = Slots([(at(f"mix_a{i}", [P, 2, T], 10, skip=4096 * i), at(f"mix_b{i}", [P, 2, T], 10,
                                                                           skip=4096 * i + 2048)) for i in range(2)])
        y_r = []
        unit10_free = [yf[-1]]
        for j in range(4):
            n1, b1, f1 = gemm_banks.take()
            t1 = gemm(b1, f1, yfh, yfl, yf, True)
            n2, b2, f2 = gemm_banks.take()
            t2 = gemm(b2, f2, ygh, ygl, gdn_out["y"], True)
            nt, (ma, mb), tfree = yt_tmp.take()
            fs = slice(2 * j, 2 * j + 2)
            r3 = lambda b_: b_.rearrange("p (c t) -> p c t", c=2)
            t1 = vec(lambda e, ma=ma, b1=b1, fs=fs: e.tensor_tensor(ma, r3(b1), gate_f[:, fs, :], ALU.mult), t1,
                     gate_r["f", j], *tfree, *unit10_free)
            t2 = vec(lambda e, mb=mb, b2=b2, fs=fs: e.tensor_tensor(mb, r3(b2), gate_g[:, fs, :], ALU.mult), t2,
                     gate_r["g", j])
            gemm_banks.free(n1, t1)
            gemm_banks.free(n2, t2)
            t = pool(lambda e, ma=ma, mb=mb: e.tensor_tensor(ma, ma, mb, ALU.add), t1, t2)
            t = split_from(ma, xhi[:, fs, :], xlo[:, fs, :], t, x_done)
            yt_tmp.free(nt, t)
            y_r.append(t)
        h_in = load("x_again", h, a["x"][0].rearrange("(t p) d -> p t d", p=P), gdn_out["gz_done"])

        def add_to_h(n, bank, t, j, *after, dst=None):
            hs_ = h[:, :, j * PW:(j + 1) * PW]
            t = vec(lambda e: e.tensor_tensor(hs_, bank.rearrange("p (t c) -> p t c", t=2), hs_, ALU.add), t, *after)
            gemm_banks.free(n, t)
            return t
        h_r = []
        for j in range(4):
            n, bank, free = gemm_banks.take()
            t = gemm(bank, free, xhi, xlo, y_r, False)
            pe_x_done = t
            h_r.append(add_to_h(n, bank, t, j, h_in))

        late = [gdn_out["y"][-1], yf[-1], y_r[-1], pe_x_done]
        box = [sem("rpb_landed"), 0]
        for rq in range(GRID_ROWS):
            dst = bias2[GRID * (rq % 2):GRID * (rq % 2) + GRID, :, rq // 2, :]
            src = a["rpb_skew"][:, :, (3 - rq) * GRID:(3 - rq) * GRID + T]
            t_rpb = SP.dma(box, dst, src, *late)
        band_in = load("band", band, a["bands"], *late)
        wpool_in = load("wpool", wpool, a["w_pool_2"][0].rearrange("g c d -> c g d"), *late)
        gf_src = a["norm_final"]
        for half in range(2):
            part = bias2[GRID * half:GRID * half + GRID].rearrange("p h t (r c) -> p (h t r) c", c=GRID)
            hi_part = part[:, :, 0:GRID - WIN_COLS]
            lo_part = part[:, :, WIN_COLS:GRID]
            t_b = pool(lambda e, v=hi_part: e.affine_select(
                v, v, [[0, 64], [1, GRID - WIN_COLS]], ALU.is_ge, NEG, WIN_COLS // 2, -1), t_rpb)
            t_b = pool(lambda e, v=lo_part: e.affine_select(
                v, v, [[0, 64], [-1, GRID - WIN_COLS]], ALU.is_ge, NEG, WIN_COLS // 2 - 1 - WIN_COLS, 1), t_b)

        def ffn_down(a_r, a_all, *after):
            bks = [gemm_banks.take() for _ in range(4)]
            ts = [None] * 4
            res = []
            for k in range(0, KF, 8):
                for j in range(4):
                    n, bank, free = bks[j]
                    kt = min(8, KF - k)
                    last = k + 8 >= KF
                    t = gemm_acc(bank, free if k == 0 else (), a_r[k // 2:(k + kt) // 2], k, k == 0, last)
                    if last:
                        res.append(add_to_h(n, bank, t, j, *after))
            return res, t

        def gemm_acc(bank, free, x_r_, k0, first, last):
            i = step_no[0]
            step_no[0] += 1
            n, hi, lo, kt, t_hi, t_lo = ready.pop(i)
            split_panel(i + 1)
            PE.wait(*free, *x_r_, t_hi, t_lo)
            for j in range(2):
                o = bank[:, j * 256:(j + 1) * 256]
                seq = [(xx, ww, k) for k in range(kt) for xx, ww in ((acth, hi), (actl, hi), (acth, lo))]
                for m, (xx, ww, k) in enumerate(seq):
                    end = j == 1 and m == len(seq) - 1
                    t = mm(o, xx[:, k0 + k, j * P:(j + 1) * P], ww[:, k, :], first and j == 0 and m == 0,
                           last and m == len(seq) - 1, signal=end)
            split.free(n, t)
            return t

        ff_r0 = rms(h, normed, *h_r, out_free=[y_r[-1]])
        x_ready = to_features(PR("norm_ffn"), ff_r0, [pe_x_done])
        ft = Slots([(at(f"ff_gate{i}", [P, 2, T], 10, skip=4096 * i), at(f"ff_val{i}", [P, 2, T], 10,
                                                                         skip=4096 * i + 2048)) for i in range(2)])
        ft2 = Slots([at(f"ff_tanh{i}", [P, 2, T], 16.5, skip=2048 * i) for i in range(2)])
        a_r = []
        norm_tr_done = x_ready
        for j in range(KF // 2):
            nt, bufs, tfree = ft.take()
            t_c = []
            for side_ in range(2):
                n, bank, t = projected(True)
                b3 = bank.rearrange("p (c t) -> p c t", c=2)
                acc = bufs[side_]
                base = PARAMS["fconv"][0]
                prev = [None, None]
                for c in range(2):
                    w = base + (side_ * KF + 2 * j + c) * 3
                    t2 = act(lambda e, c=c, w=w, acc=acc, b3=b3: e.activation(
                        acc[:, c, :], b3[:, c, :], ACT.Copy, scale=prm[:, w + 2:w + 3]), t, t_prm, *tfree,
                        *norm_tr_done)
                for back in (1, 2):
                    for c in range(2):
                        w = base + (side_ * KF + 2 * j + c) * 3 + 2 - back
                        prev[c] = vec(lambda e, c=c, w=w, back=back, acc=acc, b3=b3: e.scalar_tensor_tensor(
                            acc[:, c, back:], b3[:, c, 0:T - back], prm[:, w:w + 1], acc[:, c, back:],
                            ALU.mult, ALU.add), t2, prev[c])
                gemm_banks.free(n, prev[1])
                t_c.append(prev[1])
            g_, v_ = bufs
            n2, th, hfree = ft2.take()
            t = act(lambda e, g_=g_, th=th: e.activation(th, g_, ACT.Tanh), t_c[0], *hfree, *norm_tr_done)
            t = vec(lambda e, g_=g_, th=th: e.scalar_tensor_tensor(th, th, 1.0, g_, ALU.add, ALU.mult), t)
            t = pool(lambda e, v_=v_, th=th: e.tensor_tensor(th, th, v_, ALU.mult), t, t_c[1])
            ft.free(nt, t)
            t = split_from(th, acth[:, 2 * j:2 * j + 2, :], actl[:, 2 * j:2 * j + 2, :], t, *late)
            ft2.free(n2, t)
            a_r.append(t)
        h_r, pe_down = ffn_down(a_r, a_r)

        gain_in = load("gain_final", gain_final, bass.AP(tensor=gf_src.tensor, offset=gf_src.offset,
                                                         ap=[[0, P], [1, D]]), a_r[-1])
        fin_r = rms(h, normed, *h_r, out_free=[a_r[-1]])
        h2_r = [vec(lambda e, m=m: e.tensor_tensor(h[:, m, :], normed[:, m, :], gain_final, ALU.mult), fin_r[m],
                    gain_in) for m in range(2)]
        n1_r = rms(h, normed, *h2_r)
        x_ready = to_features(PR("norm1"), n1_r, [pe_down])

        tok2 = []
        for dst in (q2, k2, v2, u2):
            for j in range(2):
                n, bank, t = projected(False)
                b3 = bank.rearrange("p (t c) -> p t c", t=2)
                t = act(lambda e, dst=dst, b3=b3, j=j: e.activation(dst[:, :, j * PW:(j + 1) * PW], b3, ACT.Copy),
                        t, *late)
                gemm_banks.free(n, t)
                tok2.append(t)
        x_done = t
        sq2 = at("sq2", [P, TT, NA_W], 10)
        for kk, (src, dstT, gain) in enumerate(((q2, q2T, "qg"), (k2, k2T, "kg"))):
            s4 = src.rearrange("p t (h d) -> p (t h) d", d=NA_DIM)
            ssq = st[:, 16 + 16 * kk:32 + 16 * kk]
            t = pool(lambda e, src=src: e.tensor_tensor(sq2, src, src, ALU.mult), tok2[2 * kk], tok2[2 * kk + 1],
                     *x_ready, *([t] if kk else []))
            t = vec(lambda e, ssq=ssq: e.tensor_reduce(ssq, sq2.rearrange("p t (h d) -> p (t h) d", d=NA_DIM), AX.X,
                                                       ALU.add), t)
            t_sq = t
            tr_ = rsqrt(ssq, 16, t, scale=1.0 / NA_DIM)
            t = vec(lambda e, s4=s4, ssq=ssq: e.tensor_tensor(s4, s4, ssq.unsqueeze(2).broadcast_to([P, 16, NA_DIM]),
                                                              ALU.mult), tr_)
            for b in range(2):
                n, bank, free = side_banks.take()
                b3 = bank.rearrange("p (f t) -> p f t", f=2)
                for f in range(2):
                    for m in range(TT):
                        t2 = tr(b3[:, f, m * P:(m + 1) * P], src[:, m, (2 * b + f) * P:(2 * b + f + 1) * P], *free, t,
                                signal=(f == 1 and m == 1))
                t3 = act(lambda e, b=b, b3=b3, dstT=dstT, gain=gain: e.activation(
                    dstT[:, 2 * b:2 * b + 2, :], b3, ACT.Copy, scale=PR(gain)), t2, *late)
                side_banks.free(n, t3)
            t = t_sq
        mix_r = []
        for g in range(4):
            n, bank, free = side_banks.take()
            for m in range(TT):
                t = mm(bank[:, 0:T], u2[:, m, g * P:(g + 1) * P], band[:, g, m, :], m == 0, m == 1, *free,
                       *tok2[6:8], band_in)
            t = vec(lambda e, g=g, bank=bank: e.tensor_copy(poolT[:, g, :], bank[:, 0:T]), t)
            side_banks.free(n, t)
            n, bank, free = side_banks.take()
            t = mm(bank[:, 0:T], wpool[:, g, :], poolT[:, g, :], True, True, *free, t, wpool_in)
            sc_ = PR("pool_scale")[:, g:g + 1]
            t1 = act(lambda e, g=g, bank=bank, sc_=sc_: e.activation(xhi[:, 4 + g, :], bank[:, 0:T], ACT.Copy,
                                                                     scale=sc_), t, x_done)
            t2 = vec(lambda e, g=g, bank=bank, sc_=sc_: e.scalar_tensor_tensor(
                xlo[:, 4 + g, :], bank[:, 0:T], sc_, xhi[:, 4 + g, :].bitcast(F32), ALU.mult, ALU.subtract), t1)
            side_banks.free(n, t2)
            mix_r.append(t2)
        na_p = Slots([at(f"na_p{i}", [P, TT, T], 10, skip=2048 * i) for i in range(2)])
        na_pT = Slots([at(f"na_pT{i}", [P, TT, T], 10, skip=4096 + 2048 * i) for i in range(2)])
        qk_r = t3
        stage = {}
        nst = st[:, 48:48 + 32].rearrange("p (h c) -> p h c", c=4)
        ybank = {}
        for i in range(HEADS + 2):
            if i < HEADS:
                hh = i
                p0 = NA_DIM * (hh % 2)
                n, bank, free = side_banks.take()
                b3 = bank.rearrange("p (t k) -> p t k", t=2)
                for m in range(TT):
                    t = mm(b3[:, m, :], q2T[p0:p0 + NA_DIM, hh // 2, m * P:(m + 1) * P],
                           k2T[p0:p0 + NA_DIM, hh // 2, :], True, True, *free, qk_r, signal=(m == 1))
                npb, pb, pfree = na_p.take()
                t = vec(lambda e, b3=b3, pb=pb, hh=hh: e.scalar_tensor_tensor(
                    pb, b3, float(NA_DIM) ** -0.5, bias2[:, hh], ALU.mult, ALU.add), t, t_b, t_sq, *pfree)
                side_banks.free(n, t)
                nm, sm_ = nst[:, hh, 0:2], nst[:, hh, 2:4]
                t = vec(lambda e, pb=pb, nm=nm: e.tensor_reduce(nm, pb, AX.X, ALU.max, negate=True), t)
                tx = [act(lambda e, pb=pb, nm=nm, sm_=sm_, m=m: e.activation(
                    pb[:, m, :], pb[:, m, :], ACT.Exp, bias=nm[:, m:m + 1], accum_out=sm_[:, m:m + 1]), t)
                    for m in range(TT)]
                t = vec(lambda e, sm_=sm_: e.reciprocal(sm_, sm_), *tx)
                t = pool(lambda e, pb=pb, sm_=sm_: e.tensor_tensor(pb, pb, sm_.unsqueeze(2).broadcast_to([P, 2, T]),
                                                                   ALU.mult), t)
                stage[hh] = (npb, pb, t)
            if 1 <= i <= HEADS:
                hh = i - 1
                npb, pb, t = stage[hh]
                n, bank, free = side_banks.take()
                b3 = bank.rearrange("p (k t) -> p k t", k=2)
                for k in range(2):
                    for m in range(TT):
                        t2 = tr(b3[:, k, m * P:(m + 1) * P], pb[:, m, k * P:(k + 1) * P], *free, t,
                                signal=(k == 1 and m == 1))
                na_p.free(npb, t2)
                nT, pT, tfree = na_pT.take()
                t = act(lambda e, b3=b3, pT=pT: e.activation(pT, b3, ACT.Copy), t2, *tfree)
                side_banks.free(n, t)
                stage[hh] = (nT, pT, t)
            if i >= 2:
                hh = i - 2
                nT, pT, t = stage[hh]
                p0 = NA_DIM * (hh % 2)
                if hh % 2 == 0:
                    ybank = side_banks.take()
                n, bank, free = ybank
                for k in range(2):
                    t = mm(bank[p0:p0 + NA_DIM, 0:T], v2[:, k, hh * NA_DIM:(hh + 1) * NA_DIM], pT[:, k, :],
                           k == 0, k == 1, *free, t, *tok2[4:6])
                na_pT.free(nT, t)
                if hh % 2:
                    t = split_from(bank[:, 0:T], xhi[:, hh // 2, :], xlo[:, hh // 2, :], t, x_done)
                    side_banks.free(n, t)
                    mix_r.append(t)
        h_r = []
        for j in range(4):
            n, bank, free = gemm_banks.take()
            t = gemm(bank, free, xhi, xlo, mix_r, False)
            h_r.append(add_to_h(n, bank, t, j))
        pe_x_done = t

        g_r = rms(h, normed, *h_r, out_free=[mix_r[-1]])
        x_ready = to_features(PR("norm2"), g_r, [pe_x_done])
        a_r = []
        ft = Slots([(at(f"f2_a{i}", [P, 2, T], 10, skip=4096 * i), at(f"f2_b{i}", [P, 2, T], 10,
                                                                      skip=4096 * i + 2048)) for i in range(2)])
        for j in range(KF // 2):
            nt, (ga, va), tfree = ft.take()
            n, bank, t = projected(True)
            b3 = bank.rearrange("p (c t) -> p c t", c=2)
            t = act(lambda e, ga=ga, b3=b3: e.activation(ga, b3, ACT.Tanh, scale=0.5), t, *tfree, *x_ready)
            t_g = vec(lambda e, ga=ga, b3=b3: e.scalar_tensor_tensor(ga, ga, 1.0, b3, ALU.add, ALU.mult), t)
            gemm_banks.free(n, t_g)
            n, bank, t = projected(True)
            b3 = bank.rearrange("p (c t) -> p c t", c=2)
            t = vec(lambda e, ga=ga, va=va, b3=b3: e.scalar_tensor_tensor(va, b3, 0.5, ga, ALU.mult, ALU.mult), t,
                    t_g, *tfree)
            gemm_banks.free(n, t)
            t = split_from(va, acth[:, 2 * j:2 * j + 2, :], actl[:, 2 * j:2 * j + 2, :], t, pe_down)
            ft.free(nt, t)
            a_r.append(t)
        h_r, _ = ffn_down(a_r, a_r)
        outbox = [sem("output_written"), 0]
        for j in range(4):
            t_out = SP.dma(outbox, out[0].rearrange("(t p) d -> p t d", p=P)[:, :, j * PW:(j + 1) * PW],
                           h[:, :, j * PW:(j + 1) * PW], h_r[j])
        SP.wait(t_out)


def _constants():
    c = np.zeros((P, N_CONSTS), np.float32)
    i, j = np.indices((P, P))
    c[:, slice(*CONSTS["ident"])] = np.eye(P)
    c[:, slice(*CONSTS["upper"])] = i <= j
    c[:, slice(*CONSTS["ones"])] = 1
    causal = np.where(j <= i, 0, NEG)
    c[:, slice(*CONSTS["causal"])] = np.concatenate([causal, 0 * causal, causal], 1)
    c[:, slice(*CONSTS["decay_mask"])] = np.where(i <= j, 0, NEG)
    for n, side in enumerate((16, 32, 64)):
        lo = CONSTS["level"][0] + n * P
        c[:, lo:lo + P] = (i // (2 * side) == j // (2 * side)) & (i % (2 * side) < side) & (j % (2 * side) >= side)
    return c


def _bands():
    t = np.arange(T)
    b = np.zeros((4, T, T), np.float32)
    for g, w in enumerate(POOL_WINDOWS):
        lo, hi = np.clip(t - w // 2, 0, T), np.clip(t + w // 2, 0, T)
        inside = (t[:, None] >= lo[None]) & (t[:, None] < hi[None])
        b[g] = inside / (hi - lo)[None].astype(np.float32) - np.eye(T)
    return np.ascontiguousarray(b.reshape(4, TT, P, T).transpose(2, 0, 1, 3))


_BIG = ["x", "w_in", "w_branch_fox", "w_branch_gdn", "w_out", "w_up", "w_down", "norm_final", "w_in_2",
        "w_pool_2", "w_out_2", "w_gate_2", "w_up_2", "w_down_2"]


def kernel(**inputs):
    import concourse.bacc as bacc
    from concourse.bass_utils import run_bass_kernel_spmd

    def g(name):
        return np.asarray(inputs[name])

    def tiles(v):
        return v.reshape(-1, P).T

    params = np.empty((P, N_PARAMS), np.float32)
    for name, v in (("norm_mix", tiles(g("norm_mix")[0])), ("norm_ffn", tiles(g("norm_ffn")[0])),
                    ("norm1", tiles(g("norm1_g_2")[0])), ("norm2", tiles(g("norm2_g_2")[0])),
                    ("gconv", g("gdn_conv_w")[0].reshape(4, 24, P).transpose(2, 1, 0).reshape(P, 96)),
                    ("fconv", g("ffn_conv_w")[0].reshape(3, 2 * KF, P).transpose(2, 1, 0).reshape(P, 2 * KF * 3)),
                    ("gdn_norm", g("gdn_norm").T), ("pool_scale", tiles(g("pool_scale_2")[0])),
                    ("qg", np.tile(g("q_norm_g_2")[0], 2)[:, None]), ("kg", np.tile(g("k_norm_g_2")[0], 2)[:, None]),
                    ("gate_bias", np.concatenate([g("fox_f_bias"), g("gdn_dt_bias")], 1)),
                    ("a_log", g("gdn_a_log"))):
        params[:, slice(*PARAMS[name])] = v
    nc = bacc.Bacc("TRN2", target_bir_lowering=False, num_devices=1)
    arrays, args = {}, {}
    feed = {n: np.ascontiguousarray(g(n)) for n in _BIG}
    col = np.arange(GRID)
    rel = np.clip(col[None] - col[:, None] + WIN_COLS - 1, 0, RPB_COLS - 1)
    skew = g("rpb_2")[0][:, 4:11][:, :, rel].transpose(2, 0, 1, 3).reshape(GRID, HEADS, 7 * GRID)
    feed.update(rpb_skew=np.ascontiguousarray(skew), params=params, constants=_constants(), bands=_bands())
    for name, v in feed.items():
        arrays[f"in_{name}"] = v
        args[name] = nc.dram_tensor(f"in_{name}", v.shape, F32, kind="ExternalInput").ap()
    out = nc.dram_tensor("out", (1, T, D), F32, kind="ExternalOutput").ap()
    sa = nc.dram_tensor("blocks_to_invert", (NBLK, UNITS, BLOCK, BLOCK), F32).ap()
    sx = nc.dram_tensor("blocks_inverted", (NBLK, UNITS, BLOCK, BLOCK), F32).ap()
    build(nc, args, out, sa, sx)
    r = run_bass_kernel_spmd(nc, [arrays], core_ids=[0])
    return r.results[0]["out"]
```

```python
from contextlib import ExitStack

import numpy as np

import concourse.bass as bass
from concourse import mybir

F32 = mybir.dt.float32
F32R = mybir.dt.float32r
ALU = mybir.AluOpType
ACT = mybir.ActivationFunctionType
AX = mybir.AxisListType

P = 128
T = 256
TT = T // P
D = 1024
KD = D // P
HEADS = 8
DH = 128
UNITS = HEADS * TT
FF = 2816
KF = FF // P
PW = 256
HALF = 4
AHEAD = 3
EPS = 1e-6
NEG = -1e30
GRID = 64
GRID_ROWS = T // GRID
WIN_COLS = 16
RPB_ROWS, RPB_COLS = 15, 31
NA_DIM = 64
NA_W = HEADS * NA_DIM
POOL_WINDOWS = (2, 4, 8, 16)
BLOCK = 16
NBLK = P // BLOCK

SIZES = (D, D, D, HEADS, D, D, D, HEADS, HEADS, D, D, D)
C_FQ, C_FK, C_FV, C_FF, C_GQ, C_GK, C_GV, C_GA, C_GB, C_GZ, C_GF, C_GG = (sum(SIZES[:i]) for i in range(12))
SMALL = 3 * HEADS

PARAMS = {}
_at = 0
for _name, _n in (("norm_mix", KD), ("norm_ffn", KD), ("norm1", KD), ("norm2", KD), ("norm_final", KD), ("gconv", 24 * 4),
                  ("fconv", 2 * KF * 3), ("gdn_norm", 1), ("pool_scale", 4), ("qg", 1), ("kg", 1),
                  ("gate_bias", 2 * HEADS), ("a_log", HEADS)):
    PARAMS[_name] = (_at, _at + _n)
    _at += _n
N_PARAMS = _at

CONSTS = {}
_at = 0
for _name, _n in (("ident", P), ("upper", P), ("ones", P), ("causal", 3 * P), ("decay_mask", P),
                  ("level", 3 * P)):
    CONSTS[_name] = (_at, _at + _n)
    _at += _n
N_CONSTS = _at


class Queue:

    def __init__(self, engine, sem):
        self.engine, self.sem, self.count, self.seen = engine, sem, 0, {}

    def wait(self, *tokens):
        for token in tokens:
            if token is None:
                continue
            sem, value = token
            if self.seen.get(id(sem), 0) < value:
                self.seen[id(sem)] = value
                self.engine.wait_ge(sem, value)

    def run(self, make, *after, signal=True):
        self.wait(*after)
        if not signal:
            make(self.engine)
            return None
        self.count += 1
        make(self.engine).then_inc(self.sem, 1)
        return (self.sem, self.count)

    def dma(self, sem_box, out, in_, *after):
        self.wait(*after)
        sem_box[1] += 16
        self.engine.dma_start(out, in_).then_inc(sem_box[0], 16)
        return (sem_box[0], sem_box[1])


class Buffer:

    def __init__(self, ap):
        self.ap, self.readers, self.held = ap, [], False


class Slots:

    def __init__(self, buffers):
        self.buffers, self.at = [b if isinstance(b, Buffer) else Buffer(b) for b in buffers], 0

    def take(self):
        for _ in self.buffers:
            b = self.buffers[self.at % len(self.buffers)]
            self.at += 1
            if not b.held:
                b.held = True
                return b, b.ap, list(b.readers)
        raise AssertionError("every buffer is held")

    def free(self, b, *tokens):
        b.readers, b.held = list(tokens), False


def build(nc, a, out, scratch_a, scratch_x):
    ctx = ExitStack()
    with ctx:
        def sem(name):
            return ctx.enter_context(nc.semaphore(name))

        PE, DVE, SC, PL, SP = (Queue(e, sem(f"done_{n}")) for n, e in (
            ("pe", nc.tensor), ("dve", nc.vector), ("act", nc.scalar), ("pool", nc.gpsimd), ("sp", nc.sync)))

        BASE, UNIT = 16512, 8192

        def at(name, shape, unit, dt=F32, skip=0):
            return nc.alloc_sbuf_tensor_at(name, shape, dt, offset=BASE + int(unit * UNIT) + skip)[:]

        xhi = at("xhi", [P, KD, T], 1, F32R)
        xlo = at("xlo", [P, KD, T], 2, F32R)
        raw = Slots([at(f"panel_raw{i}", [P, KD, PW], 3 + i) for i in range(3)])
        split = Slots([(at(f"panel_hi{i}", [P, HALF, PW], 6 + i / 2, F32R),
                        at(f"panel_lo{i}", [P, HALF, PW], 8 + i / 2, F32R)) for i in range(4)])
        acc_t = Slots([at(f"conv_acc{i}", [P, 2, T], 10, skip=2048 * i) for i in range(2)])
        tmp_t = Slots([at(f"conv_tmp{i}", [P, 2, T], 10, skip=4096 + 2048 * i) for i in range(2)])
        fox_p = Slots([at(f"fox_p{i}", [P, 3 * P], 10, skip=1536 * i) for i in range(3)])
        fox_pT = Slots([at(f"fox_pT{i}", [P, 3 * P], 10, skip=4608 + 1536 * i) for i in range(2)])
        tok_k = at("tok_k", [P, UNITS, DH], 11)
        tok_q = at("tok_q", [P, UNITS, DH], 12)
        tok_v = at("tok_v", [P, UNITS, DH], 13)
        tok_kb = at("tok_kb", [P, UNITS, DH], 14)
        tok_kbe = at("tok_kbe", [P, HEADS, DH], 15)
        tok_kdec = at("tok_kdec", [P, HEADS, DH], 15.5)
        tok_qdec = at("tok_qdec", [P, HEADS, DH], 16)
        qdecT = at("qdecT", [P, HEADS, P], 16.5)
        kT = at("kT", [P, UNITS, P], 17)
        qT = at("qT", [P, UNITS, P], 18)
        kbT = at("kbT", [P, UNITS, P], 19)
        decayT = at("decayT", [P, UNITS, P], 20)
        AT = at("AT", [P, UNITS, P], 11)
        attnT = at("attnT", [P, UNITS, P], 12)
        X = at("X", [P, UNITS, P], 17)
        XT = at("XT", [P, UNITS, P], 18)
        PX = at("PX", [P, UNITS, P], 19)
        BT = at("BT", [P, UNITS, P], 14)
        U0 = at("U0", [P, HEADS, DH], 20)
        U1 = at("U1", [P, HEADS, DH], 20.5)
        nwT = at("nwT", [P, HEADS, P], 11)
        S1 = at("S1", [P, HEADS, DH], 11.5)
        o_tok = at("o_tok", [P, UNITS, DH], 14)
        qfT = at("qfT", [P, HEADS, T], 21)
        kfT = at("kfT", [P, HEADS, T], 22)
        yfh = at("yf_hi", [P, HEADS, T], 21, F32R)
        yfl = at("yf_lo", [P, HEADS, T], 22, F32R)
        vf = at("vf", [P, TT, D], 23)
        gz = at("gz", [P, TT, D], 24)
        gate_f = at("gate_f", [P, KD, T], 0)
        gate_g = at("gate_g", [P, KD, T], 18)
        ygh = at("yg_hi", [P, HEADS, T], 17, F32R)
        ygl = at("yg_lo", [P, HEADS, T], 19, F32R)
        h = at("h", [P, TT, D], 24)
        acth = at("act_hi", [P, KF, T], 11, F32R)
        actl = at("act_lo", [P, KF, T], 13.75, F32R)
        q2 = at("q2", [P, TT, NA_W], 17)
        k2 = at("k2", [P, TT, NA_W], 17.5)
        v2 = at("v2", [P, TT, NA_W], 18)
        u2 = at("u2", [P, TT, NA_W], 18.5)
        q2T = at("q2T", [P, 4, T], 19)
        k2T = at("k2T", [P, 4, T], 19.5)
        bias2 = at("bias2", [P, HEADS, TT, T], 20)
        band = at("band", [P, 4, TT, T], 22)
        wpool = at("wpool", [P, 4, P], 23)
        poolT = at("poolT", [P, 4, T], 23.25)
        gain_final = at("gain_final", [P, D], 19.5)
        small_at = [BASE + 25 * UNIT]

        def small(name, shape, dt=F32, bytes_=4):
            n = bytes_
            for s in shape[1:]:
                n *= s
            t = nc.alloc_sbuf_tensor_at(name, shape, dt, offset=small_at[0])[:]
            small_at[0] += -(-n // 32) * 32
            return t

        cst = small("constants", [P, N_CONSTS])
        prm = small("params", [P, N_PARAMS])
        st = small("stats", [P, 160])
        blkA = at("blocks_A", [P, BLOCK, BLOCK], 16)
        blkX = at("blocks_X", [P, BLOCK, BLOCK], 16, skip=1024)
        blkT = at("blocks_T", [P, BLOCK * BLOCK], 16, skip=2048)
        wsm = at("small_raw", [P, KD, SMALL], 15)
        wsmh = at("small_hi", [P, KD, SMALL], 15, F32R, skip=1024)
        wsml = at("small_lo", [P, KD, SMALL], 15, F32R, skip=2048)
        row_nc = small("minus_c_rows", [HEADS, T])
        row_gc = at("gc_rows", [HEADS, T], 23)
        gts = at("gates", [P, 528], 23, skip=2048)

        def C(name):
            lo, hi = CONSTS[name]
            return cst[:, lo:hi]

        def PR(name):
            lo, hi = PARAMS[name]
            return prm[:, lo:hi]

        ident, upper, ones = C("ident"), C("upper"), C("ones")
        banks = [ctx.enter_context(nc.psum_tensor(f"bank{i}", [P, 512], F32)) for i in range(8)]
        banks = [Buffer(b[:, :]) for b in banks]
        few_banks, fox_banks, gemm_banks = Slots(banks[:2]), Slots(banks[2:4]), Slots(banks[:4])
        side_banks = Slots(banks[4:])

        raw_sem = [[sem(f"panel_landed{i}"), 0] for i in range(3)]

        def load(name, out_, in_, *after, q=SP):
            return q.dma([sem(f"landed_{name}"), 0], out_, in_, *after)

        x_in = load("x", h, a["x"][0].rearrange("(t p) d -> p t d", p=P))
        c_in = load("constants", cst, a["constants"])
        p_in = load("params", prm, a["params"])
        w_in = a["w_in"][0]

        def w_rows(w, k0, kt, c0, n):
            return w[k0 * P:(k0 + kt) * P, c0:c0 + n].rearrange("(k p) c -> p k c", p=P)

        sm_in = [load("small_f", wsm[:, :, 0:HEADS], w_rows(w_in, 0, KD, C_FF, HEADS)),
                 load("small_ab", wsm[:, :, HEADS:SMALL], w_rows(w_in, 0, KD, C_GA, 2 * HEADS))]

        plan = []
        for c in [C_GK, C_GQ, C_GV, C_GZ, C_FQ, C_FK, C_FV, C_GF, C_GG]:
            plan += [(w_in, 0, KD, c + j * PW) for j in range(4)]
        for j in range(4):
            plan += [(a["w_branch_fox"][0], 0, KD, j * PW), (a["w_branch_gdn"][0], 0, KD, j * PW)]
        plan += [(a["w_out"][0], 0, KD, j * PW) for j in range(4)]
        for j in range(KF // 2):
            plan += [(a["w_up"][0], 0, KD, j * PW), (a["w_up"][0], 0, KD, FF + j * PW)]
        plan += [(a["w_down"][0], k, min(8, KF - k), j * PW) for k in range(0, KF, 8) for j in range(4)]
        plan += [(a["w_in_2"][0], 0, KD, j * PW) for j in (0, 1, 2, 3, 6, 7, 4, 5)]
        plan += [(a["w_out_2"][0], k, KD // 2, j * PW) for k in (4, 0) for j in range(4)]
        for j in range(KF // 2):
            plan += [(a["w_gate_2"][0], 0, KD, j * PW), (a["w_up_2"][0], 0, KD, j * PW)]
        plan += [(a["w_down_2"][0], k, min(8, KF - k), j * PW) for k in range(0, KF, 8) for j in range(4)]
        landed, ready = {}, {}

        def fetch(i):
            if i >= len(plan):
                return
            w, k0, kt, c0 = plan[i]
            n, buf, readers = raw.take()
            landed[i] = (n, buf, kt, SP.dma(raw_sem[i % 3], buf[:, 0:kt, :], w_rows(w, k0, kt, c0, PW), *readers))

        halves = [(i, k, min(HALF, kt - k)) for i, (_, _, kt, _) in enumerate(plan) for k in range(0, kt, HALF)]
        split_at, raw_read = [0], {}

        def split_next():
            if split_at[0] >= len(halves):
                return
            i, k0, kt = halves[split_at[0]]
            n_raw, buf, panel_kt, tok = landed[i]
            n, (hi, lo), readers = split.take()
            src = buf[:, k0:k0 + kt, :]
            t_hi = SC.run(lambda e: e.activation(hi[:, 0:kt, :], src, ACT.Copy), tok, *readers)
            t_lo = DVE.run(lambda e: e.tensor_tensor(lo[:, 0:kt, :], src, hi[:, 0:kt, :].bitcast(F32),
                                                     ALU.subtract), tok, t_hi, *readers)
            ready[split_at[0]] = (n, hi, lo, t_hi, t_lo)
            split_at[0] += 1
            if k0 + kt == panel_kt:
                raw.free(n_raw, t_hi, t_lo)
                fetch(i + 3)

        half_no = [0]

        def gemm(bank, bank_free, xh, xl, x_ready, feature_major, k_base=0, first=True, last=True):
            panel = halves[half_no[0]][0]
            PE.wait(*bank_free)
            while half_no[0] < len(halves) and halves[half_no[0]][0] == panel:
                _, k0, kt = halves[half_no[0]]
                n, hi, lo, t_hi, t_lo = ready.pop(half_no[0])
                half_no[0] += 1
                split_next()
                PE.wait(t_hi, t_lo)
                end = k0 + kt == plan[panel][2]
                for j in range(2):
                    js = slice(j * P, (j + 1) * P)
                    o = bank[:, j * 256:(j + 1) * 256]
                    seq = [(xx, ww, k) for k in range(kt) for xx, ww in ((xh, hi), (xl, hi), (xh, lo))]
                    for m, (xx, ww, k) in enumerate(seq):
                        kx = k_base + k0 + k
                        PE.wait(x_ready[kx // 2])
                        l, r = (ww[:, k, js], xx[:, kx, :]) if feature_major else (xx[:, kx, js], ww[:, k, :])
                        done = mm(o, l, r, first and k0 == 0 and j == 0 and m == 0,
                                  last and end and m == len(seq) - 1, signal=(j == 1 and m == len(seq) - 1))
                split.free(n, done)
                step_side()
            return done

        def mm(o, l, r, start=True, stop=True, *after, signal=True):
            return PE.run(lambda e: e.matmul(o, l, r, start=start, stop=stop, skip_group_check=True),
                          *after, signal=signal)

        def tr(o, i_, *after, signal=True):
            return PE.run(lambda e: e.transpose(o, i_, ident), *after, signal=signal)

        def vec(fn, *after):
            return DVE.run(fn, *after)

        def pool(fn, *after):
            return PL.run(fn, (PL.sem, PL.count) if PL.count else None, *after)

        def act(fn, *after):
            return SC.run(fn, *after)

        half_exp = st[:, 127:128]
        t_half = pool(lambda e: e.memset(half_exp, -0.5))

        def rsqrt(cols, n, *after, scale=1.0):
            t = vec(lambda e: e.tensor_scalar(cols, cols, scale, EPS, ALU.mult, ALU.add), *after)
            return pool(lambda e: e.tensor_tensor(cols, cols, half_exp.broadcast_to([P, n]), ALU.pow), t, t_half)

        norm_junk = [at(f"norm_junk{m}", [P, PW], 10, skip=1024 * m) for m in range(2)]
        norm_gain = Slots([at(f"norm_gained{i}", [P, TT, PW], 10, skip=2048 + 2048 * i) for i in range(2)])
        norm_row = at("norm_row", [P, T], 10, skip=6144)
        norm_tmp = Slots([at(f"norm_tmp{i}", [P, 2, T], 16.5, skip=2048 * i) for i in range(2)])
        row_sums = st[:, 0:16].rearrange("p (s m j) -> p s m j", s=2, m=2)
        rsq = st[:, 120:124]

        junk_done = [None, None]

        class Norm:

            def __init__(self, final_gain=None):
                self.final, self.banks, self.sums, self.fed = final_gain, [], [], []

            def squares(self, j, *after):
                cols = slice(j * PW, (j + 1) * PW)
                srcs = [(0, h[:, :, cols], after)]
                if self.final is not None:
                    n, gained, free = norm_gain.take()
                    t = vec(lambda e: e.tensor_tensor(gained, h[:, :, cols], self.final[:, cols].unsqueeze(1)
                                                      .broadcast_to([P, TT, PW]), ALU.mult), *after, *free)
                    srcs.append((1, gained, (t,)))
                for s, src, need in srcs:
                    t0 = act(lambda e: e.activation(norm_junk[0], src[:, 0, :], ACT.Square,
                                                    accum_out=row_sums[:, s, 0, j:j + 1]), *need, junk_done[0])
                    t1 = vec(lambda e: e.tensor_tensor_reduce(norm_junk[1], src[:, 1, :], src[:, 1, :], 1.0, 0.0,
                                                              ALU.mult, ALU.add, row_sums[:, s, 1, j:j + 1]), *need, junk_done[1])
                    self.sums += [t0, t1]
                    junk_done[:] = [t0, t1]
                if self.final is not None:
                    norm_gain.free(n, t0, t1)

            def transposes(self, *after):
                j = len(self.banks)
                n, bank, free = side_banks.take()
                b3 = bank.rearrange("p (k t) -> p k t", k=2)
                PE.wait(*free, *after)
                for k in range(2):
                    for m in range(TT):
                        f = 2 * j + k
                        t = tr(b3[:, k, m * P:(m + 1) * P], h[:, m, f * P:(f + 1) * P], signal=(k == 1 and m == 1))
                self.banks.append((n, b3, t))

            def finish(self, gain, *x_free):
                S = 1 if self.final is None else 2
                t = vec(lambda e: e.tensor_reduce(rsq[:, 0:2 * S].rearrange("p (s m) -> p s m", s=S),
                                                  row_sums[:, 0:S], AX.X, ALU.add), *self.sums)
                r = rsq[:, 0:2]
                t = rsqrt(r, 2, t, scale=1.0 / D)
                if self.final is not None:
                    r2 = rsq[:, 2:4]
                    t_r1 = t
                    t = vec(lambda e: e.tensor_tensor(r2, r2, r, ALU.mult), t)
                    t = vec(lambda e: e.tensor_tensor(r2, r2, r, ALU.mult), t)
                    t = rsqrt(r2, 2, t, scale=1.0 / D)
                    self.h2_scale = (r, t_r1)
                    rr = st[:, 48:50]
                    t = vec(lambda e: e.tensor_tensor(rr, r2, r, ALU.mult), t)
                    r = rr
                n, bank, free = gemm_banks.take()
                PE.wait(*free, t)
                for m in range(TT):
                    t = mm(bank[:, m * P:(m + 1) * P], r[:, m:m + 1].broadcast_to([P, P]), ident, signal=(m == 1))
                t_row = act(lambda e: e.activation(norm_row, bank[:, 0:T], ACT.Copy), t)
                gemm_banks.free(n, t_row)
                done = []
                for j, (n, b3, t_tr) in enumerate(self.banks):
                    nt, tmp, tfree = norm_tmp.take()
                    for k in range(2):
                        f = 2 * j + k
                        t = vec(lambda e: e.scalar_tensor_tensor(tmp[:, k, :], b3[:, k, :], gain[:, f:f + 1], norm_row,
                                                                 ALU.mult, ALU.mult), t_tr, t_row, t_prm, *tfree)
                    side_banks.free(n, t)
                    t = split_from(tmp, xhi[:, 2 * j:2 * j + 2, :], xlo[:, 2 * j:2 * j + 2, :], t, *x_free)
                    norm_tmp.free(nt, t)
                    done.append(t)
                return done

        def split_from(src, hi, lo, *after):
            t = act(lambda e: e.activation(hi, src, ACT.Copy), *after)
            return vec(lambda e: e.tensor_tensor(lo, src, hi.bitcast(F32), ALU.subtract), t, *after)

        for i in range(3):
            fetch(i)

        PE.wait(c_in)
        side = []

        def step_side():
            for g in list(side):
                try:
                    next(g)
                except StopIteration:
                    side.remove(g)

        t_prm = [vec(lambda e: e.tensor_scalar(PR("gconv"), PR("gconv"), 0.5, None, ALU.mult), p_in),
                 vec(lambda e: e.tensor_scalar(PR("fconv")[:, 0:KF * 3], PR("fconv")[:, 0:KF * 3], 0.5, None,
                                               ALU.mult)),
                 vec(lambda e: e.tensor_scalar(PR("gdn_norm"), PR("gdn_norm"), 0.5, None, ALU.mult)),
                 vec(lambda e: e.tensor_tensor(PR("norm1"), PR("norm1"), PR("norm_final"), ALU.mult))][-1]
        norm = Norm()
        for j in range(4):
            norm.squares(j, x_in)
            norm.transposes(x_in)
        for _ in range(AHEAD):
            split_next()
        x_ready = norm.finish(PR("norm_mix"))

        gsm = gts[:, 0:48].rearrange("p (t c) -> p t c", t=2)
        gateT = gts[0:SMALL, 264:264 + T]
        z = gts[:, 48:80].rearrange("p (t c) -> p t c", t=2)
        em = gts[:, 80:112].rearrange("p (t c) -> p t c", t=2)
        zz = gts[:, 112:144].rearrange("p (t c) -> p t c", t=2)
        z2 = gts[:, 144:176].rearrange("p (t c) -> p t c", t=2)
        lg = gts[:, 176:208].rearrange("p (t c) -> p t c", t=2)
        cum = gts[:, 208:248]
        coef = gts[:, 248:264]
        beta_u = st[:, 16:32]
        gc_u = st[:, 32:48]
        egc_u = st[:, 48:64]
        kdec_s = st[:, 64:72]
        c_u = st[:, 72:88]
        bu = beta_u.rearrange("p (h t) -> p h t", t=2)
        G = {}

        def gates():
            t_sm = split_from(wsm, wsmh, wsml, *sm_in)
            yield
            n, bank, free = side_banks.take()
            PE.wait(*free, *x_ready, t_sm)
            seq = [(xx, ww, k) for k in range(KD) for xx, ww in ((xhi, wsmh), (xlo, wsmh), (xhi, wsml))]
            for m, (xx, ww, k) in enumerate(seq):
                t = mm(bank[0:SMALL, 0:T], ww[:, k, :], xx[:, k, :], m == 0, m == len(seq) - 1,
                       signal=(m == len(seq) - 1))
            t = vec(lambda e: e.tensor_copy(gateT, bank[0:SMALL, 0:T]), t)
            side_banks.free(n, t)
            yield
            n, bank, free = side_banks.take()
            for m in range(TT):
                t_g = PE.run(lambda e: e.transpose(bank[:, m * SMALL:(m + 1) * SMALL], gateT[:, m * P:(m + 1) * P],
                                                   ident[0:SMALL, 0:SMALL]), *free, t)
            t = vec(lambda e: e.tensor_copy(gsm, bank[:, 0:48].rearrange("p (t c) -> p t c", t=2)), t_g)
            side_banks.free(n, t)
            gb_ = PR("gate_bias").unsqueeze(1).broadcast_to([P, 2, 16])
            t = vec(lambda e: e.tensor_tensor(z, gsm[:, :, 0:16], gb_, ALU.add), t)
            t = vec(lambda e: e.tensor_scalar(z[:, :, 0:8], z[:, :, 0:8], -1.0, None, ALU.mult), t)
            t_abs = vec(lambda e: e.scalar_tensor_tensor(em, z, -1.0, z, ALU.mult, ALU.min), t)
            yield
            t_e = act(lambda e: e.activation(em, em, ACT.Exp), t_abs)
            t_tb = act(lambda e: e.activation(bu, gsm[:, :, 16:24].rearrange("p t c -> p c t"), ACT.Tanh, scale=0.5))
            t_beta = G["t_beta"] = vec(lambda e: e.tensor_scalar(beta_u, beta_u, 0.5, 0.5, ALU.mult, ALU.add), t_tb)
            t_al = act(lambda e: e.activation(coef[:, 8:16], PR("a_log"), ACT.Exp), p_in)
            t = vec(lambda e: e.tensor_scalar(coef[:, 8:16], coef[:, 8:16], -1.0, None, ALU.mult), t_al)
            t_coef = vec(lambda e: e.memset(coef[:, 0:8], -1.0))
            yield
            t = vec(lambda e: e.tensor_scalar(zz, em, 2.0, None, ALU.add), t_e)
            t = vec(lambda e: e.reciprocal(zz, zz), t)
            t = vec(lambda e: e.tensor_tensor(zz, zz, em, ALU.mult), t)
            t = vec(lambda e: e.tensor_tensor(z2, zz, zz, ALU.mult), t)
            t = vec(lambda e: e.tensor_scalar(lg, z2, 1.0 / 19, None, ALU.mult), t)
            for k in range(8, 0, -1):
                t = vec(lambda e, k=k: e.scalar_tensor_tensor(lg, lg, 1.0 / (2 * k + 1), z2, ALU.add, ALU.mult), t)
            t = vec(lambda e: e.scalar_tensor_tensor(lg, lg, 1.0, zz, ALU.add, ALU.mult), t)
            t = vec(lambda e: e.tensor_scalar(z, z, 0.0, None, ALU.max), t)
            t = vec(lambda e: e.scalar_tensor_tensor(lg, lg, 2.0, z, ALU.mult, ALU.add), t)
            t_lg = vec(lambda e: e.tensor_tensor(lg, lg, coef.unsqueeze(1).broadcast_to([P, 2, 16]), ALU.mult),
                       t, t_coef)
            yield
            n, bank, free = side_banks.take()
            PE.wait(t_lg, c_in, *free)
            lg0, lg1 = lg[:, 0, :], lg[:, 1, :]
            mm(bank[:, 0:16], upper, lg0, signal=False)
            mm(bank[:, 16:24], ones, lg0[:, 0:8], True, False, signal=False)
            mm(bank[:, 16:24], upper, lg1[:, 0:8], False, True, signal=False)
            mm(bank[:, 24:32], upper, lg1[:, 8:16], signal=False)
            t_c = mm(bank[:, 32:40], ones, lg0[:, 8:16])
            t_cum = t = vec(lambda e: e.tensor_copy(cum, bank[:, 0:40]), t_c)
            side_banks.free(n, t)
            yield
            n, bank, free = side_banks.take()
            PE.wait(*free)
            for b0, c0 in ((0, 0), (256, 8)):
                mm(bank[0:8, b0:b0 + 128], lg0[:, c0:c0 + 8], upper, signal=False)
                if c0 == 0:
                    mm(bank[0:8, b0 + 128:b0 + 256], lg0[:, 0:8], ones, True, False, signal=False)
                t_r = mm(bank[0:8, b0 + 128:b0 + 256], lg1[:, c0:c0 + 8], upper, c0 != 0, True)
            t_nc = G["t_nc"] = vec(lambda e: e.tensor_scalar(row_nc, bank[0:8, 0:256], -1.0, None, ALU.mult), t_r)
            t_rows = G["t_rows"] = vec(lambda e: e.tensor_copy(row_gc, bank[0:8, 256:512]))
            side_banks.free(n, t_rows)
            yield
            cu, gu = c_u.rearrange("p (h t) -> p t h", t=2), gc_u.rearrange("p (h t) -> p t h", t=2)
            t = vec(lambda e: e.tensor_copy(cu[:, 0, :], cum[:, 0:8]), t_cum)
            t = vec(lambda e: e.tensor_copy(cu[:, 1, :], cum[:, 16:24]))
            t = vec(lambda e: e.tensor_copy(gu[:, 0, :], cum[:, 8:16]))
            t_gc = G["t_gc"] = vec(lambda e: e.tensor_copy(gu[:, 1, :], cum[:, 24:32]))
            t = vec(lambda e: e.tensor_tensor(kdec_s, cum[:, 32:40], cum[:, 8:16], ALU.subtract))
            t_kdec_s = G["t_kdec_s"] = act(lambda e: e.activation(kdec_s, kdec_s, ACT.Exp), t)
            t_egc = G["t_egc"] = act(lambda e: e.activation(egc_u, gc_u, ACT.Exp), t_gc)

        side.append(gates())

        bank_pool = [few_banks]

        def projected(feature_major):
            n, bank, free = bank_pool[0].take()
            t = gemm(bank, free, xhi, xlo, x_ready, feature_major)
            return n, bank, t

        tok_ready = {}
        GK, GQ, GV = 1, 0, 2

        def conv_silu(kind, j, dst, after_dst):
            n, bank, t = projected(True)
            b3 = bank.rearrange("p (c t) -> p c t", c=2)
            na, acc, afree = acc_t.take()
            nt, tmp, tfree = tmp_t.take()
            base = PARAMS["gconv"][0]
            first = 8 * kind + 2 * j
            for c in range(2):
                w = base + (first + c) * 4
                t2 = act(lambda e, c=c, w=w: e.activation(acc[:, c, :], b3[:, c, :], ACT.Copy,
                                                          scale=prm[:, w + 3:w + 4]), t, t_prm, *afree)
            prev = [None, None]
            for back in (1, 2, 3):
                for c in range(2):
                    w = base + (first + c) * 4 + 3 - back
                    t3 = prev[c] = vec(lambda e, c=c, w=w, back=back: e.scalar_tensor_tensor(
                        acc[:, c, back:], b3[:, c, 0:T - back], prm[:, w:w + 1], acc[:, c, back:],
                        ALU.mult, ALU.add), t2, prev[c])
            few_banks.free(n, t3)
            yield
            t4 = act(lambda e: e.activation(tmp, acc, ACT.Tanh), t3, *tfree)
            yield
            t5 = vec(lambda e: e.scalar_tensor_tensor(tmp, tmp, 1.0, acc, ALU.add, ALU.mult), t4)
            acc_t.free(na, t5)
            yield
            m, bank2, free = side_banks.take()
            PE.wait(*free, t5)
            b4 = bank2.rearrange("p (u d) -> p u d", u=4)
            for c in range(2):
                for tt in range(TT):
                    t6 = tr(b4[:, 2 * c + tt, :], tmp[:, c, tt * P:(tt + 1) * P], signal=(c == 1 and tt == 1))
            tmp_t.free(nt, t6)
            us = slice(4 * j, 4 * j + 4)
            t7 = act(lambda e: e.activation(dst[:, us, :], b4, ACT.Copy), t6, *after_dst)
            side_banks.free(m, t7)
            tok_ready[kind, j] = t7
            if kind == GV:
                return
            yield
            nq, sq, qfree = sq_t.take()
            t8 = pool(lambda e: e.tensor_tensor(sq, dst[:, us, :], dst[:, us, :], ALU.mult), t7, *qfree)
            yield
            yield
            t9 = vec(lambda e: e.tensor_reduce(ss_at[kind][:, us], sq, AX.X, ALU.add), t8)
            sq_t.free(nq, t9)
            sq_free[0] = t9

        ss_at = {1: st[:, 88:104], 0: st[:, 104:120]}
        sq_t = Slots([at(f"squares{i}", [P, 4, DH], 14, skip=2048 * i) for i in range(3)])
        sq_free = [None]

        def run_all(gens):
            for g in gens:
                next(g)
                side.append(g)

        def per_unit(col, n=UNITS):
            return col.unsqueeze(2).broadcast_to([P, n, DH])

        run_all([conv_silu(GK, j, tok_k, ()) for j in range(4)])
        run_all([conv_silu(GQ, j, tok_q, ()) for j in range(4)])
        run_all([conv_silu(GV, j, tok_v, ()) for j in range(4)])

        gdn_out = {}

        def sq_t_open():
            return any(b.held for b in sq_t.buffers) or len(tok_ready) < 12 or "t_egc" not in G

        def gdn():
            while sq_t_open():
                yield
            rk = rsqrt(ss_at[GK], 16, sq_free[0])
            rq = rsqrt(ss_at[GQ], 16, sq_free[0])
            yield
            halves = [slice(0, 8), slice(8, 16)]
            kdone = []
            for s in halves:
                t = vec(lambda e, s=s: e.tensor_tensor(tok_k[:, s, :], tok_k[:, s, :],
                                                       per_unit(ss_at[GK][:, s], 8), ALU.mult), rk)
                kdone.append(t)
            yield
            t_kb = [pool(lambda e, s=s: e.tensor_tensor(tok_kb[:, s, :], tok_k[:, s, :], per_unit(beta_u[:, s], 8),
                                                        ALU.mult), t, G["t_beta"], sq_free[0])
                    for s, t in zip(halves, kdone)]
            tq = vec(lambda e: e.tensor_scalar(ss_at[GQ], ss_at[GQ], float(DH) ** -0.5, None, ALU.mult), rq)
            t_q = [vec(lambda e, s=s: e.tensor_tensor(tok_q[:, s, :], tok_q[:, s, :], per_unit(ss_at[GQ][:, s], 8),
                                                      ALU.mult), tq) for s in halves]
            yield

            def tile(t_, n_):
                return t_.rearrange("p (h t) d -> p h t d", t=2)[:, :, n_, :]

            def tcol(c_, n_):
                return c_.rearrange("p (h t) -> p h t", t=2)[:, :, n_]
            t_qdec = pool(lambda e: e.tensor_tensor(tok_qdec, tile(tok_q, 1), per_unit(tcol(egc_u, 1), 8), ALU.mult),
                          *t_q, G["t_egc"])
            t_v = vec(lambda e: e.tensor_tensor(tok_v, tok_v, per_unit(beta_u), ALU.mult),
                      *[tok_ready[GV, j] for j in range(4)], G["t_beta"])
            kT_r = turn(tok_k, kT, [kdone[0], kdone[1]])
            yield
            yield
            t_kbe = pool(lambda e: e.tensor_tensor(tok_kbe, tile(tok_kb, 1), per_unit(tcol(egc_u, 1), 8), ALU.mult),
                         *t_kb, G["t_egc"])
            t_kdec = pool(lambda e: e.tensor_tensor(tok_kdec, tile(tok_k, 0), per_unit(kdec_s, 8), ALU.mult),
                          *kdone, G["t_kdec_s"])
            qT_r = turn(tok_q, qT, t_q)
            yield
            kbT_r = turn(tok_kb, kbT, t_kb)
            dec = []
            for b in range(4):
                n, bank, free = side_banks.take()
                b4 = bank.rearrange("p (u t) -> p u t", u=4)
                for c in range(2):
                    hh = 2 * b + c
                    t = mm(bank[:, c * T:(c + 1) * T], ident[0:8, hh:hh + 1].broadcast_to([8, P]), row_gc,
                           True, True, *free, G["t_rows"], signal=(c == 1))
                us = slice(4 * b, 4 * b + 4)
                t = vec(lambda e, us=us, b4=b4: e.tensor_tensor(decayT[:, us, :], b4, per_unit(gc_u[:, us], 4),
                                                               ALU.subtract), t, G["t_gc"])
                side_banks.free(n, t)
                dec.append(t)
            yield
            t_pl = []
            for b in range(4):
                us = slice(4 * b, 4 * b + 4)
                t = pool(lambda e, us=us: e.tensor_tensor(
                    decayT[:, us, :], decayT[:, us, :],
                    C("decay_mask").unsqueeze(1).broadcast_to([P, 4, P]), ALU.add), dec[b])
                t_pl.append(t)
            yield
            yield
            t_dec = [act(lambda e: e.activation(decayT[:, 4 * b:4 * b + 4, :], decayT[:, 4 * b:4 * b + 4, :],
                                                ACT.Exp), t_pl[b]) for b in range(4)]
            qd_r = []
            for b in range(2):
                n, bank, free = side_banks.take()
                b4 = bank.rearrange("p (u t) -> p u t", u=4)
                for u in range(4):
                    t = tr(b4[:, u, :], tok_qdec[:, 4 * b + u, :], *free, t_qdec, signal=(u == 3))
                t = act(lambda e, b=b, b4=b4: e.activation(qdecT[:, 4 * b:4 * b + 4, :], b4, ACT.Copy), t)
                side_banks.free(n, t)
                qd_r.append(t)
            yield
            at_r, an_r = [], []
            for dst, lhs_r, rhs, rr, res, wfree in (
                    (AT, kT_r, kbT, kbT_r, at_r, [t_kbe, t_kdec, t_qdec] + kT_r),
                    (attnT, kT_r, qT, qT_r, an_r, qT_r)):
                for b in range(4):
                    n, bank, free = side_banks.take()
                    b4 = bank.rearrange("p (u t) -> p u t", u=4)
                    PE.wait(*free, *lhs_r, *rr)
                    for u in range(4):
                        uu = 4 * b + u
                        t = mm(b4[:, u, :], kT[:, uu, :], rhs[:, uu, :], signal=(u == 3))
                    us = slice(4 * b, 4 * b + 4)
                    t = vec(lambda e, dst=dst, us=us, b4=b4: e.tensor_tensor(dst[:, us, :], b4, decayT[:, us, :],
                                                                             ALU.mult), t, t_dec[b], *wfree)
                    side_banks.free(n, t)
                    res.append(t)
                    kk_last = t
                if dst is AT:
                    yield
            yield
            outs = []
            box = [sem("blocks_out"), 0]
            for b in range(NBLK):
                src = AT[b * BLOCK:(b + 1) * BLOCK, :, b * BLOCK:(b + 1) * BLOCK]
                dst = scratch_a[b].rearrange("u s t -> s u t")
                outs.append(SP.dma(box, dst, src, *at_r))
            t_in = load("blocks_A", blkA, scratch_a.rearrange("b u s t -> (b u) s t"), outs[-1], *qd_r)
            x0 = pool(lambda e: e.memset(X, 0.0), kk_last, an_r[-1], *at_r)
            yield
            yield
            t0 = vec(lambda e: e.tensor_scalar(blkA, blkA, -1.0, None, ALU.mult), t_in)
            t = vec(lambda e: e.memset(blkX, 0.0), *qd_r)
            t = vec(lambda e: e.memset(blkX.rearrange("p a b -> p (a b)")[:, ::BLOCK + 1], 1.0), t)
            for i in range(1, BLOCK):
                t = vec(lambda e, i=i: e.tensor_tensor(
                    blkT[:, 0:i * i].rearrange("p (k j) -> p k j", j=i),
                    blkX[:, 0:i, 0:i].rearrange("p j k -> p k j"),
                    blkA[:, 0:i, i].unsqueeze(1).broadcast_to([P, i, i]), ALU.mult), t, t0)
                t = vec(lambda e, i=i: e.tensor_reduce(
                    blkX[:, i, 0:i], blkT[:, 0:i * i].rearrange("p (k j) -> p k j", j=i), AX.X, ALU.add), t)
            yield
            t = SP.dma([sem("blocks_back"), 0], scratch_x.rearrange("b u s t -> (b u) s t"), blkX, t)
            box = [sem("blocks_in"), 0]
            for b in range(NBLK):
                t_x = SP.dma(box, X[b * BLOCK:(b + 1) * BLOCK, :, b * BLOCK:(b + 1) * BLOCK],
                             scratch_x[b].rearrange("u s t -> s u t"), t, x0)
            yield
            yield
            xT_r = turn(X, XT, [t_x], [kk_last, an_r[-1]])
            x_r = [t_x] * 4
            bt_free = kbT_r + t_kb + [t_kbe]
            yield
            for lv in range(3):
                last_level = lv == 2
                mask = C("level")[:, lv * P:(lv + 1) * P]
                bts = [pool(lambda e, b=b: e.tensor_tensor(
                    BT[:, 4 * b:4 * b + 4, :], AT[:, 4 * b:4 * b + 4, :],
                    mask.unsqueeze(1).broadcast_to([P, 4, P]), ALU.mult), at_r[b], *bt_free) for b in range(4)]
                yield
                px = []
                for b in range(4):
                    n, bank, free = side_banks.take()
                    b4 = bank.rearrange("p (u t) -> p u t", u=4)
                    PE.wait(*free, bts[b], x_r[b])
                    for u in range(4):
                        t = mm(b4[:, u, :], BT[:, 4 * b + u, :], X[:, 4 * b + u, :], signal=(u == 3))
                    if b % 2:
                        t = act(lambda e, b=b, b4=b4: e.activation(PX[:, 4 * b:4 * b + 4, :], b4, ACT.Copy), t,
                                *bt_free, kk_last)
                    else:
                        t = vec(lambda e, b=b, b4=b4: e.tensor_copy(PX[:, 4 * b:4 * b + 4, :], b4), t,
                                *bt_free, kk_last)
                    side_banks.free(n, t)
                    px.append(t)
                yield
                new_x, new_xt = [], []
                tpes = []
                for b in range(4):
                    us = slice(4 * b, 4 * b + 4)
                    if not last_level:
                        n, bank, free = side_banks.take()
                        b4 = bank.rearrange("p (u t) -> p u t", u=4)
                        PE.wait(*free, px[b], xT_r[b])
                        for u in range(4):
                            t1 = mm(b4[:, u, :], XT[:, 4 * b + u, :], PX[:, 4 * b + u, :], signal=(u == 3))
                    n2, bank2, free2 = side_banks.take()
                    c4 = bank2.rearrange("p (u t) -> p u t", u=4)
                    PE.wait(*free2, px[b], xT_r[b])
                    for u in range(4):
                        t2 = mm(c4[:, u, :], PX[:, 4 * b + u, :], XT[:, 4 * b + u, :], signal=(u == 3))
                    if not last_level:
                        t = vec(lambda e, us=us, b4=b4: e.tensor_tensor(X[:, us, :], X[:, us, :], b4, ALU.subtract),
                                t1)
                        side_banks.free(n, t)
                        new_x.append(t)
                    t = vec(lambda e, us=us, c4=c4: e.tensor_tensor(XT[:, us, :], XT[:, us, :], c4, ALU.subtract), t2)
                    side_banks.free(n2, t)
                    new_xt.append(t)
                    tpes.append(t2)
                x_r, xT_r = new_x, new_xt
                bt_free = [tpes[-1]]
                yield
            u0_r, nw_r, s1_r, u1_r, o_r = [], [], [], [], []

            def four(b, dst, pairs, res, *after, neg=False, dfree=()):
                n, bank, free = side_banks.take()
                b4 = bank.rearrange("p (u t) -> p u t", u=4)
                PE.wait(*free, *after)
                for u in range(4):
                    ps = pairs(4 * b + u)
                    for m, (l, r) in enumerate(ps):
                        t = mm(b4[:, u, :], l, r, m == 0, m == len(ps) - 1,
                               signal=(u == 3 and m == len(ps) - 1))
                if neg or b % 2:
                    t = act(lambda e: e.activation(dst, b4, ACT.Copy, scale=-1.0 if neg else 1.0), t, *dfree)
                else:
                    t = vec(lambda e: e.tensor_copy(dst, b4), t, *dfree)
                side_banks.free(n, t)
                res.append(t)
            hs = [slice(0, 4), slice(4, 8)]
            for b in range(2):
                four(b, U0[:, hs[b], :], lambda q_: [(XT[:, 2 * q_, :], tok_v[:, 2 * q_, :])], u0_r, *xT_r, t_v,
                     dfree=[kk_last, an_r[-1]])
                four(b, nwT[:, hs[b], :], lambda q_: [(tok_kbe[:, q_, :], XT[:, 2 * q_ + 1, :])], nw_r, t_kbe,
                     neg=True, dfree=bts)
            yield
            for b in range(2):
                four(b, S1[:, hs[b], :], lambda q_: [(tok_kdec[:, q_, :], U0[:, q_, :])], s1_r, *u0_r, dfree=bts)
            yield
            for b in range(2):
                four(b, U1[:, hs[b], :], lambda q_: [(XT[:, 2 * q_ + 1, :], tok_v[:, 2 * q_ + 1, :]),
                                                     (nwT[:, q_, :], S1[:, q_, :])], u1_r, *s1_r, *nw_r)
            o4 = o_tok.rearrange("p (h t) d -> p h t d", t=2)
            for b in range(2):
                four(b, o4[:, hs[b], 0, :], lambda q_: [(attnT[:, 2 * q_, :], U0[:, q_, :])], o_r, *u0_r,
                     dfree=bt_free)
            yield
            for b in range(2):
                four(b, o4[:, hs[b], 1, :], lambda q_: [(qdecT[:, q_, :], S1[:, q_, :]),
                                                        (attnT[:, 2 * q_ + 1, :], U1[:, q_, :])], o_r, *u1_r)
            gdn_out["solve_done"] = o_r[-1]
            yield
            t = pool(lambda e: e.tensor_tensor(X, o_tok, o_tok, ALU.mult), *o_r, *u0_r)
            yield
            yield
            t = vec(lambda e: e.tensor_reduce(st[:, 0:16], X, AX.X, ALU.add), t)
            t_ro = rsqrt(st[:, 0:16], 16, t, scale=1.0 / DH)
            yield
            t = vec(lambda e: e.tensor_tensor(o_tok, o_tok, per_unit(st[:, 0:16]), ALU.mult), t_ro)
            t = pool(lambda e: e.tensor_tensor(
                o_tok.rearrange("p (h t) d -> p t h d", t=2), o_tok.rearrange("p (h t) d -> p t h d", t=2),
                gz.rearrange("p t (h d) -> p t h d", h=HEADS), ALU.mult), t, *gz_r)
            gdn_out["gz_done"] = t
            yield
            yield
            yg = []
            for b in range(4):
                n, bank, free = side_banks.take()
                b4 = bank.rearrange("p (u t) -> p u t", u=4)
                for u in range(4):
                    tt_ = tr(b4[:, u, :], o_tok[:, 4 * b + u, :], *free, t, signal=(u == 3))
                hi = ygh[:, 2 * b:2 * b + 2, :].rearrange("p h (t q) -> p (h t) q", t=2)
                lo = ygl[:, 2 * b:2 * b + 2, :].rearrange("p h (t q) -> p (h t) q", t=2)
                t1 = act(lambda e, hi=hi, b4=b4: e.activation(hi, b4, ACT.Copy, scale=PR("gdn_norm")), tt_, t_prm,
                         t_ro)
                t2 = vec(lambda e, hi=hi, lo=lo, b4=b4: e.scalar_tensor_tensor(
                    lo, b4, PR("gdn_norm"), hi.bitcast(F32), ALU.mult, ALU.subtract), t1)
                side_banks.free(n, t2)
                yg.append(t2)
            gdn_out["y"] = yg
            yield

        def turn(src, dst, ready_, dfree=()):
            res = []
            for b in range(4):
                n, bank, free = side_banks.take()
                b4 = bank.rearrange("p (u t) -> p u t", u=4)
                PE.wait(*free, *ready_)
                for u in range(4):
                    t = tr(b4[:, u, :], src[:, 4 * b + u, :], signal=(u == 3))
                if b % 2:
                    t = act(lambda e, b=b, b4=b4: e.activation(dst[:, 4 * b:4 * b + 4, :], b4, ACT.Copy), t, *dfree)
                else:
                    t = vec(lambda e, b=b, b4=b4: e.tensor_copy(dst[:, 4 * b:4 * b + 4, :], b4), t, *dfree)
                side_banks.free(n, t)
                res.append(t)
            return res

        side.append(gdn())

        gz_r = []
        for j in range(4):
            n, bank, t = projected(False)
            b3 = bank.rearrange("p (t c) -> p t c", t=2)
            dst = gz[:, :, j * PW:(j + 1) * PW]
            t = act(lambda e, dst=dst, b3=b3: e.activation(dst, b3, ACT.Tanh, scale=0.5), t)
            t = vec(lambda e, dst=dst, b3=b3: e.scalar_tensor_tensor(dst, dst, 1.0, b3, ALU.add, ALU.mult), t)
            few_banks.free(n, t)
            gz_r.append(t)
        fox_r = {}
        for name, dst, scale in (("q", qfT, float(DH) ** -0.5), ("k", kfT, 1.0)):
            for j in range(4):
                n, bank, t = projected(True)
                b3 = bank.rearrange("p (c t) -> p c t", c=2)
                t = act(lambda e, dst=dst, b3=b3, j=j, s_=scale: e.activation(dst[:, 2 * j:2 * j + 2, :], b3, ACT.Copy,
                                                                            scale=s_), t)
                few_banks.free(n, t)
                fox_r[name, j] = t
        for j in range(4):
            n, bank, t = projected(False)
            b3 = bank.rearrange("p (t c) -> p t c", t=2)
            t = act(lambda e, b3=b3, j=j: e.activation(vf[:, :, j * PW:(j + 1) * PW], b3, ACT.Copy), t)
            few_banks.free(n, t)
            fox_r["v", j] = t

        yf = []

        def fox_head(hh):
            fst = st[:, 128 + 4 * hh:132 + 4 * hh]
            nm, sums = fst[:, 0:2], fst[:, 2:4]
            parts = [slice(0, P), slice(P, 3 * P)]
            n, bank, free = fox_banks.take()
            PE.wait(*free, fox_r["q", hh // 2], fox_r["k", hh // 2], G["t_nc"])
            e_h = ident[0:8, hh:hh + 1].broadcast_to([8, P])
            mm(bank[:, 0:P], qfT[:, hh, 0:P], kfT[:, hh, 0:P], True, False, signal=False)
            mm(bank[:, 0:P], e_h, row_nc[:, 0:P], False, True, signal=False)
            mm(bank[:, P:3 * P], qfT[:, hh, P:T], kfT[:, hh, :], True, False, signal=False)
            t_s = mm(bank[:, P:3 * P], e_h, row_nc, False, True)
            yield
            npb, pb, pfree = fox_p.take()
            tx = []
            for m, s in enumerate(parts):
                tx.append(vec(lambda e: e.scalar_tensor_tensor(
                    pb[:, s], bank[:, s], c_u[:, 2 * hh + m:2 * hh + m + 1], C("causal")[:, s], ALU.add, ALU.add),
                    t_s, *pfree))
            fox_banks.free(n, tx[1])
            for m, s in enumerate(parts):
                t = vec(lambda e: e.tensor_reduce(nm[:, m:m + 1], pb[:, s], AX.X, ALU.max, negate=True), tx[m])
                tx[m] = act(lambda e: e.activation(pb[:, s], pb[:, s], ACT.Exp, bias=nm[:, m:m + 1],
                                                   accum_out=sums[:, m:m + 1]), t)
            yield
            t = vec(lambda e: e.reciprocal(sums, sums), *tx)
            for m, s in enumerate(parts):
                t_p = vec(lambda e: e.tensor_scalar(pb[:, s], pb[:, s], sums[:, m:m + 1], None, ALU.mult), t)
            yield
            n, bank2, free = fox_banks.take()
            for u in range(3):
                t = tr(bank2[:, u * P:(u + 1) * P], pb[:, u * P:(u + 1) * P], *free, t_p, signal=(u == 2))
            fox_p.free(npb, t)
            nT, pT, tfree = fox_pT.take()
            t = act(lambda e: e.activation(pT, bank2[:, 0:3 * P], ACT.Copy), t, *tfree)
            fox_banks.free(n, t)
            yield
            n, bank3, free = fox_banks.take()
            PE.wait(*free, t, *[fox_r["v", j] for j in range(4)])
            vs = slice(hh * DH, (hh + 1) * DH)
            mm(bank3[:, 0:P], vf[:, 0, vs], pT[:, 0:P], True, True, signal=False)
            mm(bank3[:, P:T], vf[:, 0, vs], pT[:, P:2 * P], True, False, signal=False)
            t = mm(bank3[:, P:T], vf[:, 1, vs], pT[:, 2 * P:3 * P], False, True)
            fox_pT.free(nT, t)
            t = split_from(bank3[:, 0:T], yfh[:, hh, :], yfl[:, hh, :], t, t_s)
            fox_banks.free(n, t)
            yf.append(t)

        def in_steps(heads):
            heads, running = list(heads), []
            while heads or running:
                for g in list(running):
                    try:
                        next(g)
                    except StopIteration:
                        running.remove(g)
                if heads:
                    running.append(heads.pop(0))
                    next(running[-1])
                yield

        side.append(in_steps(fox_head(hh) for hh in range(HEADS)))
        gate_r = {}
        for name, dst in (("f", gate_f), ("g", gate_g)):
            if name == "g":
                while "solve_done" not in gdn_out:
                    step_side()
            dfree = [gdn_out["solve_done"]] if name == "g" else []
            for j in range(4):
                n, bank, t = projected(True)
                b3 = bank.rearrange("p (c t) -> p c t", c=2)
                d = dst[:, 2 * j:2 * j + 2, :]
                t = act(lambda e: e.activation(d, b3, ACT.Tanh, scale=0.5), t, *dfree)
                few_banks.free(n, t)
                gate_r[name, j] = pool(lambda e: e.tensor_scalar(d, d, 0.5, 0.5, ALU.mult, ALU.add), t)
                x_done = t
        while side:
            step_side()
        bank_pool[0] = gemm_banks

        yt_tmp = Slots([(at(f"mix_a{i}", [P, 2, T], 10, skip=4096 * i), at(f"mix_b{i}", [P, 2, T], 10,
                                                                           skip=4096 * i + 2048)) for i in range(2)])
        y_r = []
        unit10_free = [yf[-1]]
        for j in range(4):
            n1, b1, f1 = gemm_banks.take()
            t1 = gemm(b1, f1, yfh, yfl, yf[1::2], True)
            n2, b2, f2 = gemm_banks.take()
            t2 = gemm(b2, f2, ygh, ygl, gdn_out["y"], True)
            nt, (ma, mb), tfree = yt_tmp.take()
            fs = slice(2 * j, 2 * j + 2)
            r3 = lambda b_: b_.rearrange("p (c t) -> p c t", c=2)
            t1 = vec(lambda e, ma=ma, b1=b1, fs=fs: e.tensor_tensor(ma, r3(b1), gate_f[:, fs, :], ALU.mult), t1,
                     gate_r["f", j], *tfree, *unit10_free)
            t2 = vec(lambda e, mb=mb, b2=b2, fs=fs: e.tensor_tensor(mb, r3(b2), gate_g[:, fs, :], ALU.mult), t2,
                     gate_r["g", j])
            gemm_banks.free(n1, t1)
            gemm_banks.free(n2, t2)
            t = pool(lambda e, ma=ma, mb=mb: e.tensor_tensor(ma, ma, mb, ALU.add), t1, t2)
            t = split_from(ma, xhi[:, fs, :], xlo[:, fs, :], t, x_done)
            yt_tmp.free(nt, t)
            y_r.append(t)
        h_in = load("x_again", h, a["x"][0].rearrange("(t p) d -> p t d", p=P), gdn_out["gz_done"])

        def add_to_h(n, bank, t, j, *after, dst=None):
            hs_ = h[:, :, j * PW:(j + 1) * PW]
            t = vec(lambda e: e.tensor_tensor(hs_, bank.rearrange("p (t c) -> p t c", t=2), hs_, ALU.add), t, *after)
            gemm_banks.free(n, t)
            return t
        norm = Norm()

        def norm_feed(norm, t, *after):
            j = len(norm.fed)
            norm.fed.append(t)
            norm.squares(j, t, *after)

        for j in range(4):
            n, bank, free = gemm_banks.take()
            t = gemm(bank, free, xhi, xlo, y_r, False)
            if j:
                norm.transposes(norm.fed[j - 1])
            pe_x_done = t
            norm_feed(norm, add_to_h(n, bank, t, j, h_in), y_r[-1])
        norm.transposes(norm.fed[3])
        x_ready = norm.finish(PR("norm_ffn"), pe_x_done)

        late = [gdn_out["y"][-1], yf[-1], y_r[-1], pe_x_done]
        box = [sem("rpb_landed"), 0]
        for rq in range(GRID_ROWS):
            dst = bias2[GRID * (rq % 2):GRID * (rq % 2) + GRID, :, rq // 2, :]
            src = a["rpb_skew"][:, :, (3 - rq) * GRID:(3 - rq) * GRID + T]
            t_rpb = SP.dma(box, dst, src, *late)
        band_in = load("band", band, a["bands"], *late)
        wpool_in = load("wpool", wpool, a["w_pool_2"][0].rearrange("g c d -> c g d"), *late)
        gf_src = a["norm_final"]
        t_b = []

        def mask_bias():
            for half in range(2):
                part = bias2[GRID * half:GRID * half + GRID].rearrange("p h t (r c) -> p (h t r) c", c=GRID)
                hi_part, lo_part = part[:, :, 0:GRID - WIN_COLS], part[:, :, WIN_COLS:GRID]
                t = pool(lambda e: e.affine_select(hi_part, hi_part, [[0, 64], [1, GRID - WIN_COLS]], ALU.is_ge, NEG,
                                                   WIN_COLS // 2, -1), t_rpb)
                yield
                t = pool(lambda e: e.affine_select(lo_part, lo_part, [[0, 64], [-1, GRID - WIN_COLS]], ALU.is_ge,
                                                   NEG, WIN_COLS // 2 - 1 - WIN_COLS, 1), t)
                t_b[:] = [t]
                yield

        def ffn_down(a_r, norm, *after):
            bks = [gemm_banks.take() for _ in range(4)]
            res = []
            for k in range(0, KF, 8):
                for j in range(4):
                    n, bank, free = bks[j]
                    last = k + 8 >= KF
                    t = gemm(bank, free if k == 0 else (), acth, actl, a_r, False, k, k == 0, last)
                    if last:
                        if norm and j:
                            norm.transposes(norm.fed[j - 1])
                        res.append(add_to_h(n, bank, t, j, *after))
                        if norm:
                            norm_feed(norm, res[-1], a_r[KF // 2 - 1], *after)
                        else:
                            write_out(j, res[-1])
            if norm:
                norm.transposes(norm.fed[3])
            return res, t

        ft = Slots([(at(f"ff_gate{i}", [P, 2, T], 10, skip=4096 * i), at(f"ff_val{i}", [P, 2, T], 10,
                                                                         skip=4096 * i + 2048)) for i in range(2)])
        ft2 = Slots([at(f"ff_tanh{i}", [P, 2, T], 16.5, skip=2048 * i) for i in range(2)])
        a_r = {}

        def ffn1_tail(j, nt, bufs, t_c, h_free):
            g_, v_ = bufs
            n2, th, hfree = ft2.take()
            t = act(lambda e: e.activation(th, g_, ACT.Tanh), t_c[0], *hfree, *h_free)
            yield
            t = vec(lambda e: e.scalar_tensor_tensor(th, th, 1.0, g_, ALU.add, ALU.mult), t)
            t = pool(lambda e: e.tensor_tensor(th, th, v_, ALU.mult), t, t_c[1])
            ft.free(nt, t)
            yield
            t = split_from(th, acth[:, 2 * j:2 * j + 2, :], actl[:, 2 * j:2 * j + 2, :], t, *late)
            ft2.free(n2, t)
            a_r[j] = t

        norm_tr_done = x_ready
        for j in range(KF // 2):
            nt, bufs, tfree = ft.take()
            t_c = []
            if j == 2:
                side.append(mask_bias())
            for side_ in range(2):
                n, bank, t = projected(True)
                b3 = bank.rearrange("p (c t) -> p c t", c=2)
                acc = bufs[side_]
                base = PARAMS["fconv"][0]
                prev = [None, None]
                for c in range(2):
                    w = base + (side_ * KF + 2 * j + c) * 3
                    t2 = act(lambda e, c=c, w=w, acc=acc, b3=b3: e.activation(
                        acc[:, c, :], b3[:, c, :], ACT.Copy, scale=prm[:, w + 2:w + 3]), t, t_prm, *tfree,
                        *norm_tr_done)
                for back in (1, 2):
                    for c in range(2):
                        w = base + (side_ * KF + 2 * j + c) * 3 + 2 - back
                        prev[c] = vec(lambda e, c=c, w=w, back=back, acc=acc, b3=b3: e.scalar_tensor_tensor(
                            acc[:, c, back:], b3[:, c, 0:T - back], prm[:, w:w + 1], acc[:, c, back:],
                            ALU.mult, ALU.add), t2, prev[c])
                gemm_banks.free(n, prev[1])
                t_c.append(prev[1])
            side.append(ffn1_tail(j, nt, bufs, t_c, norm_tr_done))
            if j == KF // 2 - 1:
                while len(a_r) < KF // 2 - 1:
                    step_side()
        gain_in = load("gain_final", gain_final, bass.AP(tensor=a["norm_final"].tensor, offset=a["norm_final"].offset,
                                                         ap=[[0, P], [1, D]]), *late)
        norm = Norm(gain_final)
        h_r, pe_down = ffn_down(a_r, norm, gain_in)
        x_ready = norm.finish(PR("norm1"), pe_down)
        r_h, t_rh = norm.h2_scale
        h2_r = []
        for m in range(TT):
            t = act(lambda e: e.activation(h[:, m, :], h[:, m, :], ACT.Copy, scale=r_h[:, m:m + 1]), t_rh,
                    *[b[2] for b in norm.banks], *norm.sums)
            h2_r.append(pool(lambda e: e.tensor_tensor(h[:, m, :], h[:, m, :], gain_final, ALU.mult), t, gain_in))

        tok2, t3 = {}, {}

        def qk_norm(src, dstT, ssq, sq2, gain, ready_):
            s4 = src.rearrange("p t (h d) -> p (t h) d", d=NA_DIM)
            t = pool(lambda e: e.tensor_tensor(sq2, src, src, ALU.mult), *ready_, *x_ready)
            yield
            yield
            t = vec(lambda e: e.tensor_reduce(ssq, sq2.rearrange("p t (h d) -> p (t h) d", d=NA_DIM), AX.X, ALU.add),
                    t)
            t_sq[gain] = t
            t = rsqrt(ssq, 16, t, scale=1.0 / NA_DIM)
            yield
            t = vec(lambda e: e.tensor_tensor(s4, s4, ssq.unsqueeze(2).broadcast_to([P, 16, NA_DIM]), ALU.mult), t)
            yield
            for b in range(2):
                n, bank, free = side_banks.take()
                b3 = bank.rearrange("p (f t) -> p f t", f=2)
                for f in range(2):
                    for m in range(TT):
                        t2 = tr(b3[:, f, m * P:(m + 1) * P], src[:, m, (2 * b + f) * P:(2 * b + f + 1) * P], *free, t,
                                signal=(f == 1 and m == 1))
                t3[gain] = act(lambda e: e.activation(dstT[:, 2 * b:2 * b + 2, :], b3, ACT.Copy, scale=PR(gain)), t2,
                               *late, *h2_r)
                side_banks.free(n, t3[gain])
            yield

        def pooled(g):
            n, bank, free = side_banks.take()
            for m in range(TT):
                t = mm(bank[:, 0:T], u2[:, m, g * P:(g + 1) * P], band[:, g, m, :], m == 0, m == 1, *free,
                       tok2["u", g // 2], band_in)
            t = vec(lambda e: e.tensor_copy(poolT[:, g, :], bank[:, 0:T]), t)
            side_banks.free(n, t)
            yield
            n, bank2, free = side_banks.take()
            t = mm(bank2[:, 0:T], wpool[:, g, :], poolT[:, g, :], True, True, *free, t, wpool_in)
            while "x_done" not in tok2:
                yield
            sc_ = PR("pool_scale")[:, g:g + 1]
            t1 = act(lambda e: e.activation(xhi[:, 4 + g, :], bank2[:, 0:T], ACT.Copy, scale=sc_), t, tok2["x_done"])
            t2 = vec(lambda e: e.scalar_tensor_tensor(xlo[:, 4 + g, :], bank2[:, 0:T], sc_,
                                                      xhi[:, 4 + g, :].bitcast(F32), ALU.mult, ALU.subtract), t1)
            side_banks.free(n, t2)
            mix_r[4 + g] = t2

        na_p = Slots([at(f"na_p{i}", [P, TT, T], 10, skip=2048 * i) for i in range(2)])
        na_pT = Slots([at(f"na_pT{i}", [P, TT, T], 10, skip=4096 + 2048 * i) for i in range(2)])
        nst = st[:, 48:48 + 32].rearrange("p (h c) -> p h c", c=4)
        ybank, mix_r, t_sq = {}, {}, {}

        def na_head(hh):
            p0 = NA_DIM * (hh % 2)
            n, bank, free = side_banks.take()
            b3 = bank.rearrange("p (t k) -> p t k", t=2)
            for m in range(TT):
                t = mm(b3[:, m, :], q2T[p0:p0 + NA_DIM, hh // 2, m * P:(m + 1) * P],
                       k2T[p0:p0 + NA_DIM, hh // 2, :], True, True, *free, t3["qg"], t3["kg"], signal=(m == 1))
            npb, pb, pfree = na_p.take()
            t = vec(lambda e: e.scalar_tensor_tensor(pb, b3, float(NA_DIM) ** -0.5, bias2[:, hh], ALU.mult, ALU.add),
                    t, *t_b, t_sq["qg"], t_sq["kg"], *pfree)
            side_banks.free(n, t)
            nm, sums = nst[:, hh, 0:2], nst[:, hh, 2:4]
            t = vec(lambda e: e.tensor_reduce(nm, pb, AX.X, ALU.max, negate=True), t)
            tx = [act(lambda e: e.activation(pb[:, m, :], pb[:, m, :], ACT.Exp, bias=nm[:, m:m + 1],
                                             accum_out=sums[:, m:m + 1]), t) for m in range(TT)]
            yield
            t = vec(lambda e: e.reciprocal(sums, sums), *tx)
            for m in range(TT):
                t_p = vec(lambda e: e.tensor_scalar(pb[:, m, :], pb[:, m, :], sums[:, m:m + 1], None, ALU.mult), t)
            n, bank2, free = side_banks.take()
            c3 = bank2.rearrange("p (k t) -> p k t", k=2)
            for k in range(2):
                for m in range(TT):
                    t2 = tr(c3[:, k, m * P:(m + 1) * P], pb[:, m, k * P:(k + 1) * P], *free, t_p,
                            signal=(k == 1 and m == 1))
            na_p.free(npb, t2)
            nT, pT, tfree = na_pT.take()
            t = act(lambda e: e.activation(pT, c3, ACT.Copy), t2, *tfree)
            side_banks.free(n, t)
            yield
            if hh % 2 == 0:
                ybank[0] = side_banks.take()
            n, bank3, free = ybank[0]
            for k in range(2):
                t = mm(bank3[p0:p0 + NA_DIM, 0:T], v2[:, k, hh * NA_DIM:(hh + 1) * NA_DIM], pT[:, k, :],
                       k == 0, k == 1, *free, t, tok2["v", 0], tok2["v", 1])
            na_pT.free(nT, t)
            if hh % 2:
                t = split_from(bank3[:, 0:T], xhi[:, hh // 2, :], xlo[:, hh // 2, :], t, tok2["x_done"])
                side_banks.free(n, t)
                mix_r[hh // 2] = t

        sq2 = [at(f"sq2_{i}", [P, TT, NA_W], 10, skip=4096 * i) for i in range(2)]
        for name, dst in (("q", q2), ("k", k2), ("u", u2), ("v", v2)):
            for j in range(2):
                n, bank, t = projected(False)
                b3 = bank.rearrange("p (t c) -> p t c", t=2)
                t = act(lambda e: e.activation(dst[:, :, j * PW:(j + 1) * PW], b3, ACT.Copy), t, *late)
                gemm_banks.free(n, t)
                tok2[name, j] = t
                if j and name == "q":
                    side.append(qk_norm(q2, q2T, st[:, 16:32], sq2[0], "qg", [tok2["q", 0], t]))
                if j and name == "k":
                    side.append(qk_norm(k2, k2T, st[:, 32:48], sq2[1], "kg", [tok2["k", 0], t]))
                if j and name == "u":
                    side.append(in_steps(pooled(g) for g in range(4)))
        tok2["x_done"] = t
        while len(t3) < 2:
            step_side()
        while side:
            step_side()
        side.append(in_steps(na_head(hh) for hh in range(HEADS)))
        bks = [gemm_banks.take() for _ in range(4)]
        for j in range(4):
            n, bank, free = bks[j]
            gemm(bank, free, xhi, xlo, {2: mix_r[5], 3: mix_r[7]}, False, 4, True, False)
        while side:
            step_side()
        norm = Norm()
        for j in range(4):
            n, bank, free = bks[j]
            t = gemm(bank, (), xhi, xlo, {0: mix_r[1], 1: mix_r[3]}, False, 0, False, True)
            if j:
                norm.transposes(norm.fed[j - 1])
            norm_feed(norm, add_to_h(n, bank, t, j, *h2_r), mix_r[3])
        pe_x_done = t
        norm.transposes(norm.fed[3])

        x_ready = norm.finish(PR("norm2"), pe_x_done)
        a_r = {}
        ft = Slots([(at(f"f2_a{i}", [P, 2, T], 10, skip=4096 * i), at(f"f2_b{i}", [P, 2, T], 10,
                                                                      skip=4096 * i + 2048)) for i in range(2)])
        for j in range(KF // 2):
            nt, (ga, va), tfree = ft.take()
            n, bank, t = projected(True)
            b3 = bank.rearrange("p (c t) -> p c t", c=2)
            t = act(lambda e, ga=ga, b3=b3: e.activation(ga, b3, ACT.Tanh, scale=0.5), t, *tfree, *x_ready)
            t_g = vec(lambda e: e.scalar_tensor_tensor(ga, ga, 1.0, b3, ALU.add, ALU.mult), t)
            gemm_banks.free(n, t_g)
            n, bank, t = projected(True)
            b3 = bank.rearrange("p (c t) -> p c t", c=2)
            t = vec(lambda e: e.scalar_tensor_tensor(va, b3, 0.5, ga, ALU.mult, ALU.mult), t, t_g, *tfree)
            gemm_banks.free(n, t)
            t = split_from(va, acth[:, 2 * j:2 * j + 2, :], actl[:, 2 * j:2 * j + 2, :], t, pe_down)
            ft.free(nt, t)
            a_r[j] = t
        outbox = [sem("output_written"), 0]
        t_out = None

        def write_out(j, t):
            cols = slice(j * PW, (j + 1) * PW)
            SP.dma(outbox, out[0].rearrange("(t p) d -> p t d", p=P)[:, :, cols], h[:, :, cols], t)

        ffn_down(a_r, None)
        t_out = (outbox[0], outbox[1])
        SP.wait(t_out)


def _constants():
    c = np.zeros((P, N_CONSTS), np.float32)
    i, j = np.indices((P, P))
    c[:, slice(*CONSTS["ident"])] = np.eye(P)
    c[:, slice(*CONSTS["upper"])] = i <= j
    c[:, slice(*CONSTS["ones"])] = 1
    causal = np.where(j <= i, 0, NEG)
    c[:, slice(*CONSTS["causal"])] = np.concatenate([causal, 0 * causal, causal], 1)
    c[:, slice(*CONSTS["decay_mask"])] = np.where(i <= j, 0, NEG)
    for n, side in enumerate((16, 32, 64)):
        lo = CONSTS["level"][0] + n * P
        c[:, lo:lo + P] = (i // (2 * side) == j // (2 * side)) & (i % (2 * side) < side) & (j % (2 * side) >= side)
    return c


def _bands():
    t = np.arange(T)
    b = np.zeros((4, T, T), np.float32)
    for g, w in enumerate(POOL_WINDOWS):
        lo, hi = np.clip(t - w // 2, 0, T), np.clip(t + w // 2, 0, T)
        inside = (t[:, None] >= lo[None]) & (t[:, None] < hi[None])
        b[g] = inside / (hi - lo)[None].astype(np.float32) - np.eye(T)
    return np.ascontiguousarray(b.reshape(4, TT, P, T).transpose(2, 0, 1, 3))


_BIG = ["x", "w_in", "w_branch_fox", "w_branch_gdn", "w_out", "w_up", "w_down", "norm_final", "w_in_2",
        "w_pool_2", "w_out_2", "w_gate_2", "w_up_2", "w_down_2"]


def kernel(**inputs):
    import concourse.bacc as bacc
    from concourse.bass_utils import run_bass_kernel_spmd

    def g(name):
        return np.asarray(inputs[name])

    def tiles(v):
        return v.reshape(-1, P).T

    params = np.empty((P, N_PARAMS), np.float32)
    for name, v in (("norm_mix", tiles(g("norm_mix")[0])), ("norm_ffn", tiles(g("norm_ffn")[0])),
                    ("norm1", tiles(g("norm1_g_2")[0])), ("norm2", tiles(g("norm2_g_2")[0])), ("norm_final", tiles(g("norm_final"))),
                    ("gconv", g("gdn_conv_w")[0].reshape(4, 24, P).transpose(2, 1, 0).reshape(P, 96)),
                    ("fconv", g("ffn_conv_w")[0].reshape(3, 2 * KF, P).transpose(2, 1, 0).reshape(P, 2 * KF * 3)),
                    ("gdn_norm", g("gdn_norm").T), ("pool_scale", tiles(g("pool_scale_2")[0])),
                    ("qg", np.tile(g("q_norm_g_2")[0], 2)[:, None]), ("kg", np.tile(g("k_norm_g_2")[0], 2)[:, None]),
                    ("gate_bias", np.concatenate([g("fox_f_bias"), g("gdn_dt_bias")], 1)),
                    ("a_log", g("gdn_a_log"))):
        params[:, slice(*PARAMS[name])] = v
    nc = bacc.Bacc("TRN2", target_bir_lowering=False, num_devices=1)
    arrays, args = {}, {}
    feed = {n: np.ascontiguousarray(g(n)) for n in _BIG}
    col = np.arange(GRID)
    rel = np.clip(col[None] - col[:, None] + WIN_COLS - 1, 0, RPB_COLS - 1)
    skew = g("rpb_2")[0][:, 4:11][:, :, rel].transpose(2, 0, 1, 3).reshape(GRID, HEADS, 7 * GRID)
    feed.update(rpb_skew=np.ascontiguousarray(skew), params=params, constants=_constants(), bands=_bands())
    for name, v in feed.items():
        arrays[f"in_{name}"] = v
        args[name] = nc.dram_tensor(f"in_{name}", v.shape, F32, kind="ExternalInput").ap()
    out = nc.dram_tensor("out", (1, T, D), F32, kind="ExternalOutput").ap()
    sa = nc.dram_tensor("blocks_to_invert", (NBLK, UNITS, BLOCK, BLOCK), F32).ap()
    sx = nc.dram_tensor("blocks_inverted", (NBLK, UNITS, BLOCK, BLOCK), F32).ap()
    build(nc, args, out, sa, sx)
    r = run_bass_kernel_spmd(nc, [arrays], core_ids=[0])
    return r.results[0]["out"]
```

```python
from contextlib import ExitStack

import numpy as np

import concourse.bass as bass
from concourse import mybir

F32 = mybir.dt.float32
F32R = mybir.dt.float32r
ALU = mybir.AluOpType
ACT = mybir.ActivationFunctionType
AX = mybir.AxisListType

P = 128
T = 256
TT = T // P
D = 1024
KD = D // P
HEADS = 8
DH = 128
UNITS = HEADS * TT
FF = 2816
KF = FF // P
PW = 256
HALF = 4
WARM_UP = 3
AHEAD = 3
EPS = 1e-6
NEG = -1e30
GRID = 64
GRID_ROWS = T // GRID
WIN_COLS = 16
RPB_ROWS, RPB_COLS = 15, 31
NA_DIM = 64
NA_W = HEADS * NA_DIM
POOL_WINDOWS = (2, 4, 8, 16)
POOL_REACH = max(POOL_WINDOWS) // 2
BLOCK = 16
NBLK = P // BLOCK

SIZES = (D, D, D, HEADS, D, D, D, HEADS, HEADS, D, D, D)
C_FQ, C_FK, C_FV, C_FF, C_GQ, C_GK, C_GV, C_GA, C_GB, C_GZ, C_GF, C_GG = (sum(SIZES[:i]) for i in range(12))
SMALL = 3 * HEADS

PARAMS = {}
_at = 0
for _name, _n in (("norm_mix", KD), ("norm_ffn", KD), ("norm1", KD), ("norm2", KD), ("norm_final", KD), ("gconv", 24 * 4),
                  ("fconv", 2 * KF * 3), ("gdn_norm", 1), ("pool_scale", 4), ("qg", 1), ("kg", 1),
                  ("gate_bias", 2 * HEADS), ("a_log", HEADS)):
    PARAMS[_name] = (_at, _at + _n)
    _at += _n
N_PARAMS = _at

CONSTS = {}
_at = 0
for _name, _n in (("ident", P), ("upper", P), ("ones", 4), ("causal", P), ("decay_mask", P),
                  ("level", 3 * P)):
    CONSTS[_name] = (_at, _at + _n)
    _at += _n
N_CONSTS = _at


class Queue:

    def __init__(self, engine, sem):
        self.engine, self.sem, self.count, self.seen = engine, sem, 0, {}

    def wait(self, *tokens):
        for token in tokens:
            if token is None:
                continue
            sem, value = token
            if self.seen.get(id(sem), 0) < value:
                self.seen[id(sem)] = value
                self.engine.wait_ge(sem, value)

    def run(self, make, *after, signal=True):
        self.wait(*after)
        if not signal:
            make(self.engine)
            return None
        self.count += 1
        make(self.engine).then_inc(self.sem, 1)
        return (self.sem, self.count)

    def dma(self, sem_box, out, in_, *after):
        self.wait(*after)
        sem_box[1] += 16
        self.engine.dma_start(out, in_).then_inc(sem_box[0], 16)
        return (sem_box[0], sem_box[1])


class Buffer:

    def __init__(self, ap):
        self.ap, self.readers, self.held = ap, [], False


class Slots:

    def __init__(self, buffers):
        self.buffers, self.at = [b if isinstance(b, Buffer) else Buffer(b) for b in buffers], 0

    def take(self):
        for _ in self.buffers:
            b = self.buffers[self.at % len(self.buffers)]
            self.at += 1
            if not b.held:
                b.held = True
                return b, b.ap, list(b.readers)
        raise AssertionError("every buffer is held")

    def free(self, b, *tokens):
        b.readers, b.held = list(tokens), False


def build(nc, a, out, scratch_a, scratch_x, scratch_c):
    ctx = ExitStack()
    with ctx:
        def sem(name):
            return ctx.enter_context(nc.semaphore(name))

        PE, DVE, SC, PL, SP = (Queue(e, sem(f"done_{n}")) for n, e in (
            ("pe", nc.tensor), ("dve", nc.vector), ("act", nc.scalar), ("pool", nc.gpsimd), ("sp", nc.sync)))

        BASE, UNIT = 16512, 8192

        def at(name, shape, unit, dt=F32, skip=0):
            return nc.alloc_sbuf_tensor_at(name, shape, dt, offset=BASE + int(unit * UNIT) + skip)[:]

        xhi = at("xhi", [P, KD, T], 1, F32R)
        xlo = at("xlo", [P, KD, T], 2, F32R)
        raw = Slots([at(f"panel_raw{i}", [P, KD, PW], 3 + i) for i in range(3)])
        split = Slots([(at(f"panel_hi{i}", [P, HALF, PW], 6 + i / 2, F32R),
                        at(f"panel_lo{i}", [P, HALF, PW], 8 + i / 2, F32R)) for i in range(4)])
        acc_t = Slots([at(f"conv_acc{i}", [P, 2, T], 17, skip=2048 * i) for i in range(4)])
        tmp_t = Slots([at(f"conv_tmp{i}", [P, 2, T], 10, skip=2048 * i) for i in range(4)])
        fox_p = Slots([at(f"fox_p{i}", [P, 3 * P], 10, skip=1536 * i) for i in range(3)])
        fox_pT = Slots([at(f"fox_pT{i}", [P, 3 * P], 10, skip=4608 + 1536 * i) for i in range(2)])
        tok_k = at("tok_k", [P, UNITS, DH], 11)
        tok_q = at("tok_q", [P, UNITS, DH], 12)
        tok_v = at("tok_v", [P, UNITS, DH], 13)
        tok_kb = at("tok_kb", [P, UNITS, DH], 14)
        tok_kbe = at("tok_kbe", [P, HEADS, DH], 15)
        tok_kdec = at("tok_kdec", [P, HEADS, DH], 15.5)
        tok_qdec = at("tok_qdec", [P, HEADS, DH], 16)
        qdecT = at("qdecT", [P, HEADS, P], 16.5)
        kT = at("kT", [P, UNITS, P], 17)
        qT = at("qT", [P, UNITS, P], 18)
        kbT = at("kbT", [P, UNITS, P], 19)
        decayT = at("decayT", [P, UNITS, P], 20)
        AT = at("AT", [P, UNITS, P], 11)
        attnT = at("attnT", [P, UNITS, P], 12)
        X = at("X", [P, UNITS, P], 17)
        XT = at("XT", [P, UNITS, P], 18)
        PX = at("PX", [P, UNITS, P], 19)
        BT = at("BT", [P, UNITS, P], 14)
        U0 = at("U0", [P, HEADS, DH], 20)
        U1 = at("U1", [P, HEADS, DH], 20.5)
        nwT = at("nwT", [P, HEADS, P], 11)
        S1 = at("S1", [P, HEADS, DH], 11.5)
        o_tok = at("o_tok", [P, UNITS, DH], 14)
        qfT = at("qfT", [P, HEADS, T], 21)
        kfT = at("kfT", [P, HEADS, T], 22)
        yfh = at("yf_hi", [P, HEADS, T], 21, F32R)
        yfl = at("yf_lo", [P, HEADS, T], 22, F32R)
        vf = at("vf", [P, TT, D], 23)
        gz = at("gz", [P, TT, D], 24)
        gate_f = at("gate_f", [P, KD, T], 0)
        gate_g = at("gate_g", [P, KD, T], 18)
        ygh = at("yg_hi", [P, HEADS, T], 17, F32R)
        ygl = at("yg_lo", [P, HEADS, T], 19, F32R)
        h = at("h", [P, TT, D], 24)
        yh, yl = at("y_hi", [P, KD, T], 12, F32R), at("y_lo", [P, KD, T], 13, F32R)
        acth = at("act_hi", [P, KF, T], 11, F32R)
        actl = at("act_lo", [P, KF, T], 13.75, F32R)
        q2 = at("q2", [P, TT, NA_W], 17)
        k2 = at("k2", [P, TT, NA_W], 17.5)
        v2 = at("v2", [P, TT, NA_W], 18)
        u2 = at("u2", [P, TT, NA_W], 18.5)
        q2T = at("q2T", [P, 4, T], 19)
        k2T = at("k2T", [P, 4, T], 19.5)
        bias2 = at("bias2", [P, HEADS, TT, T], 20)
        band = at("band", [P, 4, TT, T], 22)
        wpool = at("wpool", [P, 4, P], 23)
        poolT = at("poolT", [P, 4, T], 23.25)
        gain_final = at("gain_final", [P, D], 19.5)
        small_at = [BASE + 25 * UNIT]

        def small(name, shape, dt=F32, bytes_=4):
            n = bytes_
            for s in shape[1:]:
                n *= s
            t = nc.alloc_sbuf_tensor_at(name, shape, dt, offset=small_at[0])[:]
            small_at[0] += -(-n // 32) * 32
            return t

        norm_row = nc.alloc_sbuf_tensor_at("norm_row", [P, T], F32, offset=small_at[0])[:]
        key_bias = small("key_bias", [P, 3 * P])
        cst = small("constants", [P, N_CONSTS])
        prm = small("params", [P, N_PARAMS])
        st = small("stats", [P, 160])
        blkA = at("blocks_A", [P, BLOCK, BLOCK], 16)
        blkX = at("blocks_X", [P, BLOCK, BLOCK], 16, skip=1024)
        blkT = at("blocks_T", [P, BLOCK * BLOCK], 16, skip=2048)
        wsm = at("small_raw", [P, KD, SMALL], 15)
        wsmh = at("small_hi", [P, KD, SMALL], 15, F32R, skip=1024)
        wsml = at("small_lo", [P, KD, SMALL], 15, F32R, skip=2048)
        row_nc = at("minus_c_rows", [HEADS, T], 0, skip=1024)
        row_gc = at("gc_rows", [HEADS, T], 0)
        gts = at("gates", [P, 528], 0, skip=2048)

        def C(name):
            lo, hi = CONSTS[name]
            return cst[:, lo:hi]

        def PR(name):
            lo, hi = PARAMS[name]
            return prm[:, lo:hi]

        ident, upper, ones = C("ident"), C("upper"), C("ones")[:, 0:1].broadcast_to([P, P])
        banks = [ctx.enter_context(nc.psum_tensor(f"bank{i}", [P, 512], F32)) for i in range(8)]
        banks = [Buffer(b[:, :]) for b in banks]
        few_banks, fox_banks, gemm_banks = Slots(banks[:2]), Slots(banks[2:4]), Slots(banks[:4])
        side_banks = Slots(banks[4:])

        raw_sem = [[sem(f"panel_landed{i}"), 0] for i in range(3)]

        def load(name, out_, in_, *after, q=SP):
            return q.dma([sem(f"landed_{name}"), 0], out_, in_, *after)

        x_rows = a["x"][0].rearrange("(t p) d -> p t d", p=P)
        x_in = [load("x0", h[:, :, 0:PW], x_rows[:, :, 0:PW])]
        id_in = load("identity", cst[:, 0:P], a["constants"][:, 0:P])
        x_in += [load(f"x{j}", h[:, :, j * PW:(j + 1) * PW], x_rows[:, :, j * PW:(j + 1) * PW]) for j in range(1, 4)]
        p_in = load("params", prm, a["params"])
        w_in = a["w_in"][0]

        def w_rows(w, k0, kt, c0, n):
            return w[k0 * P:(k0 + kt) * P, c0:c0 + n].rearrange("(k p) c -> p k c", p=P)

        def small_loads():
            return [load("small_f", wsm[:, :, 0:HEADS], w_rows(w_in, 0, KD, C_FF, HEADS)),
                    load("small_ab", wsm[:, :, HEADS:SMALL], w_rows(w_in, 0, KD, C_GA, 2 * HEADS))]

        plan = []

        def k_halves(*panels):
            return [(w, k, HALF, c) for k in (0, HALF) for w, c in panels]

        conv_order = [(C_GK, 2), (C_GZ, 0), (C_GK, 3), (C_GQ, 0), (C_GZ, 1), (C_GQ, 1), (C_GQ, 2), (C_GZ, 2),
                      (C_GQ, 3), (C_GV, 0), (C_GZ, 3), (C_GV, 1), (C_GV, 2), (C_GV, 3)]
        plan += k_halves((w_in, C_GK), (w_in, C_GK + PW)) + [(w_in, 0, KD, c + j * PW) for c, j in conv_order]
        plan += [(w_in, 0, KD, c + j * PW) for j in range(4) for c in (C_FQ, C_FK, C_FV)]
        for w, c in ((w_in, C_GF), (a["w_branch_fox"][0], 0), (w_in, C_GG), (a["w_branch_gdn"][0], 0)):
            plan += [(w, 0, KD, c + j * PW) for j in range(4)]
        plan += [(a["w_out"][0], 0, KD, j * PW) for j in range(4)]
        plan += k_halves((a["w_up"][0], 0), (a["w_up"][0], FF))
        for j in range(1, KF // 2):
            plan += [(a["w_up"][0], 0, KD, j * PW), (a["w_up"][0], 0, KD, FF + j * PW)]
        plan += [(a["w_down"][0], k, min(8, KF - k), j * PW) for k in range(0, KF, 8) for j in range(4)]
        plan += k_halves((a["w_in_2"][0], 0), (a["w_in_2"][0], 2 * PW))
        plan += [(a["w_in_2"][0], 0, KD, j * PW) for j in (1, 3, 4, 6, 7, 5)]
        plan += [(a["w_out_2"][0], k, KD // 2, j * PW) for k in (4, 0) for j in range(4)]
        plan += k_halves((a["w_gate_2"][0], 0), (a["w_up_2"][0], 0))
        for j in range(1, KF // 2):
            plan += [(a["w_gate_2"][0], 0, KD, j * PW), (a["w_up_2"][0], 0, KD, j * PW)]
        plan += [(a["w_down_2"][0], k, min(8, KF - k), j * PW) for k in range(0, KF, 8) for j in range(4)]
        landed, ready = {}, {}

        def fetch(i):
            if i >= len(plan):
                return
            w, k0, kt, c0 = plan[i]
            n, buf, readers = raw.take()
            landed[i] = (n, buf, kt, SP.dma(raw_sem[i % 3], buf[:, 0:kt, :], w_rows(w, k0, kt, c0, PW), *readers))

        halves = [(i, k, min(HALF, kt - k)) for i, (_, _, kt, _) in enumerate(plan) for k in range(0, kt, HALF)]
        split_at = [0]

        def split_next():
            if split_at[0] >= len(halves):
                return
            i, k0, kt = halves[split_at[0]]
            n_raw, buf, panel_kt, tok = landed[i]
            n, (hi, lo), readers = split.take()
            src = buf[:, k0:k0 + kt, :]
            t_hi = SC.run(lambda e: e.activation(hi[:, 0:kt, :], src, ACT.Copy), tok, *readers)
            t_lo = DVE.run(lambda e: e.tensor_tensor(lo[:, 0:kt, :], src, hi[:, 0:kt, :].bitcast(F32),
                                                     ALU.subtract), tok, t_hi, *readers)
            ready[split_at[0]] = (n, hi, lo, t_hi, t_lo)
            split_at[0] += 1
            if k0 + kt == panel_kt:
                raw.free(n_raw, t_hi, t_lo)
                fetch(i + 3)

        half_no = [0]

        def gemm(bank, bank_free, xh, xl, x_ready, feature_major, k_base=0, first=True, last=True):
            panel = halves[half_no[0]][0]
            PE.wait(*bank_free)
            while half_no[0] < len(halves) and halves[half_no[0]][0] == panel:
                _, k0, kt = halves[half_no[0]]
                n, hi, lo, t_hi, t_lo = ready.pop(half_no[0])
                half_no[0] += 1
                split_next()
                PE.wait(t_hi, t_lo)
                end = k0 + kt == plan[panel][2]
                for j in range(2):
                    js = slice(j * P, (j + 1) * P)
                    o = bank[:, j * 256:(j + 1) * 256]
                    seq = [(xx, ww, k) for k in range(kt) for xx, ww in ((xh, hi), (xl, hi), (xh, lo))]
                    for m, (xx, ww, k) in enumerate(seq):
                        kx = k_base + k0 + k
                        PE.wait(x_ready[kx // 2])
                        l, r = (ww[:, k, js], xx[:, kx, :]) if feature_major else (xx[:, kx, js], ww[:, k, :])
                        done = mm(o, l, r, first and k0 == 0 and j == 0 and m == 0,
                                  last and end and m == len(seq) - 1, signal=(j == 1 and m == len(seq) - 1))
                split.free(n, done)
                step_side()
            return done

        def mm(o, l, r, start=True, stop=True, *after, signal=True):
            return PE.run(lambda e: e.matmul(o, l, r, start=start, stop=stop, skip_group_check=True),
                          *after, signal=signal)

        def tr(o, i_, *after, signal=True):
            return PE.run(lambda e: e.transpose(o, i_, ident), *after, signal=signal)

        def vec(fn, *after):
            return DVE.run(fn, *after)

        def pool(fn, *after):
            return PL.run(fn, (PL.sem, PL.count) if PL.count else None, *after)

        def act(fn, *after):
            return SC.run(fn, *after)

        half_exp = st[:, 127:128]
        t_half = pool(lambda e: e.memset(half_exp, -0.5))

        def rsqrt(cols, n, *after, scale=1.0):
            t = vec(lambda e: e.tensor_scalar(cols, cols, scale, EPS, ALU.mult, ALU.add), *after)
            return pool(lambda e: e.tensor_tensor(cols, cols, half_exp.broadcast_to([P, n]), ALU.pow), t, t_half)

        norm_junk = [at(f"norm_junk{m}", [P, PW], 10, skip=1024 * m) for m in range(2)]
        norm_gain = Slots([at(f"norm_gained{i}", [P, TT, PW], 10, skip=2048 + 2048 * i) for i in range(2)])
        row_sums = st[:, 0:16].rearrange("p (s m j) -> p s m j", s=2, m=2)
        rsq = st[:, 120:124]

        junk_done = [None, None]

        def split_from(src, hi, lo, *after):
            t = act(lambda e: e.activation(hi, src, ACT.Copy), *after)
            return vec(lambda e: e.tensor_tensor(lo, src, hi.bitcast(F32), ALU.subtract), t, *after)

        class Norm:

            def __init__(self, gain, final_gain=None, x_free=()):
                self.gain, self.final, self.x_free = gain, final_gain, x_free
                self.sums, self.fed, self.turned, self.x_ready = [], [], [], {}

            def feed(self, *after):
                j = len(self.fed)
                self.fed.append(after)
                cols = slice(j * PW, (j + 1) * PW)
                if self.final is not None:
                    n, gained, free = norm_gain.take()
                    t_gained = pool(lambda e: e.tensor_tensor(gained, h[:, :, cols], self.final[:, cols].unsqueeze(1)
                                                              .broadcast_to([P, TT, PW]), ALU.mult), *after, *free)
                self.squares(0, j, h[:, :, cols], *after)
                if self.final is not None:
                    side.append(self.gained_squares(j, n, gained, t_gained))

            def gained_squares(self, j, n, gained, t):
                self.squares(1, j, gained, t)
                norm_gain.free(n, *junk_done)
                yield

            def squares(self, s, j, src, *after):
                t0 = act(lambda e: e.activation(norm_junk[0], src[:, 0, :], ACT.Square,
                                                accum_out=row_sums[:, s, 0, j:j + 1]), *after, junk_done[0])
                t1 = vec(lambda e: e.tensor_tensor_reduce(norm_junk[1], src[:, 1, :], src[:, 1, :], 1.0, 0.0,
                                                          ALU.mult, ALU.add, row_sums[:, s, 1, j:j + 1]),
                         *after, junk_done[1])
                self.sums += [t0, t1]
                junk_done[:] = [t0, t1]

            def turn(self, *gain_ready):
                j = len(self.turned)
                n, bank, free = side_banks.take()
                b3 = bank.rearrange("p (k t) -> p k t", k=2)
                PE.wait(*free, *self.fed[j])
                for k in range(2):
                    for m in range(TT):
                        f = 2 * j + k
                        t = tr(b3[:, k, m * P:(m + 1) * P], h[:, m, f * P:(f + 1) * P], signal=(k == 1 and m == 1))
                self.turned.append(t)
                gain = [self.gain[:, 2 * j + k:2 * j + k + 1] for k in range(2)]
                for k in range(2):
                    t = act(lambda e: e.activation(xhi[:, 2 * j + k, :], b3[:, k, :], ACT.Copy, scale=gain[k]), t,
                            *gain_ready, *self.x_free)
                for k in range(2):
                    t_lo = vec(lambda e: e.scalar_tensor_tensor(xlo[:, 2 * j + k, :], b3[:, k, :], gain[k],
                                                                xhi[:, 2 * j + k, :].bitcast(F32), ALU.mult,
                                                                ALU.subtract), t)
                side_banks.free(n, t_lo)
                self.x_ready[j] = t_lo

            def scales(self):
                S = 1 if self.final is None else 2
                t = vec(lambda e: e.tensor_reduce(rsq[:, 0:2 * S].rearrange("p (s m) -> p s m", s=S),
                                                  row_sums[:, 0:S], AX.X, ALU.add), *self.sums)
                r = rsq[:, 0:2]
                t = rsqrt(r, 2, t, scale=1.0 / D)
                if self.final is not None:
                    r2 = rsq[:, 2:4]
                    self.h2_scale = (r, t)
                    t = vec(lambda e: e.tensor_tensor(r2, r2, r, ALU.mult), t)
                    t = vec(lambda e: e.tensor_tensor(r2, r2, r, ALU.mult), t)
                    t = rsqrt(r2, 2, t, scale=1.0 / D)
                    t = vec(lambda e: e.tensor_tensor(r2, r2, r, ALU.mult), t)
                    r = r2
                self.r, self.r_ready = r, t

            def rest(self, row=True):
                self.turn()
                self.scales()
                if row:
                    yield
                    yield
                    n, bank, free = side_banks.take()
                    PE.wait(*free, self.r_ready)
                    for m in range(TT):
                        t = mm(bank[:, m * P:(m + 1) * P], self.r[:, m:m + 1].broadcast_to([P, P]), ident,
                               signal=(m == 1))
                    self.row_ready = act(lambda e: e.activation(norm_row, bank[:, 0:T], ACT.Copy), t)
                    side_banks.free(n, self.row_ready)

        row2 = norm_row.unsqueeze(1).broadcast_to([P, 2, T])

        def by_token(dst, src, norm, *after):
            for m in range(TT):
                t = act(lambda e: e.activation(dst[:, m, :], src[:, m, :], ACT.Copy, scale=norm.r[:, m:m + 1]),
                        norm.r_ready, *after)
            return t

        fetch(0)
        c_in = load("constants", cst[:, P:], a["constants"][:, P:])
        fetch(1)
        sm_in = small_loads()
        fetch(2)

        PE.wait(id_in)
        side = []

        def step_side():
            for g in list(side):
                try:
                    next(g)
                except StopIteration:
                    side.remove(g)

        zeros = at("zeros", [P, 512], 20)
        t = vec(lambda e: e.memset(zeros, 0.0))
        for _ in range(WARM_UP):
            mm(banks[0].ap, zeros[:, 0:P], zeros, True, True, t, signal=False)
        norm = Norm(PR("norm_mix"))
        for j in range(4):
            norm.feed(x_in[j])
        norm.scales()
        t_prm = [vec(lambda e: e.tensor_scalar(PR("gconv"), PR("gconv"), 0.5, None, ALU.mult), p_in),
                 vec(lambda e: e.tensor_scalar(PR("fconv")[:, 0:KF * 3], PR("fconv")[:, 0:KF * 3], 0.5, None,
                                               ALU.mult)),
                 vec(lambda e: e.tensor_scalar(PR("gdn_norm"), PR("gdn_norm"), 0.5, None, ALU.mult)),
                 vec(lambda e: e.tensor_tensor(PR("norm1"), PR("norm1"), PR("norm_final"), ALU.mult)),
                 vec(lambda e: e.tensor_scalar(PR("qg"), PR("qg"), float(NA_DIM) ** -0.5, None, ALU.mult))][-1]
        norm.fed = []
        for j in range(4):
            cols = slice(j * PW, (j + 1) * PW)
            norm.fed.append([
                act(lambda e: e.activation(h[:, 0, cols], h[:, 0, cols], ACT.Copy, scale=norm.r[:, 0:1]), norm.r_ready)
                if j < 2 else
                vec(lambda e: e.tensor_scalar(h[:, 0, cols], h[:, 0, cols], norm.r[:, 0:1], None, ALU.mult),
                    norm.r_ready),
                vec(lambda e: e.tensor_scalar(h[:, 1, cols], h[:, 1, cols], norm.r[:, 1:2], None, ALU.mult),
                    norm.r_ready)])
        for j in range(4):
            norm.turn(t_prm)
            if j != 2:
                split_next()
        x_ready = norm.x_ready

        gsm = gts[:, 0:48].rearrange("p (t c) -> p t c", t=2)
        gateT = gts[0:SMALL, 264:264 + T]
        z = gts[:, 48:80].rearrange("p (t c) -> p t c", t=2)
        em = gts[:, 80:112].rearrange("p (t c) -> p t c", t=2)
        zz = gts[:, 112:144].rearrange("p (t c) -> p t c", t=2)
        z2 = gts[:, 144:176].rearrange("p (t c) -> p t c", t=2)
        lg = gts[:, 176:208].rearrange("p (t c) -> p t c", t=2)
        cum = gts[:, 208:248]
        coef = gts[:, 248:264]
        beta_u = st[:, 16:32]
        gc_u = st[:, 32:48]
        egc_u = st[:, 48:64]
        kdec_s = st[:, 64:72]
        c_u = st[:, 72:88]
        bu = beta_u.rearrange("p (h t) -> p h t", t=2)
        G = {}

        def rows_of(sums, h0, n):
            src = scratch_c[sums]
            return bass.AP(tensor=src.tensor, offset=src.offset + h0 * T, ap=[[0, P], [1, n]])

        key_bias_in, key_bias_r = [sem("key_bias_landed"), 0], {}

        def load_key_bias(hh, *after):
            SP.dma(key_bias_in, key_bias[:, 0:P], rows_of(0, hh, P), *after)
            t = SP.dma(key_bias_in, key_bias[:, P:3 * P], rows_of(0, hh, T))
            for s in (slice(0, P), slice(2 * P, 3 * P)):
                t = pool(lambda e: e.tensor_tensor(key_bias[:, s], key_bias[:, s], C("causal"), ALU.add), t, c_in)
            key_bias_r[hh] = t

        def gates():
            for _ in range(12):
                yield
            t_sm = split_from(wsm, wsmh, wsml, *sm_in)
            yield
            yield
            n, bank, free = side_banks.take()
            PE.wait(*free, x_ready[3], t_sm)
            seq = [(xx, ww, k) for k in range(KD) for xx, ww in ((xhi, wsmh), (xlo, wsmh), (xhi, wsml))]
            for m, (xx, ww, k) in enumerate(seq):
                t = mm(bank[0:SMALL, 0:T], ww[:, k, :], xx[:, k, :], m == 0, m == len(seq) - 1,
                       signal=(m == len(seq) - 1))
            t = vec(lambda e: e.tensor_copy(gateT, bank[0:SMALL, 0:T]), t)
            side_banks.free(n, t)
            yield
            yield
            n, bank, free = side_banks.take()
            for m in range(TT):
                t_g = PE.run(lambda e: e.transpose(bank[:, m * SMALL:(m + 1) * SMALL], gateT[:, m * P:(m + 1) * P],
                                                   ident[0:SMALL, 0:SMALL]), *free, t)
            t = vec(lambda e: e.tensor_copy(gsm, bank[:, 0:48].rearrange("p (t c) -> p t c", t=2)), t_g)
            side_banks.free(n, t)
            gb_ = PR("gate_bias").unsqueeze(1).broadcast_to([P, 2, 16])
            t = vec(lambda e: e.tensor_tensor(z, gsm[:, :, 0:16], gb_, ALU.add), t)
            t = vec(lambda e: e.tensor_scalar(z[:, :, 0:8], z[:, :, 0:8], -1.0, None, ALU.mult), t)
            t_abs = vec(lambda e: e.scalar_tensor_tensor(em, z, -1.0, z, ALU.mult, ALU.min), t)
            yield
            yield
            t_e = act(lambda e: e.activation(em, em, ACT.Exp), t_abs)
            t_tb = act(lambda e: e.activation(bu, gsm[:, :, 16:24].rearrange("p t c -> p c t"), ACT.Tanh, scale=0.5))
            G["t_beta"] = vec(lambda e: e.tensor_scalar(beta_u, beta_u, 0.5, 0.5, ALU.mult, ALU.add), t_tb)
            t_al = act(lambda e: e.activation(coef[:, 8:16], PR("a_log"), ACT.Exp), p_in)
            t = vec(lambda e: e.tensor_scalar(coef[:, 8:16], coef[:, 8:16], -1.0, None, ALU.mult), t_al)
            t_coef = vec(lambda e: e.memset(coef[:, 0:8], -1.0))
            yield
            yield
            t = vec(lambda e: e.tensor_scalar(zz, em, 2.0, None, ALU.add), t_e)
            t = vec(lambda e: e.reciprocal(zz, zz), t)
            t = vec(lambda e: e.tensor_tensor(zz, zz, em, ALU.mult), t)
            t = vec(lambda e: e.tensor_tensor(z2, zz, zz, ALU.mult), t)
            t = vec(lambda e: e.tensor_scalar(lg, z2, 1.0 / 19, None, ALU.mult), t)
            for k in range(8, 0, -1):
                if k % 3 == 0:
                    yield
                t = vec(lambda e: e.scalar_tensor_tensor(lg, lg, 1.0 / (2 * k + 1), z2, ALU.add, ALU.mult), t)
            t = vec(lambda e: e.scalar_tensor_tensor(lg, lg, 1.0, zz, ALU.add, ALU.mult), t)
            t = vec(lambda e: e.tensor_scalar(z, z, 0.0, None, ALU.max), t)
            t = vec(lambda e: e.scalar_tensor_tensor(lg, lg, 2.0, z, ALU.mult, ALU.add), t)
            t_lg = vec(lambda e: e.tensor_tensor(lg, lg, coef.unsqueeze(1).broadcast_to([P, 2, 16]), ALU.mult),
                       t, t_coef)
            yield
            yield
            n, bank, free = side_banks.take()
            PE.wait(t_lg, c_in, *free)
            lg0, lg1 = lg[:, 0, :], lg[:, 1, :]
            mm(bank[:, 0:16], upper, lg0, signal=False)
            mm(bank[:, 16:24], ones, lg0[:, 0:8], True, False, signal=False)
            mm(bank[:, 16:24], upper, lg1[:, 0:8], False, True, signal=False)
            mm(bank[:, 24:32], upper, lg1[:, 8:16], signal=False)
            t_c = mm(bank[:, 32:40], ones, lg0[:, 8:16])
            t_cum = t = vec(lambda e: e.tensor_copy(cum, bank[:, 0:40]), t_c)
            side_banks.free(n, t)
            yield
            yield
            n, bank, free = side_banks.take()
            PE.wait(*free)
            for b0, c0 in ((0, 0), (256, 8)):
                mm(bank[0:8, b0:b0 + 128], lg0[:, c0:c0 + 8], upper, signal=False)
                if c0 == 0:
                    mm(bank[0:8, b0 + 128:b0 + 256], lg0[:, 0:8], ones, True, False, signal=False)
                t_r = mm(bank[0:8, b0 + 128:b0 + 256], lg1[:, c0:c0 + 8], upper, c0 != 0, True)
            t_nc = vec(lambda e: e.tensor_scalar(row_nc, bank[0:8, 0:256], -1.0, None, ALU.mult), t_r)
            t_rows = vec(lambda e: e.tensor_copy(row_gc, bank[0:8, 256:512]))
            side_banks.free(n, t_rows)
            G["rows_out"] = [load("c_rows_out", scratch_c[0], row_nc, t_nc),
                             load("gc_rows_out", scratch_c[1], row_gc, t_rows)]
            load_key_bias(0, G["rows_out"][0])
            G["gc_everywhere"] = load("gc_rows_in", decayT.rearrange("p u t -> p (u t)"), rows_of(1, 0, HEADS * T),
                                      G["rows_out"][1])
            yield
            yield
            cu, gu = c_u.rearrange("p (h t) -> p t h", t=2), gc_u.rearrange("p (h t) -> p t h", t=2)
            t = vec(lambda e: e.tensor_copy(cu[:, 0, :], cum[:, 0:8]), t_cum)
            t = vec(lambda e: e.tensor_copy(cu[:, 1, :], cum[:, 16:24]))
            t = vec(lambda e: e.tensor_copy(gu[:, 0, :], cum[:, 8:16]))
            t_gc = G["t_gc"] = vec(lambda e: e.tensor_copy(gu[:, 1, :], cum[:, 24:32]))
            t = vec(lambda e: e.tensor_tensor(kdec_s, cum[:, 32:40], cum[:, 8:16], ALU.subtract))
            G["t_kdec_s"] = act(lambda e: e.activation(kdec_s, kdec_s, ACT.Exp), t)
            G["t_egc"] = act(lambda e: e.activation(egc_u, gc_u, ACT.Exp), t_gc)

        side.append(gates())

        bank_pool = [few_banks]

        def projected(feature_major):
            n, bank, free = bank_pool[0].take()
            t = gemm(bank, free, xhi, xlo, x_ready, feature_major)
            return n, bank, t

        def projected_pair(feature_major):
            got = [bank_pool[0].take() for _ in range(2)]
            for k in (0, HALF):
                done = [gemm(bank, () if k else free, xhi, xlo, x_ready, feature_major, k, not k, k > 0)
                        for _, bank, free in got]
            return [(n, bank, t) for (n, bank, _), t in zip(got, done)]

        tok_ready = {}
        GK, GQ, GV = 1, 0, 2

        def conv_silu(kind, j, dst, product=None):
            n, bank, t = product or projected(True)
            b3 = bank.rearrange("p (c t) -> p c t", c=2)
            na, acc, afree = acc_t.take()
            nt, tmp, tfree = tmp_t.take()
            base = PARAMS["gconv"][0]
            first = 8 * kind + 2 * j
            t1 = act(lambda e: e.activation(tmp, b3, ACT.Copy), t, *tfree)
            for c in range(2):
                w = base + (first + c) * 4
                t2 = act(lambda e: e.activation(acc[:, c, :], b3[:, c, :], ACT.Copy, scale=prm[:, w + 3:w + 4]), t1,
                         t_prm, *afree)
            few_banks.free(n, t2)
            yield
            prev = [None, None]
            for back in (1, 2, 3):
                if back == 3:
                    yield
                for c in range(2):
                    w = base + (first + c) * 4 + 3 - back
                    t3 = prev[c] = vec(lambda e: e.scalar_tensor_tensor(
                        acc[:, c, back:], tmp[:, c, 0:T - back], prm[:, w:w + 1], acc[:, c, back:],
                        ALU.mult, ALU.add), t2, prev[c])
            yield
            t4 = act(lambda e: e.activation(tmp, acc, ACT.Tanh), t3)
            yield
            t5 = vec(lambda e: e.scalar_tensor_tensor(tmp, tmp, 1.0, acc, ALU.add, ALU.mult), t4)
            acc_t.free(na, t5)
            yield
            m, bank2, free = side_banks.take()
            PE.wait(*free, t5)
            b4 = bank2.rearrange("p (u d) -> p u d", u=4)
            for c in range(2):
                for tt in range(TT):
                    t6 = tr(b4[:, 2 * c + tt, :], tmp[:, c, tt * P:(tt + 1) * P], signal=(c == 1 and tt == 1))
            us = slice(4 * j, 4 * j + 4)
            t7 = act(lambda e: e.activation(dst[:, us, :], b4, ACT.Copy), t6)
            side_banks.free(m, t7)
            tok_ready[kind, j] = t7
            tmp_t.free(nt, t6)
            if kind == GV:
                return
            yield
            nq, sq, qfree = sq_t.take()
            for u in range(2):
                unit, sum_ = dst[:, 4 * j + u, :], ss_at[kind][:, 4 * j + u:4 * j + u + 1]
                t8 = act(lambda e: e.activation(sq[:, u, 0:DH], unit, ACT.Square, accum_out=sum_), t7, *qfree)
            for u in range(2, 4):
                unit, sum_ = dst[:, 4 * j + u, :], ss_at[kind][:, 4 * j + u:4 * j + u + 1]
                t9 = vec(lambda e: e.tensor_tensor_reduce(sq[:, u - 2, DH:2 * DH], unit, unit, 1.0, 0.0, ALU.mult,
                                                          ALU.add, sum_), t7, *qfree)
            sq_t.free(nq, t8, t9)
            sq_done[:] = [t8, t9]

        gz_r = []

        def silu_z(j):
            n, bank, t = projected(False)
            b3 = bank.rearrange("p (t c) -> p t c", t=2)
            dst = gz[:, :, j * PW:(j + 1) * PW]
            nt, tmp, tfree = tmp_t.take()
            t = act(lambda e: e.activation(tmp, b3, ACT.Tanh, scale=0.5), t, *tfree)
            t = vec(lambda e: e.scalar_tensor_tensor(dst, tmp, 1.0, b3, ALU.add, ALU.mult), t)
            few_banks.free(n, t)
            tmp_t.free(nt, t)
            gz_r.append(t)
            yield

        ss_at = {1: st[:, 88:104], 0: st[:, 104:120]}
        sq_t = Slots([at(f"squares{i}", [P, 2, T], 14, skip=2048 * i) for i in range(3)])
        sq_done = []

        def run_all(gens):
            for g in gens:
                next(g)
                side.append(g)

        def per_unit(col, n=UNITS):
            return col.unsqueeze(2).broadcast_to([P, n, DH])

        products = projected_pair(True)
        run_all([conv_silu(GK, 0, tok_k, products[0])])
        side.append(conv_silu(GK, 1, tok_k, products[1]))
        conv_of = {C_GK: (GK, tok_k), C_GQ: (GQ, tok_q), C_GV: (GV, tok_v)}
        run_all([silu_z(j) if c == C_GZ else conv_silu(conv_of[c][0], j, conv_of[c][1]) for c, j in conv_order])

        gdn_out = {}

        def q_k_open():
            return any(b.held for b in sq_t.buffers) or len(tok_ready) < 12 or "t_egc" not in G

        def gdn():
            while q_k_open():
                yield
            rk = rsqrt(ss_at[GK], 16, *sq_done)
            rq = rsqrt(ss_at[GQ], 16, *sq_done)
            yield
            halves = [slice(0, 8), slice(8, 16)]
            kdone = []
            for s in halves:
                t = vec(lambda e: e.tensor_tensor(tok_k[:, s, :], tok_k[:, s, :],
                                                  per_unit(ss_at[GK][:, s], 8), ALU.mult), rk)
                kdone.append(t)
            yield
            t_kb = [pool(lambda e: e.tensor_tensor(tok_kb[:, s, :], tok_k[:, s, :], per_unit(beta_u[:, s], 8),
                                                   ALU.mult), t, G["t_beta"], *sq_done)
                    for s, t in zip(halves, kdone)]
            tq = vec(lambda e: e.tensor_scalar(ss_at[GQ], ss_at[GQ], float(DH) ** -0.5, None, ALU.mult), rq)
            t_q = [vec(lambda e: e.tensor_tensor(tok_q[:, s, :], tok_q[:, s, :], per_unit(ss_at[GQ][:, s], 8),
                                                 ALU.mult), tq) for s in halves]
            yield

            def tile(t_, n_):
                return t_.rearrange("p (h t) d -> p h t d", t=2)[:, :, n_, :]

            def tcol(c_, n_):
                return c_.rearrange("p (h t) -> p h t", t=2)[:, :, n_]
            t_qdec = pool(lambda e: e.tensor_tensor(tok_qdec, tile(tok_q, 1), per_unit(tcol(egc_u, 1), 8), ALU.mult),
                          *t_q, G["t_egc"])
            t_v = vec(lambda e: e.tensor_tensor(tok_v, tok_v, per_unit(beta_u), ALU.mult),
                      *[tok_ready[GV, j] for j in range(4)], G["t_beta"])
            kT_r = turn(tok_k, kT, [kdone[0], kdone[1]])
            yield
            yield
            t_kbe = pool(lambda e: e.tensor_tensor(tok_kbe, tile(tok_kb, 1), per_unit(tcol(egc_u, 1), 8), ALU.mult),
                         *t_kb, G["t_egc"])
            t_kdec = pool(lambda e: e.tensor_tensor(tok_kdec, tile(tok_k, 0), per_unit(kdec_s, 8), ALU.mult),
                          *kdone, G["t_kdec_s"])
            qT_r = turn(tok_q, qT, t_q)
            yield
            kbT_r = turn(tok_kb, kbT, t_kb)
            dec = []
            for b in range(4):
                us = slice(4 * b, 4 * b + 4)
                t = vec(lambda e: e.tensor_tensor(decayT[:, us, :], decayT[:, us, :], per_unit(gc_u[:, us], 4),
                                                  ALU.subtract), G["gc_everywhere"], G["t_gc"])
                dec.append(t)
            yield
            t_pl = []
            for b in range(4):
                us = slice(4 * b, 4 * b + 4)
                t = pool(lambda e: e.tensor_tensor(
                    decayT[:, us, :], decayT[:, us, :],
                    C("decay_mask").unsqueeze(1).broadcast_to([P, 4, P]), ALU.add), dec[b])
                t_pl.append(t)
            yield
            yield
            t_dec = [act(lambda e: e.activation(decayT[:, 4 * b:4 * b + 4, :], decayT[:, 4 * b:4 * b + 4, :],
                                                ACT.Exp), t_pl[b]) for b in range(4)]
            qd_r = []
            for b in range(2):
                n, bank, free = side_banks.take()
                b4 = bank.rearrange("p (u t) -> p u t", u=4)
                for u in range(4):
                    t = tr(b4[:, u, :], tok_qdec[:, 4 * b + u, :], *free, t_qdec, signal=(u == 3))
                t = act(lambda e: e.activation(qdecT[:, 4 * b:4 * b + 4, :], b4, ACT.Copy), t)
                side_banks.free(n, t)
                qd_r.append(t)
            yield
            at_r, an_r = [], []
            for dst, lhs_r, rhs, rr, res, wfree in (
                    (AT, kT_r, kbT, kbT_r, at_r, [t_kbe, t_kdec, t_qdec] + kT_r),
                    (attnT, kT_r, qT, qT_r, an_r, qT_r)):
                for b in range(4):
                    n, bank, free = side_banks.take()
                    b4 = bank.rearrange("p (u t) -> p u t", u=4)
                    PE.wait(*free, *lhs_r, *rr)
                    for u in range(4):
                        uu = 4 * b + u
                        t = mm(b4[:, u, :], kT[:, uu, :], rhs[:, uu, :], signal=(u == 3))
                    us = slice(4 * b, 4 * b + 4)
                    t = vec(lambda e: e.tensor_tensor(dst[:, us, :], b4, decayT[:, us, :], ALU.mult), t,
                            t_dec[b], *wfree)
                    side_banks.free(n, t)
                    res.append(t)
                    kk_last = t
                if dst is AT:
                    yield
            yield
            outs = []
            box = [sem("blocks_out"), 0]
            for b in range(NBLK):
                src = AT[b * BLOCK:(b + 1) * BLOCK, :, b * BLOCK:(b + 1) * BLOCK]
                dst = scratch_a[b].rearrange("u s t -> s u t")
                outs.append(SP.dma(box, dst, src, *at_r))
            t_in = load("blocks_A", blkA, scratch_a.rearrange("b u s t -> (b u) s t"), outs[-1], *qd_r)
            x0 = z0 = [pool(lambda e: e.memset(m_, 0.0), kk_last, an_r[-1], *at_r) for m_ in (X, XT, PX)][-1]
            yield
            yield
            bt_free = kbT_r + t_kb + [t_kbe]

            def below(lv, *free):
                mask = C("level")[:, lv * P:(lv + 1) * P].unsqueeze(1).broadcast_to([P, 4, P])
                return [pool(lambda e: e.tensor_tensor(BT[:, 4 * b:4 * b + 4, :], AT[:, 4 * b:4 * b + 4, :], mask,
                                                       ALU.mult), at_r[b], *free) for b in range(4)]

            bts = below(0, *bt_free)
            t0 = vec(lambda e: e.tensor_scalar(blkA, blkA, -1.0, None, ALU.mult), t_in)
            t = vec(lambda e: e.memset(blkX, 0.0), *qd_r)
            t = vec(lambda e: e.memset(blkX.rearrange("p a b -> p (a b)")[:, ::BLOCK + 1], 1.0), t)
            for i in range(1, BLOCK):
                if i % 3 == 0:
                    yield
                t = vec(lambda e: e.tensor_tensor(
                    blkT[:, 0:i * i].rearrange("p (k j) -> p k j", j=i),
                    blkX[:, 0:i, 0:i].rearrange("p j k -> p k j"),
                    blkA[:, 0:i, i].unsqueeze(1).broadcast_to([P, i, i]), ALU.mult), t, t0)
                t = vec(lambda e: e.tensor_reduce(
                    blkX[:, i, 0:i], blkT[:, 0:i * i].rearrange("p (k j) -> p k j", j=i), AX.X, ALU.add), t)
            blkXT = blkT.rearrange("p (a b) -> p a b", b=BLOCK)
            t_t = vec(lambda e: e.tensor_copy(blkXT, blkX.rearrange("p a b -> p b a")), t)
            yield
            backs = [SP.dma([sem(f"blocks_back{m}"), 0], scratch_x[m].rearrange("b u s t -> (b u) s t"), blk, tok)
                     for m, (blk, tok) in enumerate(((blkX, t), (blkXT, t_t)))]
            x_r, xT_r = [], []
            for m, (mat, res) in enumerate(((X, x_r), (XT, xT_r))):
                box = [sem(f"blocks_in{m}"), 0]
                for b in range(NBLK):
                    t_in = SP.dma(box, mat[b * BLOCK:(b + 1) * BLOCK, :, b * BLOCK:(b + 1) * BLOCK],
                                  scratch_x[m, b].rearrange("u s t -> s u t"), backs[m], x0)
                res.append(t_in)
            for _ in range(4):
                yield
            for lv in range(3):
                w = BLOCK << lv
                last_level = lv == 2

                def columns(m_, b, half):
                    v = m_[:, 8 * b:8 * b + 8, :].rearrange("p u (g h w) -> p u g h w", h=2, w=w)[:, :, :, half, :]
                    return v.rearrange("p u g w -> p u (g w)") if w == 64 else v

                inner, lower = (slice(0, 64), slice(64, P)) if last_level else (slice(0, P), slice(0, P))
                px = []
                for b in range(2):
                    n, bank, free = side_banks.take()
                    PE.wait(*free, *bts, *x_r)
                    for u in range(8):
                        src = columns(X, b, 0)[:, u]
                        o = bank[:, 64 * u:64 * u + 64].rearrange("p (g w) -> p g w", w=w) if w < 64 \
                            else bank[lower, 64 * u:64 * u + 64]
                        t = mm(o, BT[inner, 8 * b + u, lower], src[inner], signal=(u == 7))
                    dst = columns(PX, b, 0)[lower]
                    src = bank.rearrange("p (u g w) -> p u g w", u=8, w=w) if w < 64 \
                        else bank[lower].rearrange("p (u w) -> p u w", u=8)
                    if b:
                        t = act(lambda e: e.activation(dst, src, ACT.Copy), t, z0)
                    else:
                        t = vec(lambda e: e.tensor_copy(dst, src), t, z0)
                    side_banks.free(n, t)
                    px.append(t)
                if not last_level:
                    bts = below(lv + 1, *px)
                yield
                products = []
                for b in range(2):
                    n, bank, free = side_banks.take()
                    PE.wait(*free, *px, *xT_r)
                    for u in range(8):
                        o = bank[:, 64 * u:64 * u + 64]
                        if w < 64:
                            o = o.rearrange("p (g w) -> p g w", w=w)
                        tpe = mm(o[inner], PX[lower, 8 * b + u, 0:64 if last_level else P],
                                 columns(XT, b, 1)[lower, u], signal=(u == 7))
                    src = bank.rearrange("p (u g w) -> p u g w", u=8, w=w) if w < 64 \
                        else bank[inner].rearrange("p (u w) -> p u w", u=8)
                    products.append((n, columns(XT, b, 1)[inner], src))
                if lv == 0:
                    z0 = pool(lambda e: e.memset(PX, 0.0), tpe)
                bt_free = [tpe]
                xT_r = []
                for n, dst, src in products:
                    xT_r.append(vec(lambda e: e.tensor_tensor(dst, dst, src, ALU.subtract), tpe))
                    side_banks.free(n, xT_r[-1])
                yield
                yield
                if lv == 0:
                    x_r = turn(XT, X, xT_r, [tpe])
                elif lv == 1:
                    x_r = []
                    for b in range(2):
                        n, bank, free = side_banks.take()
                        for u in range(8):
                            t = PE.run(lambda e: e.transpose(bank[0:64, 64 * u:64 * u + 64],
                                                             XT[0:64, 8 * b + u, 0:64], ident[0:64, 0:64]),
                                       *free, *xT_r, signal=(u == 7))
                        t = act(lambda e: e.activation(X[0:64, 8 * b:8 * b + 8, 0:64],
                                                       bank[0:64].rearrange("p (u w) -> p u w", u=8), ACT.Copy), t)
                        side_banks.free(n, t)
                        x_r.append(t)
                yield
            u0_r, nw_r, s1_r, u1_r, o_r = [], [], [], [], []

            def four(b, dst, pairs, res, *after, neg=False, dfree=()):
                n, bank, free = side_banks.take()
                b4 = bank.rearrange("p (u t) -> p u t", u=4)
                PE.wait(*free, *after)
                for u in range(4):
                    ps = pairs(4 * b + u)
                    for m, (l, r) in enumerate(ps):
                        t = mm(b4[:, u, :], l, r, m == 0, m == len(ps) - 1,
                               signal=(u == 3 and m == len(ps) - 1))
                if neg or b % 2:
                    t = act(lambda e: e.activation(dst, b4, ACT.Copy, scale=-1.0 if neg else 1.0), t, *dfree)
                else:
                    t = vec(lambda e: e.tensor_copy(dst, b4), t, *dfree)
                side_banks.free(n, t)
                res.append(t)
            hs = [slice(0, 4), slice(4, 8)]
            for b in range(2):
                four(b, U0[:, hs[b], :], lambda q_: [(XT[:, 2 * q_, :], tok_v[:, 2 * q_, :])], u0_r, *xT_r, t_v,
                     dfree=[kk_last, an_r[-1]])
                four(b, nwT[:, hs[b], :], lambda q_: [(tok_kbe[:, q_, :], XT[:, 2 * q_ + 1, :])], nw_r, t_kbe,
                     neg=True, dfree=bts)
            yield
            for b in range(2):
                four(b, S1[:, hs[b], :], lambda q_: [(tok_kdec[:, q_, :], U0[:, q_, :])], s1_r, *u0_r, dfree=bts)
            yield
            for b in range(2):
                four(b, U1[:, hs[b], :], lambda q_: [(XT[:, 2 * q_ + 1, :], tok_v[:, 2 * q_ + 1, :]),
                                                     (nwT[:, q_, :], S1[:, q_, :])], u1_r, *s1_r, *nw_r)
            o4 = o_tok.rearrange("p (h t) d -> p h t d", t=2)
            for b in range(2):
                four(b, o4[:, hs[b], 0, :], lambda q_: [(attnT[:, 2 * q_, :], U0[:, q_, :])], o_r, *u0_r,
                     dfree=bt_free)
            yield
            for b in range(2):
                four(b, o4[:, hs[b], 1, :], lambda q_: [(qdecT[:, q_, :], S1[:, q_, :]),
                                                        (attnT[:, 2 * q_ + 1, :], U1[:, q_, :])], o_r, *u1_r)
            gdn_out["solve_done"] = o_r[-1]
            yield
            t = [act(lambda e: e.activation(X[:, s, :], o_tok[:, s, :], ACT.Square), *o_r, *u0_r) for s in halves]
            yield
            for s, t_sq in zip(halves, t):
                t = vec(lambda e: e.tensor_reduce(st[:, s], X[:, s, :], AX.X, ALU.add), t_sq)
            yield
            t_ro = rsqrt(st[:, 0:16], 16, t, scale=1.0 / DH)
            t_gz = [pool(lambda e: e.tensor_tensor(tile(o_tok, m), tile(o_tok, m),
                                                   gz[:, m].rearrange("p (h d) -> p h d", h=HEADS), ALU.mult),
                         t_sq, *gz_r) for m in range(TT)]
            yield
            yield
            t = [vec(lambda e: e.tensor_tensor(o_tok[:, s, :], o_tok[:, s, :], per_unit(st[:, s], 8), ALU.mult),
                     t_ro, *t_gz) for s in halves][-1]
            yield
            gdn_out["gz_done"] = t
            yield
            yield
            yg = []
            for b in range(4):
                n, bank, free = side_banks.take()
                b4 = bank.rearrange("p (u t) -> p u t", u=4)
                for u in range(4):
                    tt_ = tr(b4[:, u, :], o_tok[:, 4 * b + u, :], *free, t, signal=(u == 3))
                hi = ygh[:, 2 * b:2 * b + 2, :].rearrange("p h (t q) -> p (h t) q", t=2)
                lo = ygl[:, 2 * b:2 * b + 2, :].rearrange("p h (t q) -> p (h t) q", t=2)
                t1 = act(lambda e: e.activation(hi, b4, ACT.Copy, scale=PR("gdn_norm")), tt_, t_prm,
                         t_ro)
                t2 = vec(lambda e: e.scalar_tensor_tensor(
                    lo, b4, PR("gdn_norm"), hi.bitcast(F32), ALU.mult, ALU.subtract), t1)
                side_banks.free(n, t2)
                yg.append(t2)
            gdn_out["y"] = yg
            yield

        def turn(src, dst, ready_, dfree=()):
            res = []
            for b in range(4):
                n, bank, free = side_banks.take()
                b4 = bank.rearrange("p (u t) -> p u t", u=4)
                PE.wait(*free, *ready_)
                for u in range(4):
                    t = tr(b4[:, u, :], src[:, 4 * b + u, :], signal=(u == 3))
                if b % 2:
                    t = act(lambda e: e.activation(dst[:, 4 * b:4 * b + 4, :], b4, ACT.Copy), t, *dfree)
                else:
                    t = vec(lambda e: e.tensor_copy(dst[:, 4 * b:4 * b + 4, :], b4), t, *dfree)
                side_banks.free(n, t)
                res.append(t)
            return res

        side.append(gdn())

        yf = []

        def fox_head(hh):
            fst = st[:, 128 + 4 * hh:132 + 4 * hh]
            nm, sums = fst[:, 0:2], fst[:, 2:4]
            parts = [slice(0, P), slice(P, 3 * P)]
            n, bank, free = fox_banks.take()
            PE.wait(*free, fox_r["q", hh // 2], fox_r["k", hh // 2])
            mm(bank[:, 0:P], qfT[:, hh, 0:P], kfT[:, hh, 0:P], signal=False)
            t_s = mm(bank[:, P:3 * P], qfT[:, hh, P:T], kfT[:, hh, :])
            yield
            npb, pb, pfree = fox_p.take()
            tx = []
            for m, s in enumerate(parts):
                tx.append(vec(lambda e: e.scalar_tensor_tensor(
                    pb[:, s], bank[:, s], c_u[:, 2 * hh + m:2 * hh + m + 1], key_bias[:, s], ALU.add, ALU.add),
                    t_s, key_bias_r[hh], *pfree))
            fox_banks.free(n, tx[1])
            if hh + 1 < HEADS:
                load_key_bias(hh + 1, tx[1])
            for m, s in enumerate(parts):
                t = vec(lambda e: e.tensor_reduce(nm[:, m:m + 1], pb[:, s], AX.X, ALU.max, negate=True), tx[m])
                tx[m] = t
            yield
            for m, s in enumerate(parts):
                tx[m] = act(lambda e: e.activation(pb[:, s], pb[:, s], ACT.Exp, bias=nm[:, m:m + 1],
                                                   accum_out=sums[:, m:m + 1]), tx[m])
            yield
            t = vec(lambda e: e.reciprocal(sums, sums), *tx)
            for m, s in enumerate(parts):
                t_p = vec(lambda e: e.tensor_scalar(pb[:, s], pb[:, s], sums[:, m:m + 1], None, ALU.mult), t)
            yield
            n, bank2, free = fox_banks.take()
            for u in range(3):
                t = tr(bank2[:, u * P:(u + 1) * P], pb[:, u * P:(u + 1) * P], *free, t_p, signal=(u == 2))
            fox_p.free(npb, t)
            nT, pT, tfree = fox_pT.take()
            t = act(lambda e: e.activation(pT, bank2[:, 0:3 * P], ACT.Copy), t, *tfree)
            fox_banks.free(n, t)
            yield
            n, bank3, free = fox_banks.take()
            PE.wait(*free, t, fox_r["v", hh // 2])
            vs = slice(hh * DH, (hh + 1) * DH)
            mm(bank3[:, 0:P], vf[:, 0, vs], pT[:, 0:P], True, True, signal=False)
            mm(bank3[:, P:T], vf[:, 0, vs], pT[:, P:2 * P], True, False, signal=False)
            t = mm(bank3[:, P:T], vf[:, 1, vs], pT[:, 2 * P:3 * P], False, True)
            fox_pT.free(nT, t)
            t = split_from(bank3[:, 0:T], yfh[:, hh, :], yfl[:, hh, :], t, t_s)
            fox_banks.free(n, t)
            yf.append(t)

        def in_steps(works, pace=1, may_start=lambda n: True):
            works, running, wait, started = list(works), [], 0, 0
            while works or running:
                for g in list(running):
                    try:
                        next(g)
                    except StopIteration:
                        running.remove(g)
                wait -= 1
                if works and wait <= 0 and may_start(started):
                    running.append(works.pop(0))
                    next(running[-1])
                    wait, started = pace, started + 1
                yield

        fox_r = {}
        for j in range(4):
            for name, dst, scale in (("q", qfT, float(DH) ** -0.5), ("k", kfT, 1.0)):
                n, bank, t = projected(True)
                b3 = bank.rearrange("p (c t) -> p c t", c=2)
                t = act(lambda e: e.activation(dst[:, 2 * j:2 * j + 2, :], b3, ACT.Copy, scale=scale), t)
                few_banks.free(n, t)
                fox_r[name, j] = t
            n, bank, t = projected(False)
            fox_r["v", j] = vec(lambda e: e.tensor_copy(vf[:, :, j * PW:(j + 1) * PW],
                                                        bank.rearrange("p (t c) -> p t c", t=2)), t)
            few_banks.free(n, fox_r["v", j])
            if j == 0:
                side.append(in_steps((fox_head(hh) for hh in range(HEADS)), 3,
                                     lambda hh: ("v", hh // 2) in fox_r))
        gate_r = {}

        def gate(name, dst, j, *after):
            n, bank, t = projected(True)
            d = dst[:, 2 * j:2 * j + 2, :]
            x_read = act(lambda e: e.activation(d, bank.rearrange("p (c t) -> p c t", c=2), ACT.Tanh, scale=0.5), t,
                         *after)
            few_banks.free(n, x_read)
            gate_r[name, j] = pool(lambda e: e.tensor_scalar(d, d, 0.5, 0.5, ALU.mult, ALU.add), x_read)
            return x_read

        for j in range(4):
            gate("f", gate_f, j, *G["rows_out"])
        while len(yf) < HEADS:
            step_side()
        for j in range(4):
            n, bank, free = few_banks.take()
            t = gemm(bank, free, yfh, yfl, yf[1::2], True)
            d = gate_f[:, 2 * j:2 * j + 2, :]
            gate_r["f", j] = vec(lambda e: e.tensor_tensor(d, bank.rearrange("p (c t) -> p c t", c=2), d, ALU.mult), t,
                                 gate_r["f", j])
            few_banks.free(n, gate_r["f", j])
        while "solve_done" not in gdn_out:
            step_side()
        for j in range(4):
            x_done = gate("g", gate_g, j, gdn_out["solve_done"])
        while side:
            step_side()
        bank_pool[0] = gemm_banks

        y_r = []

        def mix(j, t):
            d_f, d_g = gate_f[:, 2 * j:2 * j + 2, :], gate_g[:, 2 * j:2 * j + 2, :]
            t = pool(lambda e: e.tensor_tensor(d_g, d_g, d_f, ALU.add), t, gate_r["f", j])
            yield
            y_r.append(split_from(d_g, yh[:, 2 * j:2 * j + 2, :], yl[:, 2 * j:2 * j + 2, :], t))

        for j in range(4):
            n, bank, free = gemm_banks.take()
            t = gemm(bank, free, ygh, ygl, gdn_out["y"], True)
            d = gate_g[:, 2 * j:2 * j + 2, :]
            t = vec(lambda e: e.tensor_tensor(d, bank.rearrange("p (c t) -> p c t", c=2), d, ALU.mult), t,
                    gate_r["g", j])
            gemm_banks.free(n, t)
            if j == 3:
                while side:
                    step_side()
            run_all([mix(j, t)])
        while side:
            step_side()
        h_in = load("x_again", h, a["x"][0].rearrange("(t p) d -> p t d", p=P), gdn_out["gz_done"])

        def add_to_h(n, bank, t, j, *after):
            hs_ = h[:, :, j * PW:(j + 1) * PW]
            t = vec(lambda e: e.tensor_tensor(hs_, bank.rearrange("p (t c) -> p t c", t=2), hs_, ALU.add), t, *after)
            gemm_banks.free(n, t)
            return t
        norm = Norm(PR("norm_ffn"), x_free=[x_done])
        for j in range(4):
            n, bank, free = gemm_banks.take()
            t = gemm(bank, free, yh, yl, y_r, False)
            pe_h_done = t
            t_h = add_to_h(n, bank, t, j, h_in)
            if j:
                norm.turn()
            norm.feed(t_h, y_r[-1])
        x_ready = norm.x_ready
        side.append(norm.rest())

        late = [gdn_out["y"][-1], yf[-1], y_r[-1], pe_h_done]
        box = [sem("rpb_landed"), 0]
        for rq in range(GRID_ROWS):
            dst = bias2[GRID * (rq % 2):GRID * (rq % 2) + GRID, :, rq // 2, :]
            src = a["rpb_skew"][:, :, (3 - rq) * GRID:(3 - rq) * GRID + T]
            t_rpb = SP.dma(box, dst, src, *late)
        band_in = load("band", band, a["bands"], *late)
        wpool_in = load("wpool", wpool, a["w_pool_2"][0].rearrange("g c d -> c g d"), *late)
        t_b = []

        def mask_bias():
            for half in range(2):
                part = bias2[GRID * half:GRID * half + GRID].rearrange("p h t (r c) -> p (h t r) c", c=GRID)
                hi_part, lo_part = part[:, :, 0:GRID - WIN_COLS], part[:, :, WIN_COLS:GRID]
                t = pool(lambda e: e.affine_select(hi_part, hi_part, [[0, 64], [1, GRID - WIN_COLS]], ALU.is_ge, NEG,
                                                   WIN_COLS // 2, -1), t_rpb)
                yield
                t = pool(lambda e: e.affine_select(lo_part, lo_part, [[0, 64], [-1, GRID - WIN_COLS]], ALU.is_ge,
                                                   NEG, WIN_COLS // 2 - 1 - WIN_COLS, 1), t)
                t_b[:] = [t]
                yield

        def ffn_down(a_r, norm, *after):
            bks = [gemm_banks.take() for _ in range(4)]
            res = []
            for k in range(0, KF, 8):
                for j in range(4):
                    n, bank, free = bks[j]
                    last = k + 8 >= KF
                    t = gemm(bank, free if k == 0 else (), acth, actl, a_r, False, k, k == 0, last)
                    if last:
                        res.append(add_to_h(n, bank, t, j, *after))
                        if norm and j:
                            norm.turn()
                        if norm:
                            norm.feed(res[-1], a_r[KF // 2 - 1], *after)
                        else:
                            write_out(j, res[-1])
            return res, t

        ft = Slots([(at(f"ff_gate{i}", [P, 2, T], 10, skip=4096 * i), at(f"ff_val{i}", [P, 2, T], 10,
                                                                         skip=4096 * i + 2048)) for i in range(2)])
        ft2 = Slots([at(f"ff_tanh{i}", [P, 2, T], 18, skip=2048 * i) for i in range(4)])
        ft_raw = Slots([at(f"ff_raw{i}", [P, 2, T], 17, skip=2048 * i) for i in range(3)])
        a_r = {}

        def ffn1_conv(side_, bank, t, acc, tfree, nr, raw_, out_tok):
            for _ in range(1 + (side_ == 1 and out_tok["j"] == 0)):
                yield
            base = PARAMS["fconv"][0] + (side_ * KF + 2 * out_tok["j"]) * 3
            for c in range(2):
                w = base + 3 * c
                t2 = act(lambda e: e.activation(acc[:, c, :], raw_[:, c, :], ACT.Copy, scale=prm[:, w + 2:w + 3]),
                         t, t_prm, *tfree)
            prev = [None, None]
            for back in (1, 2):
                for c in range(2):
                    w = base + 3 * c + 2 - back
                    prev[c] = vec(lambda e: e.scalar_tensor_tensor(
                        acc[:, c, back:], raw_[:, c, 0:T - back], prm[:, w:w + 1], acc[:, c, back:],
                        ALU.mult, ALU.add), t2, prev[c])
            ft_raw.free(nr, prev[1])
            out_tok[side_] = prev[1]

        def ffn1_tail(j, nt, bufs, t_c):
            while 1 not in t_c:
                yield
            g_, v_ = bufs
            n2, th, hfree = ft2.take()
            t = act(lambda e: e.activation(th, g_, ACT.Tanh), t_c[0], *hfree)
            yield
            t = vec(lambda e: e.scalar_tensor_tensor(th, th, 1.0, g_, ALU.add, ALU.mult), t)
            t = pool(lambda e: e.tensor_tensor(th, th, v_, ALU.mult), t, t_c[1])
            ft.free(nt, t)
            yield
            yield
            t = split_from(th, acth[:, 2 * j:2 * j + 2, :], actl[:, 2 * j:2 * j + 2, :], t)
            ft2.free(n2, t)
            a_r[j] = t

        for j in range(KF // 2):
            t_c = {"j": j}
            if j == 3:
                side.append(mask_bias())
            pair = projected_pair(True) if j == 0 else None
            for side_ in range(2):
                n, bank, t = pair[side_] if pair else projected(True)
                b3 = bank.rearrange("p (c t) -> p c t", c=2)
                if side_ == 0:
                    nt, bufs, tfree = ft.take()
                nr, raw_, rfree = ft_raw.take()
                t = vec(lambda e: e.tensor_tensor(raw_, b3, row2, ALU.mult), t, norm.row_ready, *rfree, *late)
                gemm_banks.free(n, t)
                side.append(ffn1_conv(side_, bank, t, bufs[side_], tfree, nr, raw_, t_c))
            side.append(ffn1_tail(j, nt, bufs, t_c))
        while len(a_r) < KF // 2 - 1:
            step_side()
        gain_in = load("gain_final", gain_final, bass.AP(tensor=a["norm_final"].tensor, offset=a["norm_final"].offset,
                                                         ap=[[0, P], [1, D]]), *late)
        norm = Norm(PR("norm1"), gain_final)
        h_r, pe_down = ffn_down(a_r, norm, gain_in)
        x_ready = norm.x_ready
        side.append(norm.rest(False))
        pair = projected_pair(False)
        r_h, t_rh = norm.h2_scale
        h2_r = []
        for m in range(TT):
            t = act(lambda e: e.activation(h[:, m, :], h[:, m, :], ACT.Copy, scale=r_h[:, m:m + 1]), t_rh,
                    *norm.turned, *norm.sums)
            h2_r.append(pool(lambda e: e.tensor_tensor(h[:, m, :], h[:, m, :], gain_final, ALU.mult), t, gain_in))

        tok2, t3 = {}, {}
        sq2_t = Slots([at(f"sq2_{i}", [P, TT, PW], 23.5, skip=2048 * i) for i in range(2)])
        mixh, mixl = at("mix_hi", [P, KD, T], 11, F32R), at("mix_lo", [P, KD, T], 12, F32R)

        def qk_norm(name, src, dstT, gain, j):
            s4 = src[:, :, j * PW:(j + 1) * PW].rearrange("p t (h d) -> p t h d", d=NA_DIM)
            ssq = st[:, 16 * (1 + (name == "k")) + 8 * j:][:, 0:8]
            s2 = ssq.rearrange("p (t h) -> p t h", t=2)
            nq, sq2, qfree = sq2_t.take()
            t = act(lambda e: e.activation(sq2, src[:, :, j * PW:(j + 1) * PW], ACT.Square), tok2[name, j], *qfree)
            yield
            t = vec(lambda e: e.tensor_reduce(s2, sq2.rearrange("p t (h d) -> p t h d", d=NA_DIM), AX.X, ALU.add), t)
            sq2_t.free(nq, t)
            t = rsqrt(ssq, 8, t, scale=1.0 / NA_DIM)
            yield
            yield
            t = vec(lambda e: e.tensor_tensor(s4, s4, s2.unsqueeze(3).broadcast_to([P, 2, 4, NA_DIM]), ALU.mult), t)
            yield
            n, bank, free = side_banks.take()
            b3 = bank.rearrange("p (f t) -> p f t", f=2)
            for f in range(2):
                for m in range(TT):
                    t2 = tr(b3[:, f, m * P:(m + 1) * P], src[:, m, (2 * j + f) * P:(2 * j + f + 1) * P], *free, t,
                            signal=(f == 1 and m == 1))
            t = act(lambda e: e.activation(dstT[:, 2 * j:2 * j + 2, :], b3, ACT.Copy, scale=PR(gain)), t2,
                    *late, *h2_r)
            side_banks.free(n, t)
            yield
            t3[name, j] = t

        def pooled(g):
            yield
            n, bank, free = side_banks.take()
            for m, to in enumerate((slice(0, P + POOL_REACH), slice(P - POOL_REACH, T))):
                t = mm(bank[:, to], u2[:, m, g * P:(g + 1) * P], band[:, g, m, to], m == 0, m == 1, *free,
                       tok2["u", g // 2], band_in)
            t = vec(lambda e: e.tensor_copy(poolT[:, g, :], bank[:, 0:T]), t)
            side_banks.free(n, t)
            yield
            n, bank2, free = side_banks.take()
            t = mm(bank2[:, 0:T], wpool[:, g, :], poolT[:, g, :], True, True, *free, t, wpool_in)
            sc_ = PR("pool_scale")[:, g:g + 1]
            t1 = act(lambda e: e.activation(mixh[:, 4 + g, :], bank2[:, 0:T], ACT.Copy, scale=sc_), t, pe_down)
            t2 = vec(lambda e: e.scalar_tensor_tensor(mixl[:, 4 + g, :], bank2[:, 0:T], sc_,
                                                      mixh[:, 4 + g, :].bitcast(F32), ALU.mult, ALU.subtract), t1)
            side_banks.free(n, t2)
            mix_r[4 + g] = t2

        na_p = Slots([at(f"na_p{i}", [P, TT, T], 13, skip=2048 * i) for i in range(4)])
        na_pT = Slots([at(f"na_pT{i}", [P, TT, T], 14, skip=2048 * i) for i in range(4)])
        nst = st[:, 48:48 + 32].rearrange("p (h c) -> p h c", c=4)
        ybank, mix_r = {}, {}

        def na_head(hh):
            p0 = NA_DIM * (hh % 2)
            n, bank, free = side_banks.take()
            b3 = bank.rearrange("p (t k) -> p t k", t=2)
            for m in range(TT):
                t = mm(b3[:, m, :], q2T[p0:p0 + NA_DIM, hh // 2, m * P:(m + 1) * P],
                       k2T[p0:p0 + NA_DIM, hh // 2, :], True, True, *free, t3["q", hh // 4],
                       t3["k", hh // 4], signal=(m == 1))
            npb, pb, pfree = na_p.take()
            nm, sums = nst[:, hh, 0:2], nst[:, hh, 2:4]
            for m in range(TT):
                t = vec(lambda e: e.tensor_tensor_reduce(pb[:, m, :], b3[:, m, :], bias2[:, hh, m, :], 1.0, 3 * NEG,
                                                         ALU.add, ALU.max, nm[:, m:m + 1]), t, *t_b, *pfree)
            side_banks.free(n, t)
            t = vec(lambda e: e.tensor_scalar(nm, nm, -1.0, None, ALU.mult), t)
            yield
            tx = [act(lambda e: e.activation(pb[:, m, :], pb[:, m, :], ACT.Exp, bias=nm[:, m:m + 1],
                                             accum_out=sums[:, m:m + 1]), t) for m in range(TT)]
            yield
            t = vec(lambda e: e.reciprocal(sums, sums), *tx)
            for m in range(TT):
                t_p = vec(lambda e: e.tensor_scalar(pb[:, m, :], pb[:, m, :], sums[:, m:m + 1], None, ALU.mult), t)
            yield
            n, bank2, free = side_banks.take()
            c3 = bank2.rearrange("p (k t) -> p k t", k=2)
            for k in range(2):
                for m in range(TT):
                    t2 = tr(c3[:, k, m * P:(m + 1) * P], pb[:, m, k * P:(k + 1) * P], *free, t_p,
                            signal=(k == 1 and m == 1))
            na_p.free(npb, t2)
            nT, pT, tfree = na_pT.take()
            t = act(lambda e: e.activation(pT, c3, ACT.Copy), t2, *tfree)
            side_banks.free(n, t)
            yield
            while ("v", hh // 4) not in tok2:
                yield
            if hh % 2 == 0:
                ybank[0] = side_banks.take()
            n, bank3, free = ybank[0]
            for k in range(2):
                t = mm(bank3[p0:p0 + NA_DIM, 0:T], v2[:, k, hh * NA_DIM:(hh + 1) * NA_DIM], pT[:, k, :],
                       k == 0, k == 1, *free, t, tok2["v", hh // 4])
            na_pT.free(nT, t)
            if hh % 2:
                t = split_from(bank3[:, 0:T], mixh[:, hh // 2, :], mixl[:, hh // 2, :], t, pe_down)
                side_banks.free(n, t)
                mix_r[hh // 2] = t

        for name, dst, j in (("q", q2, 0), ("k", k2, 0), ("q", q2, 1), ("k", k2, 1), ("v", v2, 0), ("u", u2, 0),
                             ("u", u2, 1), ("v", v2, 1)):
            n, bank, t = pair.pop(0) if pair else projected(False)
            tok2[name, j] = by_token(dst[:, :, j * PW:(j + 1) * PW], bank.rearrange("p (t c) -> p t c", t=2), norm, t,
                                     *late)
            gemm_banks.free(n, tok2[name, j])
            x_done = t
            if name == "q":
                side.append(qk_norm("q", q2, q2T, "qg", j))
            if name == "k":
                side.append(qk_norm("k", k2, k2T, "kg", j))
            if name == "v" and j == 0:
                side.append(in_steps((na_head(hh) for hh in range(HEADS)), 1,
                                     lambda hh: ("k", hh // 4) in t3 and ("q", hh // 4) in t3))
            if name == "u":
                side.append(in_steps(pooled(g) for g in range(2 * j, 2 * j + 2)))
        bks = [gemm_banks.take() for _ in range(4)]
        while 7 not in mix_r:
            step_side()
        for j in range(4):
            n, bank, free = bks[j]
            gemm(bank, free, mixh, mixl, {2: mix_r[5], 3: mix_r[7]}, False, 4, True, False)
        while side:
            step_side()
        norm = Norm(PR("norm2"), x_free=[x_done])
        for j in range(4):
            n, bank, free = bks[j]
            t = gemm(bank, (), mixh, mixl, {0: mix_r[1], 1: mix_r[3]}, False, 0, False, True)
            t_h = add_to_h(n, bank, t, j, *h2_r)
            if j:
                norm.turn()
            norm.feed(t_h, mix_r[3])
        x_ready = norm.x_ready
        side.append(norm.rest())

        a_r = {}
        ft = Slots([(at(f"f2_a{i}", [P, 2, T], 10, skip=4096 * i), at(f"f2_b{i}", [P, 2, T], 10,
                                                                      skip=4096 * i + 2048)) for i in range(2)])
        ft2 = Slots([at(f"f2_tanh{i}", [P, 2, T], 17, skip=2048 * i) for i in range(4)])

        def ffn2_tail(j, nt, ga, va, t_g, t_v):
            n2, th, hfree = ft2.take()
            t = act(lambda e: e.activation(th, ga, ACT.Tanh, scale=0.5), t_g, *hfree)
            yield
            t = vec(lambda e: e.scalar_tensor_tensor(th, th, 1.0, ga, ALU.add, ALU.mult), t)
            t = pool(lambda e: e.tensor_tensor(th, th, va, ALU.mult), t, t_v)
            ft.free(nt, t)
            yield
            yield
            t = split_from(th, acth[:, 2 * j:2 * j + 2, :], actl[:, 2 * j:2 * j + 2, :], t, pe_down)
            ft2.free(n2, t)
            a_r[j] = t

        for j in range(KF // 2):
            pair = projected_pair(True) if j == 0 else None
            n, bank, t = pair[0] if pair else projected(True)
            nt, (ga, va), tfree = ft.take()
            t_g = vec(lambda e: e.tensor_tensor(ga, bank.rearrange("p (c t) -> p c t", c=2), row2, ALU.mult), t,
                      norm.row_ready, *tfree)
            gemm_banks.free(n, t_g)
            n, bank, t = pair[1] if pair else projected(True)
            t_v = vec(lambda e: e.scalar_tensor_tensor(va, bank.rearrange("p (c t) -> p c t", c=2), 0.5, row2,
                                                       ALU.mult, ALU.mult), t, *tfree)
            gemm_banks.free(n, t_v)
            side.append(ffn2_tail(j, nt, ga, va, t_g, t_v))
        while len(a_r) < KF // 2 - 1:
            step_side()
        outbox = [sem("output_written"), 0]

        def write_out(j, t):
            cols = slice(j * PW, (j + 1) * PW)
            SP.dma(outbox, out[0].rearrange("(t p) d -> p t d", p=P)[:, :, cols], h[:, :, cols], t)

        ffn_down(a_r, None)
        SP.wait((outbox[0], outbox[1]), *G["rows_out"])


def _constants():
    c = np.zeros((P, N_CONSTS), np.float32)
    i, j = np.indices((P, P))
    c[:, slice(*CONSTS["ident"])] = np.eye(P)
    c[:, slice(*CONSTS["upper"])] = i <= j
    c[:, slice(*CONSTS["ones"])] = 1
    causal = np.where(j <= i, 0, NEG)
    c[:, slice(*CONSTS["causal"])] = causal
    c[:, slice(*CONSTS["decay_mask"])] = np.where(i <= j, 0, NEG)
    for n, side in enumerate((16, 32, 64)):
        lo = CONSTS["level"][0] + n * P
        c[:, lo:lo + P] = (i // (2 * side) == j // (2 * side)) & (i % (2 * side) < side) & (j % (2 * side) >= side)
    return c


def _bands():
    t = np.arange(T)
    b = np.zeros((4, T, T), np.float32)
    for g, w in enumerate(POOL_WINDOWS):
        lo, hi = np.clip(t - w // 2, 0, T), np.clip(t + w // 2, 0, T)
        inside = (t[:, None] >= lo[None]) & (t[:, None] < hi[None])
        b[g] = inside / (hi - lo)[None].astype(np.float32) - np.eye(T)
    return np.ascontiguousarray(b.reshape(4, TT, P, T).transpose(2, 0, 1, 3))


_BIG = ["x", "w_in", "w_branch_fox", "w_branch_gdn", "w_out", "w_up", "w_down", "norm_final", "w_in_2",
        "w_pool_2", "w_out_2", "w_gate_2", "w_up_2", "w_down_2"]


def kernel(**inputs):
    import concourse.bacc as bacc
    from concourse.bass_utils import run_bass_kernel_spmd

    def g(name):
        return np.asarray(inputs[name])

    def tiles(v):
        return v.reshape(-1, P).T

    params = np.empty((P, N_PARAMS), np.float32)
    for name, v in (("norm_mix", tiles(g("norm_mix")[0])), ("norm_ffn", tiles(g("norm_ffn")[0])),
                    ("norm1", tiles(g("norm1_g_2")[0])), ("norm2", tiles(g("norm2_g_2")[0])),
                    ("norm_final", tiles(g("norm_final"))),
                    ("gconv", g("gdn_conv_w")[0].reshape(4, 24, P).transpose(2, 1, 0).reshape(P, 96)),
                    ("fconv", g("ffn_conv_w")[0].reshape(3, 2 * KF, P).transpose(2, 1, 0).reshape(P, 2 * KF * 3)),
                    ("gdn_norm", g("gdn_norm").T), ("pool_scale", tiles(g("pool_scale_2")[0])),
                    ("qg", np.tile(g("q_norm_g_2")[0], 2)[:, None]), ("kg", np.tile(g("k_norm_g_2")[0], 2)[:, None]),
                    ("gate_bias", np.concatenate([g("fox_f_bias"), g("gdn_dt_bias")], 1)),
                    ("a_log", g("gdn_a_log"))):
        params[:, slice(*PARAMS[name])] = v
    nc = bacc.Bacc("TRN2", target_bir_lowering=False, num_devices=1)
    arrays, args = {}, {}
    feed = {n: np.ascontiguousarray(g(n)) for n in _BIG}
    col = np.arange(GRID)
    rel = np.clip(col[None] - col[:, None] + WIN_COLS - 1, 0, RPB_COLS - 1)
    skew = g("rpb_2")[0][:, 4:11][:, :, rel].transpose(2, 0, 1, 3).reshape(GRID, HEADS, 7 * GRID)
    feed.update(rpb_skew=np.ascontiguousarray(skew), params=params, constants=_constants(), bands=_bands())
    for name, v in feed.items():
        arrays[f"in_{name}"] = v
        args[name] = nc.dram_tensor(f"in_{name}", v.shape, F32, kind="ExternalInput").ap()
    out = nc.dram_tensor("out", (1, T, D), F32, kind="ExternalOutput").ap()
    sa = nc.dram_tensor("blocks_to_invert", (NBLK, UNITS, BLOCK, BLOCK), F32).ap()
    sx = nc.dram_tensor("blocks_inverted", (2, NBLK, UNITS, BLOCK, BLOCK), F32).ap()
    sc = nc.dram_tensor("gate_sums", (2, HEADS, T), F32).ap()
    build(nc, args, out, sa, sx, sc)
    r = run_bass_kernel_spmd(nc, [arrays], core_ids=[0])
    return r.results[0]["out"]
```
